# Optimizing a Trainium2 kernel written in Bass

```python
import jax, jax.numpy as jnp
from jax import lax
import numpy as np

D_MODEL = 2048
BATCH = 1
SEQ = 256
DEPTH = 2

PLE_DIM = 256
ROPE_THETA = 10000.0
NORM_EPS = 1e-6
Q_BLOCK = 128
NEG = -1e30
FORCE = 1e6

GLA_HEADS = 8
GLA_DK = 64
GLA_DV = 128
GLA_GATE_RANK = 16
GLA_TAU = 16.0
GLA_CHUNK = 64

MLA_HEADS = 8
MLA_Q_RANK = 512
MLA_KV_RANK = 512
MLA_NOPE = 128
MLA_ROPE = 64
MLA_V = 128

NSA_HEADS = 16
NSA_KV_GROUPS = 4
NSA_HPG = NSA_HEADS // NSA_KV_GROUPS
NSA_HEAD_DIM = 128
NSA_CMP_LEN = 32
NSA_CMP_STRIDE = 16
NSA_SEL_LEN = 64
NSA_SEL_TOPK = 16
NSA_WINDOW = 512
NSA_SEL_QCHUNK = 32

FFN_HIDDEN = -(-8 * D_MODEL // (3 * 256)) * 256

AB_SPLITS = (GLA_HEADS * GLA_DK, GLA_HEADS * GLA_DK, GLA_HEADS * GLA_DV, GLA_HEADS * GLA_DV,
             GLA_GATE_RANK, MLA_Q_RANK, MLA_KV_RANK, MLA_ROPE)
AB_IN = sum(AB_SPLITS)
AB_MIX = GLA_HEADS * GLA_DV + MLA_HEADS * MLA_V
NSA_KV_W = NSA_KV_GROUPS * NSA_HEAD_DIM
NSA_SPLITS = (NSA_HEADS * NSA_HEAD_DIM,) + (NSA_KV_W,) * 6 + (3 * NSA_HEADS,)
NSA_IN = sum(NSA_SPLITS)
NSA_MIX = NSA_HEADS * NSA_HEAD_DIM

kernel_name = "hybrid_gla_mla_nsa_sandwich_ple"

def split_cols(z, widths):
    out, off = [], 0
    for w in widths:
        out.append(z[..., off:off + w])
        off += w
    return out

def rms_norm(x, w):
    xf = x.astype(jnp.float32)
    y = xf * lax.rsqrt(jnp.mean(xf * xf, axis=-1, keepdims=True) + NORM_EPS)
    return (y * w.astype(jnp.float32)).astype(x.dtype)

def rope_tables(positions, dim):
    inv = jnp.power(ROPE_THETA, -jnp.arange(0, dim, 2, dtype=jnp.float32) / dim)
    ang = positions.astype(jnp.float32)[..., None] * inv
    return jnp.cos(ang), jnp.sin(ang)

def apply_rope(x, cos, sin):
    half = x.shape[-1] // 2
    xf = x.astype(jnp.float32)
    x1, x2 = xf[..., :half], xf[..., half:]
    return jnp.concatenate([x1 * cos - x2 * sin, x2 * cos + x1 * sin], axis=-1).astype(x.dtype)

def gla_chunked(q, k, v, log_a):
    B, H, S, dk = q.shape
    dv = v.shape[-1]
    L = GLA_CHUNK
    N = S // L
    f32 = jnp.float32
    qf = q.astype(f32).reshape(B, H, N, L, dk) * (dk ** -0.5)
    kf = k.astype(f32).reshape(B, H, N, L, dk)
    vf = v.astype(f32).reshape(B, H, N, L, dv)
    b = jnp.cumsum(log_a.astype(f32).reshape(B, H, N, L, dk), axis=3)
    b_end = b[:, :, :, -1:, :]
    q_dec = qf * jnp.exp(b)
    k_inv = kf * jnp.exp(-b)
    k_end = kf * jnp.exp(b_end - b)
    causal = jnp.tril(jnp.ones((L, L), dtype=bool))
    attn = jnp.where(causal, jnp.einsum('bhnid,bhnjd->bhnij', q_dec, k_inv), 0.0)
    o_intra = jnp.einsum('bhnij,bhnjv->bhniv', attn, vf)
    upd = jnp.einsum('bhnjd,bhnjv->bhndv', k_end, vf)
    decay = jnp.exp(b_end[:, :, :, 0, :])

    def step(state, inp):
        dec, u = inp
        return dec[..., None] * state + u, state

    s0 = jnp.zeros((B, H, dk, dv), f32)
    _, s_prev = lax.scan(step, s0, (jnp.moveaxis(decay, 2, 0), jnp.moveaxis(upd, 2, 0)))
    s_prev = jnp.moveaxis(s_prev, 0, 2)
    o_inter = jnp.einsum('bhnid,bhndv->bhniv', q_dec, s_prev)
    return (o_intra + o_inter).reshape(B, H, S, dv).astype(v.dtype)

def causal_attention_blocks(q, k, v, scale):
    B, H, S, dq = q.shape
    nb = S // Q_BLOCK
    q_b = jnp.moveaxis(q.reshape(B, H, nb, Q_BLOCK, dq), 2, 0)
    kpos = jnp.arange(S)

    def one(args):
        qb, i = args
        s = jnp.einsum('bhqd,bhkd->bhqk', qb, k).astype(jnp.float32) * scale
        qpos = i * Q_BLOCK + jnp.arange(Q_BLOCK)
        s = jnp.where(kpos[None, :] <= qpos[:, None], s, NEG)
        p = jax.nn.softmax(s, axis=-1)
        return jnp.einsum('bhqk,bhkd->bhqd', p.astype(v.dtype), v)

    o = lax.map(one, (q_b, jnp.arange(nb)))
    return jnp.moveaxis(o, 0, 2).reshape(B, H, S, v.shape[-1])

def gla_mla_mixer(h, cos64, sin64, w_in, w_alpha_up, b_alpha, gla_norm_w,
                  q_norm_w, w_uq, kv_norm_w, w_ukv, w_out):
    B, S, _ = h.shape
    z = h @ w_in
    q_g, k_g, v_g, g_g, a_lr, c_q, c_kv, k_r = split_cols(z, AB_SPLITS)

    def heads(t, n):
        return t.reshape(B, S, n, -1).transpose(0, 2, 1, 3)

    log_a = jax.nn.log_sigmoid((a_lr @ w_alpha_up + b_alpha).astype(jnp.float32)) / GLA_TAU
    o_gla = gla_chunked(heads(q_g, GLA_HEADS), heads(k_g, GLA_HEADS), heads(v_g, GLA_HEADS),
                        heads(log_a, GLA_HEADS))
    o_gla = rms_norm(o_gla.transpose(0, 2, 1, 3), gla_norm_w).reshape(B, S, -1) * jax.nn.silu(g_g)

    q = (rms_norm(c_q, q_norm_w) @ w_uq).reshape(B, S, MLA_HEADS, MLA_NOPE + MLA_ROPE).transpose(0, 2, 1, 3)
    kv = (rms_norm(c_kv, kv_norm_w) @ w_ukv).reshape(B, S, MLA_HEADS, MLA_NOPE + MLA_V).transpose(0, 2, 1, 3)
    q_rope = apply_rope(q[..., MLA_NOPE:], cos64[:, None], sin64[:, None])
    k_rope = apply_rope(k_r, cos64, sin64)[:, None]
    qm = jnp.concatenate([q[..., :MLA_NOPE], q_rope], axis=-1)
    km = jnp.concatenate([kv[..., :MLA_NOPE],
                          jnp.broadcast_to(k_rope, (B, MLA_HEADS, S, MLA_ROPE))], axis=-1)
    o_mla = causal_attention_blocks(qm, km, kv[..., MLA_NOPE:], (MLA_NOPE + MLA_ROPE) ** -0.5)
    o_mla = o_mla.transpose(0, 2, 1, 3).reshape(B, S, -1)
    return jnp.concatenate([o_gla, o_mla.astype(o_gla.dtype)], axis=-1) @ w_out

def nsa_compress(t, pos, w1, w2):
    S = t.shape[2]
    nc = (S - NSA_CMP_LEN) // NSA_CMP_STRIDE + 1
    idx = jnp.arange(nc)[:, None] * NSA_CMP_STRIDE + jnp.arange(NSA_CMP_LEN)[None, :]
    blocks = t[:, :, idx, :] + pos
    flat = blocks.reshape(blocks.shape[0], blocks.shape[1], nc, NSA_CMP_LEN * t.shape[-1])
    return jax.nn.gelu(flat @ w1) @ w2

def nsa_compressed_branch(q, kc, vc, cmp_pos, cmp_w1, cmp_w2, scale):
    S = q.shape[3]
    k_cmp = nsa_compress(kc, cmp_pos[0], cmp_w1[0], cmp_w2[0])
    v_cmp = nsa_compress(vc, cmp_pos[1], cmp_w1[1], cmp_w2[1])
    nc = k_cmp.shape[2]
    s = jnp.einsum('bgjsd,bgnd->bgjsn', q, k_cmp).astype(jnp.float32) * scale
    blk_end = jnp.arange(nc) * NSA_CMP_STRIDE + NSA_CMP_LEN - 1
    ok = blk_end[None, :] <= jnp.arange(S)[:, None]
    p = jnp.where(ok, jax.nn.softmax(jnp.where(ok, s, NEG), axis=-1), 0.0)
    o = jnp.einsum('bgjsn,bgnd->bgjsd', p.astype(v_cmp.dtype), v_cmp)
    return o, p

def nsa_select_blocks(p_cmp, S):
    nc = p_cmp.shape[-1]
    ns = S // NSA_SEL_LEN
    c_start = np.arange(nc) * NSA_CMP_STRIDE
    c_end = c_start + NSA_CMP_LEN
    s_start = np.arange(ns) * NSA_SEL_LEN
    s_end = s_start + NSA_SEL_LEN
    overlap = jnp.asarray(((c_start[:, None] < s_end[None, :]) &
                           (c_end[:, None] > s_start[None, :])).astype(np.float32))
    imp = jnp.einsum('bgjsn,nm->bgsm', p_cmp, overlap)
    t = jnp.arange(S)[:, None]
    m = jnp.arange(ns)[None, :]
    causal = m * NSA_SEL_LEN <= t
    cur = t // NSA_SEL_LEN
    forced = (m == 0) | (m == cur) | (m == cur - 1)
    score = jnp.where(causal, jnp.where(forced, FORCE, imp), -FORCE)
    val, idx = lax.top_k(score, min(NSA_SEL_TOPK, ns))
    return idx, val > -0.5 * FORCE

def nsa_selected_branch(q, ks, vs, sel_idx, sel_ok, scale):
    B, G, HG, S, dh = q.shape
    ns = S // NSA_SEL_LEN
    kk = sel_idx.shape[-1]
    Qc = NSA_SEL_QCHUNK
    nq = S // Qc
    k_blocks = ks.reshape(B, G, ns, NSA_SEL_LEN, dh)
    v_blocks = vs.reshape(B, G, ns, NSA_SEL_LEN, dh)
    q_ch = jnp.moveaxis(q.reshape(B, G, HG, nq, Qc, dh), 3, 0)
    i_ch = jnp.moveaxis(sel_idx.reshape(B, G, nq, Qc, kk), 2, 0)
    ok_ch = jnp.moveaxis(sel_ok.reshape(B, G, nq, Qc, kk), 2, 0)
    b_ix = jnp.arange(B)[:, None, None, None]
    g_ix = jnp.arange(G)[None, :, None, None]
    n_keys = kk * NSA_SEL_LEN

    def one(args):
        qc, ic, okc, c = args
        kg = k_blocks[b_ix, g_ix, ic].reshape(B, G, Qc, n_keys, dh)
        vg = v_blocks[b_ix, g_ix, ic].reshape(B, G, Qc, n_keys, dh)
        kpos = ic[..., None] * NSA_SEL_LEN + jnp.arange(NSA_SEL_LEN)
        qpos = c * Qc + jnp.arange(Qc)
        mask = (okc[..., None] & (kpos <= qpos[None, None, :, None, None])).reshape(B, G, Qc, n_keys)
        s = jnp.einsum('bgjqd,bgqkd->bgjqk', qc, kg).astype(jnp.float32) * scale
        p = jax.nn.softmax(jnp.where(mask[:, :, None], s, NEG), axis=-1)
        return jnp.einsum('bgjqk,bgqkd->bgjqd', p.astype(vg.dtype), vg)

    o = lax.map(one, (q_ch, i_ch, ok_ch, jnp.arange(nq)))
    return jnp.moveaxis(o, 0, 3).reshape(B, G, HG, S, dh)

def nsa_window_branch(q, kw, vw, scale):
    B, G, HG, S, dh = q.shape
    nb = S // Q_BLOCK
    span = NSA_WINDOW + Q_BLOCK
    pad = ((0, 0), (0, 0), (NSA_WINDOW, 0), (0, 0))
    k_pad = jnp.pad(kw, pad)
    v_pad = jnp.pad(vw, pad)
    q_b = jnp.moveaxis(q.reshape(B, G, HG, nb, Q_BLOCK, dh), 3, 0)

    def one(args):
        qb, i = args
        start = i * Q_BLOCK
        kb = lax.dynamic_slice_in_dim(k_pad, start, span, axis=2)
        vb = lax.dynamic_slice_in_dim(v_pad, start, span, axis=2)
        kpos = start - NSA_WINDOW + jnp.arange(span)
        qpos = start + jnp.arange(Q_BLOCK)
        mask = ((kpos[None, :] <= qpos[:, None]) & (kpos[None, :] > qpos[:, None] - NSA_WINDOW)
                & (kpos[None, :] >= 0))
        s = jnp.einsum('bgjqd,bgkd->bgjqk', qb, kb).astype(jnp.float32) * scale
        p = jax.nn.softmax(jnp.where(mask, s, NEG), axis=-1)
        return jnp.einsum('bgjqk,bgkd->bgjqd', p.astype(vb.dtype), vb)

    o = lax.map(one, (q_b, jnp.arange(nb)))
    return jnp.moveaxis(o, 0, 3).reshape(B, G, HG, S, dh)

def nsa_mixer(h, cos, sin, w_in, b_gate, cmp_pos, cmp_w1, cmp_w2, w_out):
    B, S, _ = h.shape
    G, HG, dh = NSA_KV_GROUPS, NSA_HPG, NSA_HEAD_DIM
    q, kc, vc, ks, vs, kw, vw, gl = split_cols(h @ w_in, NSA_SPLITS)
    q = apply_rope(q.reshape(B, S, G, HG, dh).transpose(0, 2, 3, 1, 4), cos[:, None, None], sin[:, None, None])

    def kvh(t):
        return t.reshape(B, S, G, dh).transpose(0, 2, 1, 3)

    kc = apply_rope(kvh(kc), cos[:, None], sin[:, None])
    ks = apply_rope(kvh(ks), cos[:, None], sin[:, None])
    kw = apply_rope(kvh(kw), cos[:, None], sin[:, None])
    vc, vs, vw = kvh(vc), kvh(vs), kvh(vw)
    scale = dh ** -0.5
    o_cmp, p_cmp = nsa_compressed_branch(q, kc, vc, cmp_pos, cmp_w1, cmp_w2, scale)
    sel_idx, sel_ok = nsa_select_blocks(p_cmp, S)
    o_sel = nsa_selected_branch(q, ks, vs, sel_idx, sel_ok, scale)
    o_win = nsa_window_branch(q, kw, vw, scale)
    gates = jax.nn.sigmoid((gl + b_gate).astype(jnp.float32)).reshape(B, S, G, HG, 3).transpose(0, 2, 3, 1, 4)
    o = gates[..., 0:1] * o_cmp + gates[..., 1:2] * o_sel + gates[..., 2:3] * o_win
    o = o.transpose(0, 3, 1, 2, 4).reshape(B, S, NSA_MIX).astype(h.dtype)
    return o @ w_out

def swiglu(h, w_gate, w_up, w_down):
    return (jax.nn.silu(h @ w_gate) * (h @ w_up)) @ w_down

def setup_inputs(seed: int = 0) -> dict:
    key = jax.random.key(seed)
    ks = jax.random.split(key, 32)
    f32 = jnp.float32
    NE = (DEPTH + 1) // 2
    NO = DEPTH // 2

    def nrm(k, shape, s):
        return jax.random.normal(k, shape, f32) * s

    def gain(k, shape):
        return 1.0 + 0.05 * jax.random.normal(k, shape, f32)

    return {
        "x": nrm(ks[0], (BATCH, SEQ, D_MODEL), 1.0),
        "p": nrm(ks[1], (DEPTH, BATCH, SEQ, PLE_DIM), 1.0),
        "positions": (jnp.arange(SEQ, dtype=jnp.int32)[None, :]
                      + jax.random.randint(ks[2], (BATCH, 1), 0, 1024, dtype=jnp.int32)),
        "ln_mix_pre": gain(ks[3], (DEPTH, D_MODEL)),
        "ln_mix_post": gain(ks[4], (DEPTH, D_MODEL)),
        "ln_ffn_pre": gain(ks[5], (DEPTH, D_MODEL)),
        "ln_ffn_post": gain(ks[6], (DEPTH, D_MODEL)),
        "ab_w_in": nrm(ks[7], (NE, D_MODEL, AB_IN), D_MODEL ** -0.5),
        "gla_w_alpha_up": nrm(ks[8], (NE, GLA_GATE_RANK, GLA_HEADS * GLA_DK), GLA_GATE_RANK ** -0.5),
        "gla_b_alpha": nrm(ks[9], (NE, GLA_HEADS * GLA_DK), 0.1),
        "gla_norm_w": gain(ks[10], (NE, GLA_DV)),
        "mla_q_norm_w": gain(ks[11], (NE, MLA_Q_RANK)),
        "mla_w_uq": nrm(ks[12], (NE, MLA_Q_RANK, MLA_HEADS * (MLA_NOPE + MLA_ROPE)), MLA_Q_RANK ** -0.5),
        "mla_kv_norm_w": gain(ks[13], (NE, MLA_KV_RANK)),
        "mla_w_ukv": nrm(ks[14], (NE, MLA_KV_RANK, MLA_HEADS * (MLA_NOPE + MLA_V)), MLA_KV_RANK ** -0.5),
        "ab_w_out": nrm(ks[15], (NE, AB_MIX, D_MODEL), AB_MIX ** -0.5),
        "nsa_w_in": nrm(ks[16], (NO, D_MODEL, NSA_IN), D_MODEL ** -0.5),
        "nsa_b_gate": nrm(ks[17], (NO, 3 * NSA_HEADS), 0.1),
        "nsa_cmp_pos": nrm(ks[18], (NO, 2, NSA_CMP_LEN, NSA_HEAD_DIM), 0.1),
        "nsa_cmp_w1": nrm(ks[19], (NO, 2, NSA_CMP_LEN * NSA_HEAD_DIM, NSA_HEAD_DIM),
                          (NSA_CMP_LEN * NSA_HEAD_DIM) ** -0.5),
        "nsa_cmp_w2": nrm(ks[20], (NO, 2, NSA_HEAD_DIM, NSA_HEAD_DIM), NSA_HEAD_DIM ** -0.5),
        "nsa_w_out": nrm(ks[21], (NO, NSA_MIX, D_MODEL), NSA_MIX ** -0.5),
        "ffn_w_gate": nrm(ks[22], (DEPTH, D_MODEL, FFN_HIDDEN), D_MODEL ** -0.5),
        "ffn_w_up": nrm(ks[23], (DEPTH, D_MODEL, FFN_HIDDEN), D_MODEL ** -0.5),
        "ffn_w_down": nrm(ks[24], (DEPTH, FFN_HIDDEN, D_MODEL), FFN_HIDDEN ** -0.5),
        "ple_w_gate": nrm(ks[25], (DEPTH, D_MODEL, D_MODEL), D_MODEL ** -0.5),
        "ple_b_gate": nrm(ks[26], (DEPTH, D_MODEL), 0.01),
        "ple_w_proj": nrm(ks[27], (DEPTH, PLE_DIM, D_MODEL), PLE_DIM ** -0.5),
    }

def reference(x, p, positions, ln_mix_pre, ln_mix_post, ln_ffn_pre, ln_ffn_post,
              ab_w_in, gla_w_alpha_up, gla_b_alpha, gla_norm_w, mla_q_norm_w, mla_w_uq,
              mla_kv_norm_w, mla_w_ukv, ab_w_out,
              nsa_w_in, nsa_b_gate, nsa_cmp_pos, nsa_cmp_w1, nsa_cmp_w2, nsa_w_out,
              ffn_w_gate, ffn_w_up, ffn_w_down, ple_w_gate, ple_b_gate, ple_w_proj):
    cos64, sin64 = rope_tables(positions, MLA_ROPE)
    cos128, sin128 = rope_tables(positions, NSA_HEAD_DIM)
    h = x
    for i in range(DEPTH):
        hn = rms_norm(h, ln_mix_pre[i])
        if i % 2 == 0:
            j = i // 2
            m = gla_mla_mixer(hn, cos64, sin64, ab_w_in[j], gla_w_alpha_up[j], gla_b_alpha[j],
                              gla_norm_w[j], mla_q_norm_w[j], mla_w_uq[j], mla_kv_norm_w[j],
                              mla_w_ukv[j], ab_w_out[j])
        else:
            j = i // 2
            m = nsa_mixer(hn, cos128, sin128, nsa_w_in[j], nsa_b_gate[j], nsa_cmp_pos[j],
                          nsa_cmp_w1[j], nsa_cmp_w2[j], nsa_w_out[j])
        h = h + rms_norm(m, ln_mix_post[i])
        f = swiglu(rms_norm(h, ln_ffn_pre[i]), ffn_w_gate[i], ffn_w_up[i], ffn_w_down[i])
        h = h + rms_norm(f, ln_ffn_post[i])
        gate = jax.nn.sigmoid(h @ ple_w_gate[i] + ple_b_gate[i])
        h = h + gate * (p[i] @ ple_w_proj[i])
    return h


_drawn_inputs = setup_inputs


def setup_inputs(seed=0):
    import zlib

    import numpy as np

    out = dict(_drawn_inputs(seed))
    spreads = {}
    factors = {'mla_q_norm_w': 4.369,
     'mla_kv_norm_w': 2.797,
     'nsa_b_gate': 3.275,
     'ple_b_gate': 44.771,
     'gla_w_alpha_up': 2.961,
     'gla_b_alpha': 6.716,
     'gla_norm_w': 4.79}
    for name, (base, spread) in spreads.items():
        noise = np.random.default_rng([zlib.crc32(name.encode()), seed]).standard_normal(out[name].shape)
        drawn = base * np.exp(spread * noise) if base else spread * noise
        out[name] = __import__('jax').numpy.asarray(drawn.astype(out[name].dtype))
    for name, factor in factors.items():
        out[name] = (out[name] * factor).astype(out[name].dtype)
    return out
```

```python
from contextlib import ExitStack

import numpy as np

import concourse.bass as bass
from concourse import mybir
from concourse.alu_op_type import AluOpType as ALU

F32 = mybir.dt.float32
F32R = mybir.dt.float32r
U32 = mybir.dt.uint32
I32 = mybir.dt.int32
ACT = mybir.ActivationFunctionType
AX = mybir.AxisListType

P = 128
D = 2048
SEQ = 256
NT = SEQ // P
KC = D // P
FFN = 5632
PLE = 256
EPS = 1e-6
NEG = -1e30
TAU = 16.0
CMP_LEN, CMP_STRIDE, NCMP = 32, 16, 15
MLA_SCALE = float((128 + 64) ** -0.5)
NSA_SCALE = float(128 ** -0.5)
GELU_C = float(2.0 * np.sqrt(2.0 / np.pi))
TWO_PI = 6.283185307179586
C1 = 6.28125
C2 = 0.00193500518798828125
C3 = TWO_PI - C1 - C2
MAGIC = 12582912.0
PI_IN = 3.1415925

ZC0, ZC1, ZC2, QG, UQN, UQR, UKK, UKV, KG, VG, GG, OUT0 = 0, 1, 2, 3, 4, 6, 7, 9, 11, 12, 14, 16
FFN0 = OUT0 + 4
GROUPS = (4, 4, 3)
FFN_SLOTS = sum(2 * n + 4 for n in GROUPS)
L1 = FFN0 + FFN_SLOTS + 8
SKC, SVC, SKS, SW1, SKW, SVS, SVW, SGT, SQ, OUT1 = (L1 + i for i in (0, 1, 2, 3, 4, 5, 6, 7, 8, 12))
FFN1 = OUT1 + 4
OUTS, FFNS = (OUT0, OUT1), (FFN0, FFN1)
PROJ = tuple(f + FFN_SLOTS for f in FFNS)
GATE = tuple(f + FFN_SLOTS + 4 for f in FFNS)
NSLOTS = GATE[1] + 4
W_GT = 48

TQ = {}
_n = 0
for _name, _k in (("mix0", 8), ("cqkv", 4), ("gla", 4), ("ffn0", 8), ("p0", 1), ("hid0", 22), ("ple0", 8),
                  ("mix1", 8), ("ffn1", 8), ("p1", 1), ("hid1", 22), ("ple1", 8)):
    TQ[_name] = _n
    _n += _k
TQ_END = _n
POW = ["mix0", "cqkv", "gla", "post0", "ffn0", "fpost0", "mix1", "post1", "ffn1", "fpost1"]
POW_W = {"mix0": 2, "cqkv": 4, "gla": 16}


def ffn_base(layer, g):
    return FFNS[layer] + sum(2 * n + 4 for n in GROUPS[:g])


MLA_STEPS = 4
NSA_STEPS = 16
MLA_AT = {(UKV + 2, 1): 0, (UKV + 2, 3): 1, (UKV + 3, 1): 2, (UKV + 3, 3): 3, (UKV + 4, 1): 4, (UKV + 4, 3): 5}


def nsa_plan():
    plan, t = {}, 0
    for g in range(3):
        for j in range(4):
            ops = [("qt", g)] if j == 1 else [("cs", g)] if j == 2 else []
            if (g, j) >= (0, 3):
                ops.append(("st", t))
                t += 1
            plan[(SQ + 1 + g, j)] = ops
    end = plan[(SQ + 3, 3)]
    end += [("qt", 3), ("st", t), ("cs", 3), ("st", t + 1)]
    end += [("st", k) for k in range(t + 2, NSA_STEPS + 2)]
    return plan


NSA_AT = nsa_plan()
CP_STEP = {0: 0, 4: 1, 8: 2, 11: 3}

GLA_AT = {(GG, 1): 0, (GG, 2): 1, (GG, 3): 2, (GG + 1, 0): 3, (GG + 1, 1): 4, (GG + 1, 2): 5}
KT_AT = {(SKC + 1, 1): 0, (SVC + 1, 1): 1, (SKS + 1, 1): 2, (SKW + 1, 1): 3}


def before(s, j):
    return (s, j - 1) if j else (s - 1, 3)


class Steps:

    def __init__(self, eng, sem):
        self.eng, self.sem, self.n, self.i, self.per, self.base = eng, sem, 0, None, 0, 0

    def __call__(self, ins):
        ins.then_inc(self.sem, 1)
        self.n += 1
        self.eng.wait_ge(self.sem, self.n if self.i is None else self.n + self.i * self.per)

    def enter(self, i, per):
        self.i, self.per, self.base = i, per, self.n

    def leave(self, times):
        assert self.n - self.base == self.per, (self.n - self.base, self.per)
        self.n = self.base + self.per * times
        self.i = None


def build(nc, T):
    def rows(a):
        return a.rearrange("(c p) n -> p c n", p=P)

    ab_in, ab_out = rows(T["ab_w_in"][0]), rows(T["ab_w_out"][0])
    uq = T["mla_w_uq"][0].rearrange("(c p) (h e) -> p c h e", p=P, e=192)
    ukv = T["mla_w_ukv"][0].rearrange("(c p) (h e) -> p c h e", p=P, e=256)
    nsa_in, nsa_out = rows(T["nsa_w_in"][0]), rows(T["nsa_w_out"][0])
    wg, wu, wd, plg, plp = ([rows(T[n][i]) for i in range(2)] for n in (
        "ffn_w_gate", "ffn_w_up", "ffn_w_down", "ple_w_gate", "ple_w_proj"))
    w1_d = T["nsa_cmp_w1"]
    tok = lambda a: a.rearrange("(m p) d -> p m d", p=P)
    x_d, out_d = tok(T["x"][0]), tok(T["out"][0])
    p_d = [tok(T["p"][i, 0]) for i in range(2)]

    ctx = ExitStack()
    with ctx:
        at = [(nc.sbuf_base + 63) // 64 * 64]

        def sb(name, shape, dt=F32):
            n = int(np.prod(shape[1:])) * 4
            t = nc.alloc_sbuf_tensor_at(name, shape, dt, offset=at[0])
            at[0] += (n + 31) // 32 * 32
            return t

        def sem(name):
            return ctx.enter_context(nc.semaphore(name))

        h = sb("h", [P, NT, D])
        XAh, XAl = sb("XAh", [P, KC, SEQ], F32R), sb("XAl", [P, KC, SEQ], F32R)
        xb0 = at[0]
        XBh, XBl = sb("XBh", [P, KC, SEQ], F32R), sb("XBl", [P, KC, SEQ], F32R)
        BLh = nc.alloc_sbuf_tensor_at("BLh", [P, 2, CMP_LEN, 60], F32R, offset=xb0)
        BLl = nc.alloc_sbuf_tensor_at("BLl", [P, 2, CMP_LEN, 60], F32R, offset=xb0 + 2 * CMP_LEN * 60 * 4)
        raw = sb("raw", [P, 4, 2048])
        wh, wl = sb("wh", [P, 2, 2048], F32R), sb("wl", [P, 2, 2048], F32R)
        ident = sb("ident", [P, P])
        cmask = sb("cmask", [P, 3, P])
        lt = sb("lt", [P, P])
        gt = sb("gt", [P, P])
        endm = sb("endm", [P, P])
        cosT, sinT = sb("cosT", [P, NT, 64]), sb("sinT", [P, NT, 64])
        vcol = sb("vcol", [P, 72])
        posT = sb("posT", [P, 64])
        okm, negm = sb("okm", [P, NT, 16]), sb("negm", [P, NT, 16])
        ss = sb("ss", [P, NT, 4])
        pwi, pwo, mhalf = sb("pwi", [P, 16]), sb("pwo", [P, 16]), sb("mhalf", [P, 16])
        sm = sb("sm", [P, 12])
        rt = sb("rt", [P, 2, 512])
        gnw = sb("gnw", [P, P])
        AL, aw = sb("AL", [17, SEQ]), sb("aw", [17, 512])
        krd = sb("krd", [P, NT, 2, 64])
        KrT = sb("KrT", [P, SEQ])
        decs = sb("decs", [P, 4, 4])
        w2s = sb("w2s", [P, 2, P])
        GE = sb("GE", [P, 2, 4, 32])
        KcT = sb("KcT", [P, 4, 32])
        gbias, gates = sb("gbias", [P, W_GT]), sb("gates", [P, NT, W_GT])
        csc, Pc = sb("csc", [P, NT, 4, 16]), sb("Pc", [P, NT, 4, 32])
        cst = sb("cst", [P, 3, 8])
        PcT = sb("PcT", [P, 2, SEQ])

        ZS = 58112
        z0 = at[0]
        assert z0 + ZS <= nc.sbuf_usable_end, (z0 + ZS, nc.sbuf_usable_end)

        def zt(name, off, shape, dt=F32):
            assert off + int(np.prod(shape[1:])) * 4 <= ZS, name
            return nc.alloc_sbuf_tensor_at(name, shape, dt, offset=z0 + off)

        vin, vin2 = zt("vin", 16384, [72, P]), zt("vin2", 16896, [64, P])
        invb, posi, posf = zt("invb", 17408, [P, 64]), zt("posi", 17664, [P, NT], I32), zt("posf", 17696, [P, NT])
        ang, kk = zt("ang", 17728, [P, NT, 64]), zt("kk", 18240, [P, NT, 64])
        qg, kg = zt("qg", 0, [P, NT, 512]), zt("kg", 4096, [P, NT, 512])
        vg, gg = zt("vg", 8192, [P, NT, 1024]), zt("gg", 16384, [P, NT, 1024])
        SP0, PT0 = zt("SP0", 16384, [P, 2, 384]), zt("PT0", 19456, [P, 2, 384])
        QnT, KnT = zt("QnT", 24576, [P, 8, SEQ]), zt("KnT", 32768, [P, 8, SEQ])
        Vm, zc = zt("Vm", 40960, [P, NT, 1024]), zt("zc", 40960, [P, NT, 1104])
        qr, QrT = zt("qr", 49792, [P, NT, 512]), zt("QrT", 53888, [P, 4, SEQ])
        loga, kinv, E1 = zt("loga", 24576, [P, NT, 512]), zt("kinv", 28672, [P, NT, 512]), zt("E1", 32768, [P, NT, 512])
        qdT, kiT = zt("qdT", 36864, [P, 4, SEQ]), zt("kiT", 40960, [P, 4, SEQ])
        SS, oT = zt("SS", 45056, [P, 4, 3, P]), zt("oT", 51200, [P, 512])
        AT = [zt("ATa", 24576, [P, 2, 512]), zt("ATb", 32768, [P, 2, 512])]
        zq, KB = zt("zq", 0, [P, 2, NT, 512]), zt("KB", 8192, [P, 2, NT, 512])
        SP1, PT1 = zt("SP1", 8192, [P, 2, 384]), zt("PT1", 11264, [P, 2, 384])
        vs, vw = zt("vs", 16384, [P, NT, 512]), zt("vw", 20480, [P, NT, 512])
        kcT, vcT = zt("kcT", 24576, [P, 4, SEQ]), zt("vcT", 28672, [P, 4, SEQ])
        ksT, kwT = zt("ksT", 32768, [P, 4, SEQ]), zt("kwT", 36864, [P, 4, SEQ])
        BT = zt("BT", 40960, [P, CMP_LEN, 60])
        VB = zt("VB", 24576, [P, 4, 4, P])
        QT = zt("QT", 48640, [P, 2, 4, SEQ])
        GX, GU = zt("GX", 48640, [P, 2, 60]), zt("GU", 49152, [P, 2, 60])
        Fm, PJ = zt("Fm", 0, [P, NT, D]), zt("PJ", 16384, [P, NT, D])
        Eb, Hb = zt("Eb", 32768, [P, NT, 512]), zt("Hb", 36864, [P, NT, 512])
        wbc, pp = zt("wbc", 40960, [P, D]), zt("pp", 49152, [P, NT, PLE])
        PXh, PXl = zt("PXh", 51200, [P, 2, SEQ], F32R), zt("PXl", 53248, [P, 2, SEQ], F32R)
        XA, XB, PX = (XAh, XAl), (XBh, XBl), (PXh, PXl)

        PG = ctx.enter_context(nc.psum_tensor("PG", [P, 2, NT, 512], F32))
        MB = ctx.enter_context(nc.psum_tensor("MB", [P, 4, 512], F32))

        raw_in = [sem(f"raw_in{j}") for j in range(4)]
        x_in, const_in = sem("x_in"), sem("const_in")
        pp_in, wbc_in, out_st = sem("pp_in"), sem("wbc_in"), sem("out_st")
        hi_ready, lo_ready = sem("hi_ready"), sem("lo_ready")
        unit_done = sem("unit_done")
        evac_a, evac_v = sem("evac_a"), sem("evac_v")
        tx_ps, tx_hi, tx_lo = sem("tx_ps"), sem("tx_hi"), sem("tx_lo")
        pw_req, pw_done = sem("pw_req"), sem("pw_done")
        const_mk = sem("const_mk")
        act_step, dve_step, pool_step, pe_step = (sem(n) for n in ("act_step", "dve_step", "pool_step", "pe_step"))
        vt_ps, vt_sb = sem("vt_ps"), sem("vt_sb")
        ang_ok, trig_ok = sem("ang_ok"), sem("trig_ok")
        sq_done = sem("sq_done")
        mul_done = sem("mul_done")
        add_done = sem("add_done")
        upd, ssq = sem("upd"), sem("ssq")
        hn_a, hn_v = sem("hn_a"), sem("hn_v")
        h_ok = sem("h_ok")
        zn_ok, kr_ok, qr_ok = sem("zn_ok"), sem("kr_ok"), sem("qr_ok")
        al_ps, al_sb = sem("al_ps"), sem("al_sb")
        qrt_ps, qrt_sb = sem("qrt_ps"), sem("qrt_sb")
        s_done, pt_done, pv_done = sem("s_done"), sem("pt_done"), sem("pv_done")
        mx_ok, exp_ok, o_hi = sem("mx_ok"), sem("exp_ok"), sem("o_hi")
        pt_sb, att_v = sem("pt_sb"), sem("att_v")
        ga_ps, ga_t, ga_n, ga_l, ga_ok = (sem(n) for n in ("ga_ps", "ga_t", "ga_n", "ga_l", "ga_ok"))
        gb_ps, ge_a, ge_v = sem("gb_ps"), sem("ge_a"), sem("ge_v")
        gt_ps, gt_sb, gu_ps, gd_sb, gs_ok = (sem(n) for n in ("gt_ps", "gt_sb", "gu_ps", "gd_sb", "gs_ok"))
        at_zero, at_ps, at_ok, go_ps, go_sq, go_ok = (sem(n) for n in (
            "at_zero", "at_ps", "at_ok", "go_ps", "go_sq", "go_ok"))
        ke_ok, kt_ps, kt_sb = sem("ke_ok"), sem("kt_ps"), sem("kt_sb")
        bt_ok, bh_ok, bl_ok = sem("bt_ok"), sem("bh_ok"), sem("bl_ok")
        ge_x, ge_e, gl_ok = sem("ge_x"), sem("ge_e"), sem("gl_ok")
        c2_ps, c2_a, c2_v, vb_zero = sem("c2_ps"), sem("c2_a"), sem("c2_v"), sem("vb_zero")
        gx_e = sem("gx_e")
        qe_ok, qt_ps, qt_sb = sem("qe_ok"), sem("qt_ps"), sem("qt_sb")
        cs_ps, cs_in, cs_e, cs_ok, cp_ps, pct_sb = (sem(n) for n in (
            "cs_ps", "cs_in", "cs_e", "cs_ok", "cp_ps", "pct_sb"))

        N_CONST = 16
        COPY0 = {QG: (qg, 0), KG: (kg, 0), UKV: (Vm, 0), UKV + 1: (Vm, 512), VG: (vg, 0), VG + 1: (vg, 512),
                 SVS: (vs, 0), SVW: (vw, 0)}
        block = ctx.enter_context(nc.Block())

        def width(s):
            kc, ncol = shape_of(s)
            return kc * ncol

        def shape_of(s):
            if s == ZC2:
                return 4, 80
            if s == SGT:
                return 4, W_GT
            if UQN <= s < KG:
                return 1, 512
            return 4, 512

        @block.sync
        def _(sp):
            sp.dma_start(h[:, 0, :], x_d[:, 0, :]).then_inc(x_in, 16)
            sp.dma_start(h[:, 1, :], x_d[:, 1, :]).then_inc(x_in, 16)
            consts = [(vin[0:16, :], T["ln_mix_pre"][0].rearrange("(c k) -> c k", k=P)),
                      (vin[16:32, :], T["ln_ffn_pre"][0].rearrange("(c k) -> c k", k=P)),
                      (vin[32:48, :], T["ln_mix_pre"][1].rearrange("(c k) -> c k", k=P)),
                      (vin[48:64, :], T["ln_ffn_pre"][1].rearrange("(c k) -> c k", k=P)),
                      (vin[64:68, :], T["mla_q_norm_w"][0].rearrange("(c k) -> c k", k=P)),
                      (vin[68:72, :], T["mla_kv_norm_w"][0].rearrange("(c k) -> c k", k=P)),
                      (vin2[0:32, :], T["nsa_cmp_pos"][0, 0]),
                      (vin2[32:64, :], T["nsa_cmp_pos"][0, 1]),
                      (posi[:, :], T["positions"].rearrange("a (m p) -> p (a m)", p=P)),
                      (invb[:, :], T["rope_inv"][0:1, :].broadcast_to([P, 64]))]
            late = [(gnw[:, :], T["gla_norm_w"][0:1, :].broadcast_to([P, P])),
                    (aw[0:16, :], T["gla_w_alpha_up"][0]),
                    (aw[16:17, :], T["gla_b_alpha"][0:1, :]),
                    (w2s[:, 0, :], T["nsa_cmp_w2"][0, 0]),
                    (w2s[:, 1, :], T["nsa_cmp_w2"][0, 1]),
                    (gbias[:, :], T["nsa_b_gate"][0:1, :].broadcast_to([P, W_GT]))]
            assert len(consts + late) == N_CONST
            for dst, src in consts:
                sp.dma_start(dst, src, allow_slow_non_contiguous=True).then_inc(const_in, 16)

            def unit(s, j, src, kc, ncol):
                if not (isinstance(s, int) and s == 0):
                    sp.wait_ge(lo_ready, 4 * s + j - 3)
                dst = raw[:, j, 0:kc * ncol].rearrange("p (c n) -> p c n", c=kc)
                if len(src.shape) == 4:
                    dst = raw[:, j, 0:kc * ncol].rearrange("p (c h e) -> p c h e", c=kc, e=src.shape[3])
                sp.dma_start(dst, src).then_inc(raw_in[j], 16)

            def k_units(s, w, col, ncol=512, kc=4, c0=0, wrap=KC):
                for j in range(4):
                    c = (c0 + j * kc) % wrap
                    unit(s, j, w[:, c:c + kc, bass.ds(col, ncol)], kc, ncol)

            for n, s in enumerate((ZC0, ZC1, ZC2)):
                k_units(s, ab_in, 3072 + 512 * n, shape_of(s)[1])
                if n == 0:
                    for dst, src in late:
                        sp.dma_start(dst, src).then_inc(const_in, 16)
            k_units(QG, ab_in, 0)
            for n in range(7):
                for j in range(4):
                    if n < 2:
                        src = uq[:, j:j + 1, 4 * n:4 * n + 4, 0:128]
                    elif n == 2:
                        src = uq[:, j:j + 1, :, 128:192]
                    elif n < 5:
                        src = ukv[:, j:j + 1, 4 * (n - 3):4 * (n - 3) + 4, 0:128]
                    else:
                        src = ukv[:, j:j + 1, 4 * (n - 5):4 * (n - 5) + 4, 128:256]
                    unit(UQN + n, j, src, 1, 512)
            for n in range(5):
                k_units(KG + n, ab_in, 512 * (n + 1))
            for layer in range(2):
                if layer == 0:
                    for n in range(4):
                        k_units(OUTS[0] + n, ab_out, 512 * n, c0=8)
                else:
                    with sp.Fori(0, 4) as i:
                        k_units(i + OUTS[1], nsa_out, i * 512)
                for g, n in enumerate(GROUPS):
                    b, p0 = ffn_base(layer, g), sum(GROUPS[:g])
                    with sp.Fori(0, n) as i:
                        k_units(i * 2 + b, wg[layer], i * 512 + 512 * p0)
                        k_units(i * 2 + (b + 1), wu[layer], i * 512 + 512 * p0)
                    with sp.Fori(0, 4) as i:
                        k_units(i + (b + 2 * n), wd[layer], i * 512, kc=n, c0=4 * p0, wrap=FFN)
                with sp.Fori(0, 4) as i:
                    for j in range(4):
                        unit(i + PROJ[layer], j, plp[layer][:, 0:2, bass.ds(i * 512 + 128 * j, 128)], 2, 128)
                with sp.Fori(0, 4) as i:
                    k_units(i + GATE[layer], plg[layer], i * 512)
                if layer == 0:
                    kv = {SKC: 0, SVC: 1, SKS: 2, SVS: 3, SKW: 4, SVW: 5}
                    for s in range(L1, SQ):
                        if s == SW1:
                            for j in range(4):
                                unit(s, j, w1_d[j // 2, :, 16 * (j % 2):16 * (j % 2) + 16, :], 16, P)
                        elif s == SGT:
                            k_units(s, nsa_in, 5120, W_GT)
                        else:
                            k_units(s, nsa_in, 2048 + 512 * kv[s])
                    with sp.Fori(0, 4) as i:
                        k_units(i + SQ, nsa_in, i * 512)
            sp.wait_ge(h_ok, 8)
            sp.dma_start(out_d, h[:, :, :]).then_inc(out_st, 16)
            sp.wait_ge(out_st, 16)

        @block.gpsimd
        def _(pool):
            step = Steps(pool, pool_step)

            def select(t, pattern, base, cm, op=ALU.is_ge, fill=0.0):
                step(pool.affine_select(out=t, in_=t, compare_op=op, fill=fill, base=base,
                                        pattern=pattern, channel_multiplier=cm))

            step(pool.memset(ident[:, :], 0.0))
            select(ident[:, :], [[-1, P]], 0, 1, ALU.not_equal, 1.0)
            step(pool.memset(mhalf[:, :], -0.5))
            step(pool.memset(cmask[:, :, :], 0.0))
            select(cmask[:, 0, :], [[-1, P]], 0, 1, fill=NEG)
            select(cmask[:, 2, :], [[-1, P]], 0, 1, fill=NEG)
            step(pool.memset(endm[:, :], 1.0 / TAU))
            select(endm[:, 0:64], [[0, 64]], 63, -1)
            select(endm[:, 64:P], [[0, 64]], -64, 1)
            step(pool.tensor_copy(lt[:, :], endm[:, :]))
            step(pool.tensor_copy(gt[:, :], endm[:, :]))
            select(lt[:, :], [[1, P]], 0, -1)
            select(gt[:, :], [[-1, P]], -1, 1)
            step(pool.memset(okm[:, :, :], 1.0))
            step(pool.memset(negm[:, :, :], 0.0))
            select(okm[:, :, :], [[P, NT], [-CMP_STRIDE, 16]], 1 - CMP_LEN, 1)
            select(negm[:, :, :], [[P, NT], [-CMP_STRIDE, 16]], 1 - CMP_LEN, 1, fill=NEG)
            step(pool.memset(AL[:, :], 1.0))
            step(pool.memset(GE[:, :, :, :], 0.0))
            step(pool.memset(Pc[:, :, :, :], 0.0))
            pool.memset(sm[:, :], 0.0).then_inc(const_mk, 1)
            for k, name in enumerate(POW):
                w = POW_W.get(name, 2)
                pool.wait_ge(pw_req, k + 1)
                pool.tensor_tensor(pwo[:, 0:w], pwi[:, 0:w], mhalf[:, 0:w], ALU.pow).then_inc(pw_done, 1)
                if name == "cqkv":
                    pool.wait_ge(gu_ps, 1)
                    pool.wait_ge(ge_v, 1)
                    pool.memset(AT[0][:, :, :], 0.0)
                    pool.memset(AT[1][:, :, :], 0.0).then_inc(at_zero, 1)
                if name == "mix1":
                    pool.wait_ge(bt_ok, 2)
                    pool.memset(VB[:, :, :, :], 0.0).then_inc(vb_zero, 1)

        @block.tensor
        def _(pe):
            mm = nc.tensor.matmul
            pstep = Steps(pe, pe_step)
            tq = [0]

            def transpose_in(src, n, q=None, gate=True):
                q = tq[0] if q is None else q
                for b in range(n):
                    if not (isinstance(q, int) and q + b < 2):
                        pe.wait_ge(tx_lo, q + (b - 1))
                    k = b % 2
                    for c in range(2):
                        for m in range(NT):
                            o = c * SEQ + m * P
                            t = nc.tensor.transpose(MB[:, k, o:o + P], src(2 * b + c, m), ident[:, :])
                    t.then_inc(tx_ps, 1)
                if isinstance(q, int):
                    tq[0] = q + n

            def unit(s, j, X, kc=4, ncol=512, need=None, par=None, c0=None, cols=0):
                pe.wait_ge(hi_ready, 4 * s + (j + 1))
                pe.wait_ge(lo_ready, 4 * s + (j + 1))
                if need is not None:
                    pe.wait_ge(tx_lo, need)
                par = s % 2 if par is None else par
                first = c0 is None
                k = j % 2
                for c in range(kc):
                    chunk = j * kc + c if first else c
                    hh, ll = (w[:, k, c * ncol:(c + 1) * ncol] for w in (wh, wl))
                    for m in range(NT):
                        o = PG[:, par, m, cols:cols + ncol]
                        xh, xl = (x[:, chunk, m * P:(m + 1) * P] for x in X)
                        beg = c == 0 and (j == 0 or not first)
                        end = c == kc - 1 and (j == 3 or not first)
                        mm(o, xh, hh, start=beg, stop=False)
                        mm(o, xh, ll, start=False, stop=False)
                        last = mm(o, xl, hh, start=False, stop=end)
                last.then_inc(unit_done, 1)

            def unit_t(s, j, X, x0):
                pe.wait_ge(hi_ready, 4 * s + j + 1)
                pe.wait_ge(lo_ready, 4 * s + j + 1)
                for f in range(4):
                    o = PG[:, s % 2, f // 2, (f % 2) * SEQ:(f % 2 + 1) * SEQ]
                    hh, ll = (w[:, j % 2, f * P:(f + 1) * P] for w in (wh, wl))
                    xh, xl = (x[:, x0 + j, :] for x in X)
                    mm(o, hh, xh, start=(j == 0 and f % 2 == 0), stop=False, skip_group_check=True)
                    mm(o, hh, xl, start=False, stop=False, skip_group_check=True)
                    last = mm(o, ll, xh, start=False, stop=(j == 3), skip_group_check=True)
                last.then_inc(unit_done, 1)

            def banks_free(s):
                if isinstance(s, int) and s < 2:
                    return
                pe.wait_ge(evac_a, s - 1)
                pe.wait_ge(evac_v, s - 1)

            def att_step(t, nsa):
                n = NSA_STEPS if nsa else MLA_STEPS
                a0 = MLA_STEPS + 2 if nsa else 0
                SP, PT = (SP1, PT1) if nsa else (SP0, PT0)
                b0 = MLA_STEPS if nsa else 0
                if a0 + t:
                    pe.wait_ge(att_v, a0 + t)
                if b0 + min(max(t - 1, 0), n):
                    pe.wait_ge(pt_sb, b0 + min(max(t - 1, 0), n))
                if 2 <= t:
                    a = t - 2
                    if nsa:
                        g, j = a // 4, a % 4
                        pe.wait_ge(pct_sb, g + 1)
                        pe.wait_ge(c2_v, 1)
                        for m in range(NT):
                            o = MB[:, m, 384:512]
                            mm(o, VB[:, g, j, :], PcT[:, g % 2, m * P:(m + 1) * P], start=True, stop=False)
                            for b, v in enumerate((vs, vw)):
                                for kt in range(m + 1):
                                    p0 = (m + kt) * P
                                    last = mm(o, v[:, kt, g * P:(g + 1) * P], PT[:, b, p0:p0 + P],
                                              start=False, stop=(b == 1 and kt == m))
                    else:
                        for b in range(2):
                            hd = 2 * a + b
                            for m in range(NT):
                                for kt in range(m + 1):
                                    p0 = (m + kt) * P
                                    last = mm(MB[:, 2 * b + m, 384:512], Vm[:, kt, hd * P:(hd + 1) * P],
                                              PT[:, b, p0:p0 + P], start=(kt == 0), stop=(kt == m))
                    last.then_inc(pv_done, 1)
                if nsa and t in CP_STEP:
                    pe.wait_ge(cs_ok, CP_STEP[t] + 1)
                    for m in range(NT):
                        last = nc.tensor.transpose(MB[:, 2 + m, 384:512],
                                                   Pc[:, m, :, :].rearrange("p j n -> p (j n)"), ident[:, :])
                    last.then_inc(cp_ps, 1)
                if 1 <= t <= n:
                    for b in range(2):
                        for k in range(3):
                            last = nc.tensor.transpose(MB[:, 2 + b, k * P:(k + 1) * P],
                                                       SP[:, b, k * P:(k + 1) * P], ident[:, :])
                    last.then_inc(pt_done, 1)
                if t < n:
                    for b in range(2):
                        for m in range(NT):
                            o = MB[:, b, m * P:m * P + (m + 1) * P]
                            if nsa:
                                g, j = t // 4, t % 4
                                last = mm(o, QT[:, g % 2, j, m * P:(m + 1) * P],
                                          (ksT, kwT)[b][:, g, 0:(m + 1) * P], start=True, stop=True)
                            else:
                                hd = 2 * t + b
                                mm(o, QnT[:, hd, m * P:(m + 1) * P], KnT[:, hd, 0:(m + 1) * P],
                                   start=True, stop=False)
                                r = slice(64 * b, 64 * b + 64)
                                last = mm(o, QrT[r, t, m * P:(m + 1) * P], KrT[r, 0:(m + 1) * P],
                                          start=False, stop=True)
                    last.then_inc(s_done, 1)

            def four_heads(banks, src, n0=0):
                for c in range(4):
                    for m in range(NT):
                        o = (c % 2) * SEQ + m * P
                        t = nc.tensor.transpose(banks(c // 2)[:, o:o + P], src(c, m), ident[:, :])
                return t

            def pair_of(hd):
                return hd // 2, slice(64 * (hd % 2), 64 * (hd % 2) + 64)

            def gla_gap(k):
                if k == 0:
                    for m in range(NT):
                        last = mm(MB[:, 2 + m, :], AL[0:17, m * P:(m + 1) * P], aw[0:17, :], start=True, stop=True)
                    last.then_inc(ga_ps, 1)
                if k == 1:
                    pe.wait_ge(ga_ok, 1)
                    for m in range(NT):
                        mm(MB[:, m, :], lt[:, :], loga[:, m, :], start=True, stop=True)
                        last = mm(MB[:, 2 + m, :], gt[:, :], loga[:, m, :], start=True, stop=True)
                    last.then_inc(gb_ps, 1)
                if k == 2:
                    pe.wait_ge(ge_v, 1)
                    four_heads(lambda b: MB[:, b, :], lambda c, m: qg[:, m, c * P:(c + 1) * P])
                    four_heads(lambda b: MB[:, 2 + b, :], lambda c, m: kinv[:, m, c * P:(c + 1) * P]).then_inc(gt_ps, 1)
                if k == 3:
                    pe.wait_ge(gt_sb, 1)
                    for c in (0, 2, 1):
                        r = slice(64 * (c % 2), 64 * (c % 2) + 64)
                        if c == 1:
                            pstep(last)
                        for hd in range(8):
                            pr, rr = pair_of(hd)
                            last = mm(MB[rr, pr, c * P:(c + 1) * P], kg[r, c // 2, hd * 64:(hd + 1) * 64],
                               vg[r, c // 2, hd * P:(hd + 1) * P], start=True, stop=True)
                    for pr in range(4):
                        for m in range(NT):
                            o = 384 + 4 * pr + 2 * m
                            last = mm(MB[:, 0, o:o + 2], loga[:, m, pr * P:(pr + 1) * P], endm[:, 0:P:64],
                                      start=True, stop=True)
                    last.then_inc(gu_ps, 1)
                if k == 4:
                    pe.wait_ge(gs_ok, 1)
                    for odd in range(2):
                        if odd:
                            pstep(last)
                        for m in range(NT):
                            for hd in range(odd, 8, 2):
                                pr, rr = pair_of(hd)
                                last = mm(MB[:, 2 * m + hd // 4, (hd % 4) * P:(hd % 4 + 1) * P],
                                          kiT[rr, pr, m * P:(m + 1) * P], qdT[rr, pr, m * P:(m + 1) * P],
                                          start=True, stop=True)
                    last.then_inc(at_ps, 1)
                if k == 5:
                    pe.wait_ge(at_ok, 1)
                    for m in range(NT):
                        for hd in range(8):
                            e = hd % 4
                            mm(MB[:, 2 * m + hd // 4, e * P:(e + 1) * P], AT[m][:, hd // 4, e * P:(e + 1) * P],
                               vg[:, m, hd * P:(hd + 1) * P], start=(e == 0), stop=False, skip_group_check=True)
                    for odd in range(2):
                        if odd:
                            pstep(last)
                        for hd in range(odd, 8, 2):
                            pr, rr = pair_of(hd)
                            e = hd % 4
                            for c in range(1, 4):
                                q = slice(64 * (c % 2), 64 * (c % 2) + 64)
                                last = mm(MB[q, 2 * (c // 2) + hd // 4, e * P:(e + 1) * P],
                                          qdT[rr, pr, c * 64:(c + 1) * 64], SS[rr, pr, c - 1, :],
                                          start=False, stop=True, skip_group_check=True)
                    last.then_inc(go_ps, 1)

            def nsa_op(op, g):
                ob = (SQ + 2 + g) % 2
                if op == "qt":
                    pe.wait_ge(qe_ok, g + 1)
                    four_heads(lambda b: PG[:, ob, b, :],
                               lambda c, m: zq[:, g % 2, m, c * P:(c + 1) * P]).then_inc(qt_ps, 1)
                if op == "cs":
                    pe.wait_ge(qt_sb, g + 1)
                    pe.wait_ge(c2_a, 1)
                    for m in range(NT):
                        for j in range(4):
                            o = m * 64 + j * 16
                            last = mm(PG[:, ob, 0, o:o + 16], QT[:, g % 2, j, m * P:(m + 1) * P],
                                      KcT[:, g, 0:16], start=True, stop=True)
                    last.then_inc(cs_ps, 1)
                if op == "st":
                    att_step(g, True)

            def gap(s, j):
                if (s, j) == (QG, 1):
                    pe.wait_ge(zn_ok, 1)
                    transpose_in(lambda c, m: zc[:, m, 16 + c * P:16 + (c + 1) * P], 4)
                    for m in range(NT):
                        last = nc.tensor.transpose(MB[0:16, 2, m * P:(m + 1) * P], zc[:, m, 0:16], ident[:, :])
                    last.then_inc(al_ps, 1)
                if (s, j) == (UQR + 2, 0):
                    pe.wait_ge(qr_ok, 1)
                    pe.wait_ge(kr_ok, 1)
                    pe.wait_ge(al_sb, 1)
                    pe.wait_ge(tx_lo, TQ["gla"])
                    four_heads(lambda b: MB[:, 2 + b, :], lambda c, m: qr[:, m, c * P:(c + 1) * P])
                    for m in range(NT):
                        last = nc.tensor.transpose(MB[:, 1, m * P:(m + 1) * P],
                                                   krd[:, m, :, :].rearrange("p a e -> p (a e)"), ident[:, :])
                    last.then_inc(qrt_ps, 1)
                if (s, j) in MLA_AT:
                    t = MLA_AT[(s, j)]
                    if t == 0:
                        pe.wait_ge(qrt_sb, 1)
                        pe.wait_ge(evac_a, UKK + 2)
                        pe.wait_ge(evac_v, UKK + 2)
                    if t == 2:
                        pe.wait_ge(evac_a, UKV + 2)
                        pe.wait_ge(evac_v, UKV + 2)
                    att_step(t, False)
                if (s, j) in GLA_AT:
                    if GLA_AT[(s, j)] == 0:
                        pe.wait_ge(att_v, MLA_STEPS + 2)
                    gla_gap(GLA_AT[(s, j)])
                if (s, j) == (OUT0, 0):
                    pe.wait_ge(go_ok, 1)
                    transpose_in(lambda c, m: gg[:, m, c * P:(c + 1) * P], 4)
                if (s, j) in KT_AT:
                    k = KT_AT[(s, j)]
                    pe.wait_ge(ke_ok, k + 1)
                    if k == 1:
                        pe.wait_ge(evac_a, SVC + 1)
                    if k:
                        pe.wait_ge(kt_sb, k)
                    four_heads(lambda b: MB[:, 2 + b, :], lambda c, m: KB[:, k % 2, m, c * P:(c + 1) * P])\
                        .then_inc(kt_ps, 1)
                if (s, j) == (SW1 + 1, 2):
                    pe.wait_ge(gl_ok, 1)
                    pe.wait_ge(tx_lo, TQ["ffn1"])
                    mm(MB[:, 0, 0:P], w2s[:, 0, :], GE[:, 0, :, :].rearrange("p g n -> p (g n)"), start=True, stop=True)
                    for g in range(4):
                        for jj in range(4):
                            last = mm(MB[32 * jj:32 * jj + 32, 1, g * P:(g + 1) * P], GE[:, 1, g, :], w2s[:, 1, :],
                                      start=True, stop=True)
                    last.then_inc(c2_ps, 1)
                for op, g in NSA_AT.get((s, j), ()):
                    nsa_op(op, g)

            def nsa_guard(s):
                g = s - (SQ + 2)
                if 0 <= g < 4:
                    pe.wait_ge(cs_in, g + 1)
                    pe.wait_ge(qt_sb, g + 1)

            pe.wait_ge(const_mk, 1)
            pe.wait_ge(const_in, 16 * N_CONST)
            nc.tensor.transpose(MB[:, 2, 0:72], vin[:, :], ident[0:72, 0:72])
            nc.tensor.transpose(MB[:, 2, P:P + 64], vin2[:, :], ident[0:64, 0:64]).then_inc(vt_ps, 1)

            def norm_in(k):
                pe.wait_ge(hn_a, k + 1)
                pe.wait_ge(hn_v, k + 1)
                transpose_in(lambda c, m: Fm[:, m, c * P:(c + 1) * P], 8)

            norm_in(0)
            for s in range(0, OUT0):
                banks_free(s)
                for j in range(4):
                    if s in (UQN, UQN + 1):
                        unit_t(s, j, XB, 0)
                    elif s == UQR:
                        unit(s, j, XB, 1)
                    elif s in (UKK, UKK + 1):
                        unit_t(s, j, XB, 4)
                    elif s in (UKV, UKV + 1):
                        unit(s, j, (XBh[:, 4:8, :], XBl[:, 4:8, :]), 1)
                    else:
                        need = TQ["cqkv"] if (s, j) == (0, 0) else None
                        unit(s, j, XA, 4, shape_of(s)[1], need)
                    if (s, j) == (QG, 3):
                        pe.wait_ge(tx_lo, TQ["gla"])
                    gap(s, j)

            for layer in range(2):
                s0 = OUTS[layer]
                nsa_guard(s0)
                banks_free(s0)
                for j in range(4):
                    if layer == 0 and j == 2:
                        pe.wait_ge(tx_lo, TQ["ffn0"])
                    if j == 0:
                        pe.wait_ge(att_v, MLA_STEPS + 2 + layer * (NSA_STEPS + 2))
                    unit(s0, j, XB)
                    gap(s0, j)
                nsa_guard(s0 + 1)
                with pe.Fori(0, 3) as i:
                    banks_free(i + (s0 + 1))
                    for j in range(4):
                        unit(i + (s0 + 1), j, XB, par=(i + (s0 + 1)) % 2)
                norm_in((1, 3)[layer])
                pe.wait_ge(pp_in, 16 * (layer + 1))
                transpose_in(lambda c, m: pp[:, m, c * P:(c + 1) * P], 1)
                for g, n in enumerate(GROUPS):
                    b = ffn_base(layer, g)
                    q0 = TQ[f"hid{layer}"] + 2 * sum(GROUPS[:g])

                    def hid_in(p):
                        pe.wait_ge(evac_v, p * 2 + (b + 2))
                        transpose_in(lambda c, m: Hb[:, m, c * P:(c + 1) * P], 2, q=p * 2 + q0)

                    for j in range(8):
                        if j % 4 == 0:
                            banks_free(b + j // 4)
                        need = TQ[f"hid{layer}"] if (g, j) == (0, 0) else None
                        unit(b + j // 4, j % 4, XA, need=need)
                    with pe.Fori(0, n - 1) as i:
                        for j in range(8):
                            s = i * 2 + (b + 2 + j // 4)
                            if j % 4 == 0:
                                banks_free(s)
                            unit(s, j % 4, XA, par=(b + j // 4) % 2)
                            if j == 0:
                                hid_in(i)
                    d0 = b + 2 * n
                    banks_free(d0)
                    for j in range(4):
                        need = q0 + 2 * n if (j + 1) * n > 4 * (n - 1) else q0 + 2 * (n - 1)
                        unit(d0, j, XB, kc=n, need=need)
                        if j == 0:
                            hid_in(n - 1)
                    tq[0] = q0 + 2 * n
                    with pe.Fori(0, 3) as i:
                        banks_free(i + (d0 + 1))
                        for j in range(4):
                            unit(i + (d0 + 1), j, XB, kc=n, par=(i + (d0 + 1)) % 2)
                with pe.Fori(0, 4) as i:
                    banks_free(i + PROJ[layer])
                    for j in range(4):
                        unit(i + PROJ[layer], j, PX, kc=2, ncol=P, par=i % 2, c0=0, cols=j * P)
                pe.wait_ge(upd, 4 * layer + 4)
                transpose_in(lambda c, m: h[:, m, c * P:(c + 1) * P], 8)
                pe.wait_ge(tx_lo, tq[0])
                with pe.Fori(0, 4) as i:
                    banks_free(i + GATE[layer])
                    for j in range(4):
                        unit(i + GATE[layer], j, XA, par=i % 2)
                if layer == 1:
                    break
                norm_in(2)
                for s in range(L1, OUT1):
                    banks_free(s)
                    nsa_guard(s)
                    for j in range(4):
                        if s == SW1:
                            kv, k = j // 2, j % 2
                            pe.wait_ge(hi_ready, 4 * s + j + 1)
                            pe.wait_ge(lo_ready, 4 * s + j + 1)
                            pe.wait_ge(bl_ok, kv + 1)
                            for l in range(16):
                                o = PG[:, s % 2, kv, 0:60]
                                hh, ll = (w[:, k, l * P:(l + 1) * P] for w in (wh, wl))
                                bh, bl = (x[:, kv, 16 * k + l, :] for x in (BLh, BLl))
                                mm(o, hh, bh, start=(k == 0 and l == 0), stop=False)
                                mm(o, hh, bl, start=False, stop=False)
                                last = mm(o, ll, bh, start=False, stop=(k == 1 and l == 15))
                            last.then_inc(unit_done, 1)
                        else:
                            need = TQ["ffn1"] if (s, j) == (L1, 0) else None
                            unit(s, j, XA, 4, shape_of(s)[1], need)
                        gap(s, j)

        @block.scalar
        def _(act):
            A = nc.scalar.activation
            step = Steps(act, act_step)

            def flat(t):
                return t.rearrange("p a t -> p (a t)")

            def split(s, j, w=2048):
                act.wait_ge(raw_in[j], s * 16 + 16)
                if not (isinstance(s, int) and 4 * s + j < 2):
                    act.wait_ge(unit_done, s * 4 + (j - 1))
                A(wh[:, j % 2, 0:w], raw[:, j, 0:w], ACT.Copy).then_inc(hi_ready, 1)

            def split_in(X, n, q, c0, col=None):
                for b in range(n):
                    act.wait_ge(tx_ps, q + (b + 1))
                    src = MB[:, b % 2, :]
                    if col is None:
                        A(flat(X[:, bass.ds(c0 + 2 * b, 2), :]), src, ACT.Copy).then_inc(tx_hi, 1)
                    else:
                        for c in range(2):
                            k = 2 * b + c
                            last = A(X[:, c0 + k, :], src[:, c * SEQ:(c + 1) * SEQ], ACT.Copy,
                                     scale=vcol[:, col + k:col + k + 1])
                        last.then_inc(tx_hi, 1)

            def norm_out(k):
                if k == 0:
                    act.wait_ge(x_in, 32)
                elif k == 2:
                    act.wait_ge(h_ok, 4)
                else:
                    act.wait_ge(upd, 2 + 4 * (k // 2))
                for m in range(NT):
                    A(Fm[:, m, :], h[:, m, :], ACT.Square, accum_out=ss[:, m, 0:1]).then_inc(ssq, 1)
                act.wait_ge(ssq, 2 * k + 2)
                act.wait_ge(pw_done, POW.index(("mix0", "ffn0", "mix1", "ffn1")[k]) + 1)
                A(Fm[:, 0, :], h[:, 0, :], ACT.Copy, scale=pwo[:, 0:1]).then_inc(hn_a, 1)

            def att_stage(t, nsa):
                n = NSA_STEPS if nsa else MLA_STEPS
                SP, PT = (SP1, PT1) if nsa else (SP0, PT0)
                b0 = MLA_STEPS if nsa else 0
                if 1 <= t <= n:
                    act.wait_ge(pt_done, b0 + t)
                    A(PT[:, :, :], MB[:, 2:4, 0:384], ACT.Copy).then_inc(pt_sb, 1)
                if nsa and t in CP_STEP:
                    g = CP_STEP[t]
                    act.wait_ge(cp_ps, g + 1)
                    A(PcT[:, g % 2, :].rearrange("p (m t) -> p m t", m=2), MB[:, 2:4, 384:512],
                      ACT.Copy).then_inc(pct_sb, 1)
                if t < n:
                    act.wait_ge(mx_ok, b0 + t + 1)
                    for b in range(2):
                        for m in range(NT):
                            c = SP[:, b, m * P:m * P + (m + 1) * P]
                            k = 2 * m + b
                            last = A(c, c, ACT.Exp, bias=sm[:, k:k + 1], accum_out=sm[:, 4 + k:5 + k])
                    last.then_inc(exp_ok, 1)
                if t >= 2:
                    act.wait_ge(pv_done, b0 + t - 1)
                    for b in range(1 if nsa else 2):
                        hd = t - 2 if nsa else 2 * (t - 2) + b
                        last = A(XBh[:, hd, :].rearrange("p (m t) -> p m t", m=2), MB[:, 2 * b:2 * b + 2, 384:512],
                                 ACT.Copy)
                    last.then_inc(o_hi, 1)

            def gla_stage(k):
                if k == 0:
                    act.wait_ge(ga_ps, 1)
                    A(loga[:, :, :], MB[:, 2:4, :], ACT.Copy).then_inc(ga_t, 1)
                    act.wait_ge(ga_n, 1)
                    step(A(E1[:, :, :], E1[:, :, :], ACT.Exp))
                    A(E1[:, :, :], E1[:, :, :], ACT.Ln, bias=1.0).then_inc(ga_l, 1)
                if k == 1:
                    act.wait_ge(gb_ps, 1)
                    A(E1[:, :, :], MB[:, 0:2, :], ACT.Exp).then_inc(ge_a, 1)
                    A(kinv[:, :, :], MB[:, 0:2, :], ACT.Exp, scale=-1.0).then_inc(ge_a, 1)
                    A(rt[:, :, :], MB[:, 2:4, :], ACT.Exp).then_inc(ge_a, 1)
                if k == 2:
                    act.wait_ge(gt_ps, 1)
                    A(flat(qdT[:, :, :]), flat(MB[:, 0:2, :]), ACT.Copy)
                    A(flat(kiT[:, :, :]), flat(MB[:, 2:4, :]), ACT.Copy).then_inc(gt_sb, 1)
                if k == 3:
                    act.wait_ge(gu_ps, 1)
                    A(flat(decs[:, :, :]), MB[:, 0, 384:400], ACT.Exp).then_inc(gd_sb, 1)
                if k == 5:
                    act.wait_ge(go_ps, 1)
                    for m in range(NT):
                        last = A(AT[m][:, :, :], MB[:, 2 * m:2 * m + 2, :], ACT.Square)
                    last.then_inc(go_sq, 1)

            def evac(s):
                act.wait_ge(unit_done, 4 * s + 4)
                src = PG[:, s % 2, 0, :]
                if s in (ZC0, ZC1, ZC2):
                    w = shape_of(s)[1]
                    A(zc[:, 0, 512 * s:512 * s + w], src[:, 0:w], ACT.Copy).then_inc(evac_a, 1)
                elif s in (UQN, UQN + 1, UKK, UKK + 1):
                    t, c = (QnT, 4 * (s - UQN)) if s < UKK else (KnT, 4 * (s - UKK))
                    A(flat(t[:, c:c + 2, :]), src, ACT.Copy).then_inc(evac_a, 1)
                elif s in (GG, GG + 1):
                    act.wait_ge(ge_v, 1)
                    if s == GG + 1:
                        act.wait_ge(evac_v, GG + 1)
                    A(rt[:, :, :], PG[:, s % 2, :, :], ACT.Tanh, scale=0.5).then_inc(evac_a, 1)
                elif s in COPY0:
                    t, c = COPY0[s]
                    A(t[:, 0, c:c + 512], src, ACT.Copy).then_inc(evac_a, 1)
                elif s == SVC:
                    A(KB[:, 1, 0, :], src, ACT.Copy).then_inc(evac_a, 1)
                elif s == SW1:
                    act.wait_ge(ge_x, 1)
                    A(GU[:, :, :], GU[:, :, :], ACT.Tanh, scale=GELU_C / 2).then_inc(ge_e, 1)
                    act.drain().then_inc(evac_a, 1)
                elif s == SGT:
                    act.wait_ge(evac_v, SGT + 1)
                    A(gates[:, :, :], gates[:, :, :], ACT.Tanh, scale=0.5).then_inc(gx_e, 1)
                    act.drain().then_inc(evac_a, 1)
                else:
                    act.drain().then_inc(evac_a, 1)

            def stage(s, j):
                k = before(s, j)
                if j == 0 and s not in (0, L1, OUT1):
                    evac(s - 1)
                if k == (QG, 1):
                    act.wait_ge(tx_ps, TQ["cqkv"] + 1)
                    split_in(XBh, 4, TQ["cqkv"], 0, 64)
                    act.wait_ge(al_ps, 1)
                    act.wait_ge(const_mk, 1)
                    A(AL[0:16, :], MB[0:16, 2, 0:SEQ], ACT.Copy).then_inc(al_sb, 1)
                if k == (UQR + 2, 0):
                    act.wait_ge(qrt_ps, 1)
                    A(flat(QrT[:, :, :]), flat(MB[:, 2:4, :]), ACT.Copy)
                    A(KrT[:, :], MB[:, 1, 0:SEQ], ACT.Copy).then_inc(qrt_sb, 1)
                if k in MLA_AT:
                    att_stage(MLA_AT[k], False)
                if k in GLA_AT:
                    gla_stage(GLA_AT[k])
                if k == (OUT0, 0):
                    split_in(XBh, 4, TQ["gla"], 8)
                    act.wait_ge(go_ok, 1)
                    act.dma_start(wbc[:, :], T["ln_mix_post"][0:1, :].broadcast_to([P, D])).then_inc(wbc_in, 16)
                    act.dma_start(pp[:, :, :], p_d[0]).then_inc(pp_in, 16)
                if k in KT_AT:
                    n = KT_AT[k]
                    act.wait_ge(kt_ps, n + 1)
                    A(flat((kcT, vcT, ksT, kwT)[n][:, :, :]), flat(MB[:, 2:4, :]), ACT.Copy).then_inc(kt_sb, 1)
                if (s, j) in ((SKC + 1, 3), (SVC + 1, 3)):
                    n = s - SKC - 1
                    act.wait_ge(bt_ok, n + 1)
                    A(BLh[:, n, :, :], BT[:, :, :], ACT.Copy).then_inc(bh_ok, 1)
                if k == (SW1 + 1, 2):
                    act.wait_ge(c2_ps, 1)
                    A(flat(KcT[:, :, :]), MB[:, 0, 0:P], ACT.Copy).then_inc(c2_a, 1)
                for op, g in NSA_AT.get(k, ()):
                    if op == "qt":
                        if g == 3:
                            evac(SQ + 3)
                        act.wait_ge(qt_ps, g + 1)
                        A(flat(QT[:, g % 2, :, :]), flat(PG[:, (SQ + g) % 2, :, :]), ACT.Copy).then_inc(qt_sb, 1)
                    if op == "cs":
                        act.wait_ge(cs_in, g + 1)
                        A(csc[:, :, :, :], csc[:, :, :, :], ACT.Exp).then_inc(cs_e, 1)
                    if op == "st":
                        att_stage(g, True)
                if k == (SQ + 3, 3):
                    act.wait_ge(att_v, MLA_STEPS + NSA_STEPS + 4)
                    act.dma_start(wbc[:, :], T["ln_mix_post"][1:2, :].broadcast_to([P, D])).then_inc(wbc_in, 16)
                    act.dma_start(pp[:, :, :], p_d[1]).then_inc(pp_in, 16)

            act.wait_ge(vt_ps, 1)
            A(vcol[:, :], MB[:, 2, 0:72], ACT.Copy).then_inc(vt_sb, 1)
            A(posT[:, :], MB[:, 2, P:P + 64], ACT.Copy).then_inc(vt_sb, 1)
            act.wait_ge(vt_sb, 2)
            act.wait_ge(ang_ok, 1)
            A(sinT[:, :, :], ang[:, :, :], ACT.Sin)
            A(cosT[:, :, :], kk[:, :, :], ACT.Sin).then_inc(trig_ok, 1)
            norm_out(0)
            split_in(XAh, 8, TQ["mix0"], 0, 0)

            for s in range(0, OUT0 + 1):
                for j in range(4):
                    split(s, j, shape_of(s)[0] * shape_of(s)[1])
                    stage(s, j)

            for layer in range(2):
                s0 = OUTS[layer]

                def mixer_panel(i):
                    s = i + s0
                    act.wait_ge(unit_done, s * 4 + 4)
                    A(rt[:, 0, :], PG[:, s % 2, 0, :], ACT.Square, accum_out=ss[:, 0, bass.ds(i, 1)]).then_inc(sq_done, 1)
                    act.wait_ge(mul_done, i + (4 * layer + 1))
                    A(rt[:, 1, :], PG[:, s % 2, 1, :], ACT.Square, accum_out=ss[:, 1, bass.ds(i, 1)]).then_inc(evac_a, 1)

                with act.Fori(0, 3) as i:
                    for j in range(4):
                        split(i + (s0 + 1), j)
                        if j == 0:
                            mixer_panel(i)
                for g, n in enumerate(GROUPS):
                    b = ffn_base(layer, g)
                    q0 = TQ[f"hid{layer}"] + 2 * sum(GROUPS[:g])

                    def gate_tanh(s):
                        act.wait_ge(unit_done, s * 4 + 4)
                        act.wait_ge(evac_v, s)
                        A(Eb[:, :, :], PG[:, b % 2, :, :], ACT.Tanh, scale=0.5).then_inc(evac_a, 1)

                    def down_panel(i, g, d):
                        s = i + d
                        if g == 0:
                            act.wait_ge(unit_done, s * 4 + 4)
                            A(Fm[:, 0, bass.ds(i * 512, 512)], PG[:, s % 2, 0, :], ACT.Copy).then_inc(evac_a, 1)
                            return
                        act.drain().then_inc(evac_a, 1)
                        if g == 2:
                            act.wait_ge(add_done, i + (4 * layer + 1))
                            A(rt[:, 0, :], Fm[:, 0, bass.ds(i * 512, 512)], ACT.Square,
                              accum_out=ss[:, 0, bass.ds(i, 1)]).then_inc(sq_done, 1)
                            act.wait_ge(evac_v, s + 1)
                            A(rt[:, 1, :], Fm[:, 1, bass.ds(i * 512, 512)], ACT.Square,
                              accum_out=ss[:, 1, bass.ds(i, 1)]).then_inc(sq_done, 1)

                    split(b, 0)
                    if g == 0:
                        mixer_panel(3)
                        act.wait_ge(evac_v, s0 + 4)
                        act.dma_start(wbc[:, :], T["ln_ffn_post"][layer:layer + 1, :].broadcast_to([P, D]))\
                            .then_inc(wbc_in, 16)
                        norm_out((1, 3)[layer])
                        split_in(XAh, 8, TQ[f"ffn{layer}"], 0, 16 + 32 * layer)
                        split_in(PXh, 1, TQ[f"p{layer}"], 0)
                    else:
                        down_panel(3, g - 1, d0)
                    for j in range(1, 4):
                        split(b, j)
                    split(b + 1, 0)
                    gate_tanh(b)
                    for j in range(1, 4):
                        split(b + 1, j)
                    with act.Fori(0, n - 1) as i:
                        s = i * 2 + (b + 2)
                        split(s, 0)
                        act.drain().then_inc(evac_a, 1)
                        split(s, 1)
                        split_in(XBh, 2, i * 2 + q0, i * 4)
                        split(s, 2)
                        split(s, 3)
                        split(s + 1, 0)
                        gate_tanh(s)
                        for j in range(1, 4):
                            split(s + 1, j)
                    d0 = b + 2 * n
                    w = n * 512
                    split(d0, 0, w)
                    act.drain().then_inc(evac_a, 1)
                    split(d0, 1, w)
                    split_in(XBh, 2, q0 + 2 * (n - 1), 4 * (n - 1))
                    split(d0, 2, w)
                    split(d0, 3, w)
                    with act.Fori(0, 3) as i:
                        split(i + (d0 + 1), 0, w)
                        down_panel(i, g, d0)
                        for j in range(1, 4):
                            split(i + (d0 + 1), j, w)
                pr, gt0 = PROJ[layer], GATE[layer]

                def proj_panel(i):
                    s = i + pr
                    act.wait_ge(unit_done, s * 4 + 4)
                    A(PJ[:, 0, bass.ds(i * 512, 512)], PG[:, s % 2, 0, :], ACT.Copy).then_inc(evac_a, 1)

                def gate_panel(i):
                    act.wait_ge(evac_v, i + (gt0 + 1))
                    A(Eb[:, :, :], Eb[:, :, :], ACT.Tanh, scale=0.5).then_inc(evac_a, 1)

                split(pr, 0, 256)
                down_panel(3, 2, d0)
                act.wait_ge(upd, 4 * layer + 4)
                act.dma_start(wbc[:, :], T["ple_b_gate"][layer:layer + 1, :].broadcast_to([P, D])).then_inc(wbc_in, 16)
                for j in range(1, 4):
                    split(pr, j, 256)
                with act.Fori(0, 3) as i:
                    split(i + (pr + 1), 0, 256)
                    proj_panel(i)
                    for j in range(1, 4):
                        split(i + (pr + 1), j, 256)
                split(gt0, 0)
                proj_panel(3)
                split_in(XAh, 8, TQ[f"ple{layer}"], 0)
                for j in range(1, 4):
                    split(gt0, j)
                with act.Fori(0, 3) as i:
                    split(i + (gt0 + 1), 0)
                    gate_panel(i)
                    for j in range(1, 4):
                        split(i + (gt0 + 1), j)
                if layer == 1:
                    gate_panel(3)
                    break
                for s in range(L1, OUT1 + 1):
                    for j in range(4):
                        split(s, j, shape_of(s)[0] * shape_of(s)[1])
                        if (s, j) == (L1, 0):
                            gate_panel(3)
                            norm_out(2)
                            split_in(XAh, 8, TQ["mix1"], 0, 32)
                        stage(s, j)

        @block.vector
        def _(v):
            V = nc.vector
            step = Steps(v, dve_step)

            def flat(t):
                return t.rearrange("p a t -> p (a t)")

            def split(s, j, w=2048):
                v.wait_ge(hi_ready, s * 4 + (j + 1))
                V.tensor_tensor(wl[:, j % 2, 0:w], raw[:, j, 0:w], wh[:, j % 2, 0:w].bitcast(F32),
                                ALU.subtract).then_inc(lo_ready, 1)

            def split_in(X, n, q, c0, col=None):
                for b in range(n):
                    v.wait_ge(tx_hi, q + (b + 1))
                    src = MB[:, b % 2, :]
                    if col is None:
                        c = bass.ds(c0 + 2 * b, 2)
                        V.tensor_tensor(flat(X[1][:, c, :]), src, flat(X[0][:, c, :]).bitcast(F32),
                                        ALU.subtract).then_inc(tx_lo, 1)
                    else:
                        for c in range(2):
                            k = 2 * b + c
                            last = V.scalar_tensor_tensor(
                                X[1][:, c0 + k, :], src[:, c * SEQ:(c + 1) * SEQ], vcol[:, col + k:col + k + 1],
                                X[0][:, c0 + k, :].bitcast(F32), ALU.mult, ALU.subtract)
                        last.then_inc(tx_lo, 1)

            def ask(name):
                v.wait_ge(pw_done, POW.index(name) + 1)

            def norm_out(k):
                name = ("mix0", "ffn0", "mix1", "ffn1")[k]
                v.wait_ge(ssq, 2 * k + 2)
                V.tensor_scalar(pwi[:, 0:2], ss[:, :, 0], 1.0 / D, EPS, ALU.mult, ALU.add).then_inc(pw_req, 1)
                ask(name)
                V.tensor_scalar(Fm[:, 1, :], h[:, 1, :], pwo[:, 1:2], None, ALU.mult).then_inc(hn_v, 1)

            def post_norm(name):
                step(V.tensor_reduce(pwi[:, 0:2], ss[:, :, :], AX.X, ALU.add))
                V.tensor_scalar(pwi[:, 0:2], pwi[:, 0:2], 1.0 / D, EPS, ALU.mult, ALU.add).then_inc(pw_req, 1)
                ask(name)
                for m in range(NT):
                    V.scalar_tensor_tensor(h[:, m, :], Fm[:, m, :], pwo[:, m:m + 1], h[:, m, :],
                                           ALU.mult, ALU.add).then_inc(upd, 1)

            def rope(src, dst, cos, sin, hd, done, par_sem):
                for m in range(NT):
                    n = 512 // (2 * hd)
                    a, b = (rt[:, k, :].rearrange("p (h x e) -> p h x e", x=2, e=hd) for k in range(2))
                    cs, sn = (t[:, m, ::64 // hd].rearrange("p (h x e) -> p h x e", h=1, x=1)
                              .broadcast_to([P, n, 2, hd]) for t in (cos, sin))
                    V.tensor_tensor(a, src(m), cs, ALU.mult)
                    ins = V.tensor_tensor(b, src(m), sn, ALU.mult)
                    if m == NT - 1:
                        ins.then_inc(par_sem, 1)
                        v.wait_ge(par_sem, cur[0] + 1)
                    else:
                        step(ins)
                    V.tensor_tensor(dst(m)[:, :, 0, :], a[:, :, 0, :], b[:, :, 1, :], ALU.subtract)
                    last = V.tensor_tensor(dst(m)[:, :, 1, :], a[:, :, 1, :], b[:, :, 0, :], ALU.add)
                    if m == 0:
                        step(last)
                last.then_inc(done, 1)

            cur = [0]

            def att_stage(t, nsa):
                n = NSA_STEPS if nsa else MLA_STEPS
                SP = SP1 if nsa else SP0
                b0 = MLA_STEPS if nsa else 0
                scale = NSA_SCALE if nsa else MLA_SCALE
                if t < n:
                    v.wait_ge(s_done, b0 + t + 1)
                    for b in range(2):
                        last = V.scalar_tensor_tensor(SP[:, b, :], MB[:, b, 0:384], scale, flat(cmask[:, :, :]),
                                                      ALU.mult, ALU.add)
                    step(last)
                    V.tensor_reduce(sm[:, 0:2], SP[:, :, 0:P], AX.X, ALU.max, negate=True)
                    V.tensor_reduce(sm[:, 2:4], SP[:, :, P:384], AX.X, ALU.max, negate=True).then_inc(mx_ok, 1)
                    v.wait_ge(exp_ok, b0 + t + 1)
                    step(V.reciprocal(sm[:, 8:12], sm[:, 4:8]))
                    if nsa:
                        f = sm[:, 8:12].rearrange("p (m b) -> p m b", m=2)
                        step(V.tensor_tensor(f, f, gates[:, :, 3 * t + 1:3 * t + 3], ALU.mult))
                    for b in range(2):
                        for m in range(NT):
                            c = SP[:, b, m * P:m * P + (m + 1) * P]
                            k = 8 + 2 * m + b
                            last = V.tensor_scalar(c, c, sm[:, k:k + 1], None, ALU.mult)
                    if t < 2:
                        last.then_inc(att_v, 1)
                if t >= 2:
                    v.wait_ge(o_hi, b0 + t - 1)
                    for b in range(1 if nsa else 2):
                        hd = t - 2 if nsa else 2 * (t - 2) + b
                        x = [q[:, hd, :].rearrange("p (m t) -> p m t", m=2) for q in XB]
                        last = V.tensor_tensor(x[1], MB[:, 2 * b:2 * b + 2, 384:512], x[0].bitcast(F32), ALU.subtract)
                    last.then_inc(att_v, 1)

            def gla_stage(k):
                if k == 0:
                    v.wait_ge(ga_t, 1)
                    V.scalar_tensor_tensor(flat(E1[:, :, :]), flat(loga[:, :, :]), -1.0, flat(loga[:, :, :]),
                                           ALU.mult, ALU.min).then_inc(ga_n, 1)
                    v.wait_ge(ga_l, 1)
                    V.scalar_tensor_tensor(flat(loga[:, :, :]), flat(loga[:, :, :]), 0.0, flat(E1[:, :, :]),
                                           ALU.min, ALU.subtract).then_inc(ga_ok, 1)
                if k == 1:
                    v.wait_ge(evac_a, KG + 1)
                    v.wait_ge(ge_a, 1)
                    V.scalar_tensor_tensor(flat(qg[:, :, :]), flat(qg[:, :, :]), 0.125, flat(E1[:, :, :]),
                                           ALU.mult, ALU.mult)
                    v.wait_ge(ge_a, 2)
                    V.tensor_tensor(kinv[:, :, :], kg[:, :, :], kinv[:, :, :], ALU.mult)
                    v.wait_ge(ge_a, 3)
                    V.tensor_tensor(kg[:, :, :], kg[:, :, :], rt[:, :, :], ALU.mult).then_inc(ge_v, 1)
                if k == 3:
                    v.wait_ge(gd_sb, 1)
                    step(V.tensor_copy(SS[:, :, 0, :], MB[:, :, 0:P]))
                    for c in (1, 2):
                        for pr in range(4):
                            ins = V.scalar_tensor_tensor(SS[:, pr, c, :], SS[:, pr, c - 1, :], decs[:, pr, c:c + 1],
                                                         MB[:, pr, c * P:(c + 1) * P], ALU.mult, ALU.add)
                        if c == 1:
                            step(ins)
                    ins.then_inc(gs_ok, 1)
                if k == 4:
                    v.wait_ge(at_zero, 1)
                    v.wait_ge(at_ps, 1)
                    mask = lt[:, :].bitcast(U32).rearrange("p (h t) -> p h t", h=1).broadcast_to([P, 4, P])
                    for m in range(NT):
                        for hf in range(2):
                            last = V.copy_predicated(AT[m][:, hf, :].rearrange("p (h t) -> p h t", h=4), mask,
                                                     MB[:, 2 * m + hf, :].rearrange("p (h t) -> p h t", h=4))
                    last.then_inc(at_ok, 1)
                if k == 5:
                    v.wait_ge(go_sq, 1)
                    for m in range(NT):
                        last = V.tensor_reduce(pwi[:, 8 * m:8 * m + 8], AT[m][:, :, :].rearrange(
                            "p f (h t) -> p (f h) t", h=4), AX.X, ALU.add)
                    step(last)
                    V.tensor_scalar(pwi[:, :], pwi[:, :], 1.0 / P, EPS, ALU.mult, ALU.add).then_inc(pw_req, 1)

            def gla_out():
                ask("gla")
                for m in range(NT):
                    for hf in range(2):
                        k = 8 * m + 4 * hf
                        r = pwo[:, k:k + 4].rearrange("p (h t) -> p h t", t=1).broadcast_to([P, 4, P])
                        step(V.tensor_tensor(oT[:, :].rearrange("p (h t) -> p h t", h=4),
                                             MB[:, 2 * m + hf, :].rearrange("p (h t) -> p h t", h=4), r, ALU.mult))
                        x = gg[:, m, 512 * hf:512 * hf + 512]
                        last = V.tensor_tensor(x, x, oT[:, :], ALU.mult)
                        if k < 12:
                            step(last)
                last.then_inc(go_ok, 1)

            def evac(s):
                v.wait_ge(unit_done, 4 * s + 4)
                cur[0] = s
                par = s % 2
                src = PG[:, par, 1, :]
                if s in (ZC0, ZC1, ZC2):
                    w = shape_of(s)[1]
                    V.tensor_copy(zc[:, 1, 512 * s:512 * s + w], src[:, 0:w]).then_inc(evac_v, 1)
                elif s in (UQN, UQN + 1, UKK, UKK + 1):
                    t, c = (QnT, 4 * (s - UQN)) if s < UKK else (KnT, 4 * (s - UKK))
                    V.tensor_copy(flat(t[:, c + 2:c + 4, :]), src).then_inc(evac_v, 1)
                elif s == UQR:
                    rope(lambda m: PG[:, par, m, :].rearrange("p (h x e) -> p h x e", x=2, e=32),
                         lambda m: qr[:, m, :].rearrange("p (h x e) -> p h x e", x=2, e=32), cosT, sinT, 32,
                         qr_ok, evac_v)
                elif s in (GG, GG + 1):
                    v.wait_ge(evac_a, s + 1)
                    c = 512 * (s - GG)
                    V.scalar_tensor_tensor(gg[:, :, c:c + 512], rt[:, :, :], 1.0, PG[:, par, :, :],
                                           ALU.add, ALU.mult).then_inc(evac_v, 1)
                    v.wait_ge(evac_v, s + 1)
                    for m in range(NT):
                        x = gg[:, m, c:c + 512].rearrange("p (h t) -> p h t", h=4)
                        gn = gnw[:, :].rearrange("p (h t) -> p h t", h=1).broadcast_to([P, 4, P])
                        last = V.scalar_tensor_tensor(x, x, 0.5, gn, ALU.mult, ALU.mult)
                    step(last)
                elif s in COPY0:
                    t, c = COPY0[s]
                    V.tensor_copy(t[:, 1, c:c + 512], src).then_inc(evac_v, 1)
                elif s == SVC:
                    V.tensor_copy(KB[:, 1, 1, :], src).then_inc(evac_v, 1)
                    v.wait_ge(evac_v, s + 1)
                    v.sem_inc(ke_ok, 1)
                elif s in (SKC, SKS, SKW) or SQ <= s < SQ + 4:
                    if s >= SQ:
                        g = s - SQ
                        if g >= 2:
                            v.wait_ge(qt_ps, g - 1)
                        dst, done = (lambda m: zq[:, g % 2, m, :]), qe_ok
                    else:
                        k = {SKC: 0, SKS: 2, SKW: 3}[s]
                        if k >= 2:
                            v.wait_ge(kt_ps, k - 1)
                        dst, done = (lambda m: KB[:, k % 2, m, :]), ke_ok
                    rope(lambda m: PG[:, par, m, :].rearrange("p (h x e) -> p h x e", x=2, e=64),
                         lambda m: dst(m).rearrange("p (h x e) -> p h x e", x=2, e=64), cosT, sinT, 64, done, evac_v)
                elif s == SW1:
                    V.tensor_copy(GX[:, :, :], PG[:, par, :, 0:60]).then_inc(evac_v, 1)
                    v.wait_ge(evac_v, s + 1)
                    step(V.tensor_tensor(GU[:, :, :], GX[:, :, :], GX[:, :, :], ALU.mult))
                    step(V.tensor_scalar(GU[:, :, :], GU[:, :, :], 0.044715, 1.0, ALU.mult, ALU.add))
                    V.tensor_tensor(GU[:, :, :], GU[:, :, :], GX[:, :, :], ALU.mult).then_inc(ge_x, 1)
                    v.wait_ge(ge_e, 1)
                    step(V.tensor_scalar(GU[:, :, :], GU[:, :, :], 1.0, 0.5, ALU.add, ALU.mult))
                    x = [t[:, :, :].rearrange("p k (g n) -> p k g n", g=4) for t in (GX, GU)]
                    V.tensor_tensor(GE[:, :, :, 0:NCMP], x[0], x[1], ALU.mult).then_inc(gl_ok, 1)
                elif s == SGT:
                    b = gbias[:, :].rearrange("p (m n) -> p m n", m=1).broadcast_to([P, NT, W_GT])
                    V.tensor_tensor(gates[:, :, :], PG[:, par, :, 0:W_GT], b, ALU.add).then_inc(evac_v, 1)
                    v.wait_ge(gx_e, 1)
                    step(V.tensor_scalar(gates[:, :, :], gates[:, :, :], 1.0, 0.5, ALU.add, ALU.mult))

            def lowrank_norm():
                v.wait_ge(evac_a, ZC2 + 1)
                for k in range(2):
                    for m in range(NT):
                        x = zc[:, m, 16 + 512 * k:528 + 512 * k]
                        step(V.tensor_tensor_reduce(out=rt[:, 0, :], in0=x, in1=x, scale=1.0, scalar=0.0,
                                                    op0=ALU.mult, op1=ALU.add,
                                                    accum_out=pwi[:, 2 * k + m:2 * k + m + 1]))
                V.tensor_scalar(pwi[:, 0:4], pwi[:, 0:4], 1.0 / 512, EPS, ALU.mult, ALU.add).then_inc(pw_req, 1)
                ask("cqkv")
                for k in range(2):
                    for m in range(NT):
                        x = zc[:, m, 16 + 512 * k:528 + 512 * k]
                        last = V.tensor_scalar(x, x, pwo[:, 2 * k + m:2 * k + m + 1], None, ALU.mult)
                last.then_inc(zn_ok, 1)
                for m in range(NT):
                    x = zc[:, m, 1040:1104].rearrange("p (x e) -> p x e", x=2)
                    a, b = (rt[:, k, 0:64].rearrange("p (x e) -> p x e", x=2) for k in range(2))
                    cs, sn = (t[:, m, ::2].rearrange("p (x e) -> p x e", x=1).broadcast_to([P, 2, 32])
                              for t in (cosT, sinT))
                    V.tensor_tensor(a, x, cs, ALU.mult)
                    step(V.tensor_tensor(b, x, sn, ALU.mult))
                    for d in range(2):
                        V.tensor_tensor(krd[:, m, d, 0:32], a[:, 0, :], b[:, 1, :], ALU.subtract)
                        last = V.tensor_tensor(krd[:, m, d, 32:64], a[:, 1, :], b[:, 0, :], ALU.add)
                    if m == 0:
                        step(last)
                last.then_inc(kr_ok, 1)
                v.wait_ge(kr_ok, 1)

            def compressed(g):
                v.wait_ge(cs_ps, g + 1)
                for m in range(NT):
                    nm = negm[:, m, :].rearrange("p (j n) -> p j n", j=1).broadcast_to([P, 4, 16])
                    last = V.scalar_tensor_tensor(
                        csc[:, m, :, :], PG[:, (SQ + g) % 2, 0, 64 * m:64 * m + 64].rearrange("p (j n) -> p j n", j=4),
                        NSA_SCALE, nm, ALU.mult, ALU.add)
                step(last)
                c8 = csc[:, :, :, :].rearrange("p m j n -> p (m j) n")
                col = lambda k: cst[:, k, :].rearrange("p (a n) -> p a n", n=1).broadcast_to([P, 8, 16])
                step(V.tensor_reduce(cst[:, 0, :], c8, AX.X, ALU.max))
                V.tensor_tensor(c8, c8, col(0), ALU.subtract).then_inc(cs_in, 1)
                v.wait_ge(cs_e, g + 1)
                step(V.tensor_reduce(cst[:, 1, :], c8, AX.X, ALU.add))
                step(V.reciprocal(cst[:, 2, :], cst[:, 1, :]))
                f = cst[:, 2, :].rearrange("p (m j) -> p m j", m=2)
                step(V.tensor_tensor(f, f, gates[:, :, 12 * g:12 * g + 12:3], ALU.mult))
                step(V.tensor_tensor(c8, c8, col(2), ALU.mult))
                if g:
                    v.wait_ge(cp_ps, g)
                ok = okm[:, :, :].rearrange("p m (j n) -> p m j n", j=1).broadcast_to([P, NT, 4, 16])
                V.tensor_tensor(Pc[:, :, :, 0:16], csc[:, :, :, :], ok, ALU.mult).then_inc(cs_ok, 1)

            def stage(s, j):
                k = before(s, j)
                if j == 0 and s not in (0, L1, OUT1):
                    evac(s - 1)
                if (s, j) == (QG, 0):
                    lowrank_norm()
                if k == (QG, 1):
                    split_in(XB, 4, TQ["cqkv"], 0, 64)
                if k in MLA_AT:
                    att_stage(MLA_AT[k], False)
                if k in GLA_AT:
                    gla_stage(GLA_AT[k])
                if (s, j) == (OUT0, 0):
                    gla_out()
                if k == (OUT0, 0):
                    split_in(XB, 4, TQ["gla"], 8)
                if (s, j) in ((SKC + 1, 3), (SVC + 1, 3)):
                    n = s - SKC - 1
                    v.wait_ge(kt_sb, n + 1)
                    if n:
                        v.wait_ge(bh_ok, 1)
                    src = (kcT, vcT)[n][:, :, :].rearrange("p g (n l) -> p l g n", l=16)
                    for a in range(2):
                        c = 32 * n + 16 * a
                        pos = posT[:, c:c + 16].rearrange("p (l g n) -> p l g n", g=1, n=1).broadcast_to([P, 16, 4, 15])
                        last = V.tensor_tensor(BT[:, 16 * a:16 * a + 16, :].rearrange("p l (g n) -> p l g n", g=4),
                                               src[:, :, :, a:a + 15], pos, ALU.add)
                    last.then_inc(bt_ok, 1)
                    v.wait_ge(bh_ok, n + 1)
                    v.wait_ge(bt_ok, n + 1)
                    V.tensor_tensor(BLl[:, n, :, :], BT[:, :, :], BLh[:, n, :, :].bitcast(F32),
                                    ALU.subtract).then_inc(bl_ok, 1)
                if k == (SW1 + 1, 2):
                    v.wait_ge(vb_zero, 1)
                    v.wait_ge(c2_ps, 1)
                    for jj in range(4):
                        r = slice(32 * jj, 32 * jj + 32)
                        last = V.tensor_copy(VB[r, :, jj, :], MB[r, 1, :].rearrange("p (g t) -> p g t", g=4))
                    last.then_inc(c2_v, 1)
                for op, g in NSA_AT.get(k, ()):
                    if op == "qt" and g == 3:
                        evac(SQ + 3)
                    if op == "cs":
                        compressed(g)
                    if op == "st":
                        att_stage(g, True)

            v.wait_ge(const_mk, 1)
            v.wait_ge(const_in, 16 * N_CONST)
            step(V.tensor_copy(posf[:, :], posi[:, :]))
            for m in range(NT):
                last = V.tensor_scalar(ang[:, m, :], invb[:, :], posf[:, m:m + 1], None, ALU.mult)
            step(last)
            step(V.tensor_scalar(kk[:, :, :], ang[:, :, :], 1.0 / TWO_PI, MAGIC, ALU.mult, ALU.add))
            step(V.tensor_scalar(kk[:, :, :], kk[:, :, :], MAGIC, None, ALU.subtract))
            for c in (C1, C2, C3):
                step(V.scalar_tensor_tensor(flat(ang[:, :, :]), flat(kk[:, :, :]), -c, flat(ang[:, :, :]),
                                            ALU.mult, ALU.add))
            step(V.tensor_scalar(ang[:, :, :], ang[:, :, :], PI_IN, -PI_IN, ALU.min, ALU.max))
            step(V.scalar_tensor_tensor(flat(kk[:, :, :]), flat(ang[:, :, :]), -1.0, flat(ang[:, :, :]),
                                        ALU.mult, ALU.min))
            V.tensor_scalar(kk[:, :, :], kk[:, :, :], TWO_PI / 4, None, ALU.add).then_inc(ang_ok, 1)
            v.wait_ge(x_in, 32)
            norm_out(0)
            v.wait_ge(vt_sb, 2)
            split_in(XA, 8, TQ["mix0"], 0, 0)
            v.wait_ge(trig_ok, 1)

            for s in range(0, OUT0 + 1):
                for j in range(4):
                    split(s, j, shape_of(s)[0] * shape_of(s)[1])
                    stage(s, j)

            for layer in range(2):
                s0 = OUTS[layer]

                def mixer_panel(i):
                    s = i + s0
                    v.wait_ge(unit_done, s * 4 + 4)
                    v.wait_ge(wbc_in, 16 * (3 * layer + 1))
                    c = bass.ds(i * 512, 512)
                    V.tensor_tensor(Fm[:, 1, c], PG[:, s % 2, 1, :], wbc[:, c], ALU.mult).then_inc(mul_done, 1)
                    v.wait_ge(sq_done, i + (12 * layer + 1))
                    V.tensor_tensor(Fm[:, 0, c], PG[:, s % 2, 0, :], wbc[:, c], ALU.mult).then_inc(evac_v, 1)

                with v.Fori(0, 3) as i:
                    for j in range(4):
                        split(i + (s0 + 1), j)
                        if j == 0:
                            mixer_panel(i)
                for g, n in enumerate(GROUPS):
                    b = ffn_base(layer, g)
                    q0 = TQ[f"hid{layer}"] + 2 * sum(GROUPS[:g])

                    def silu(s):
                        v.wait_ge(evac_a, s + 1)
                        V.scalar_tensor_tensor(Eb[:, :, :], Eb[:, :, :], 1.0, PG[:, b % 2, :, :],
                                               ALU.add, ALU.mult).then_inc(evac_v, 1)

                    def hidden(s):
                        v.wait_ge(unit_done, s * 4 + 4)
                        v.wait_ge(evac_v, s)
                        V.scalar_tensor_tensor(Hb[:, :, :], Eb[:, :, :], 0.5, PG[:, (b + 1) % 2, :, :],
                                               ALU.mult, ALU.mult).then_inc(evac_v, 1)

                    def down_panel(i, g, d):
                        s = i + d
                        v.wait_ge(unit_done, s * 4 + 4)
                        c = bass.ds(i * 512, 512)
                        if g == 0:
                            V.tensor_copy(Fm[:, 1, c], PG[:, s % 2, 1, :]).then_inc(evac_v, 1)
                            return
                        first = V.tensor_tensor(Fm[:, 0, c], PG[:, s % 2, 0, :], Fm[:, 0, c], ALU.add)
                        if g == 2:
                            first.then_inc(add_done, 1)
                        V.tensor_tensor(Fm[:, 1, c], PG[:, s % 2, 1, :], Fm[:, 1, c], ALU.add).then_inc(evac_v, 1)
                        if g == 2:
                            v.wait_ge(wbc_in, 16 * (3 * layer + 2))
                            for m in range(NT):
                                v.wait_ge(sq_done, i * 2 + (12 * layer + 5 + m))
                                last = V.tensor_tensor(Fm[:, m, c], Fm[:, m, c], wbc[:, c], ALU.mult)
                            step(last)

                    split(b, 0)
                    if g == 0:
                        mixer_panel(3)
                        v.wait_ge(evac_a, s0 + 4)
                        v.wait_ge(evac_v, s0 + 4)
                        post_norm(f"post{layer}")
                        norm_out((1, 3)[layer])
                        split_in(XA, 8, TQ[f"ffn{layer}"], 0, 16 + 32 * layer)
                        split_in(PX, 1, TQ[f"p{layer}"], 0)
                    else:
                        down_panel(3, g - 1, d0)
                    for j in range(1, 4):
                        split(b, j)
                    split(b + 1, 0)
                    silu(b)
                    for j in range(1, 4):
                        split(b + 1, j)
                    with v.Fori(0, n - 1) as i:
                        s = i * 2 + (b + 2)
                        split(s, 0)
                        hidden(i * 2 + (b + 1))
                        split(s, 1)
                        split_in(XB, 2, i * 2 + q0, i * 4)
                        split(s, 2)
                        split(s, 3)
                        split(s + 1, 0)
                        silu(s)
                        for j in range(1, 4):
                            split(s + 1, j)
                    d0 = b + 2 * n
                    w = n * 512
                    split(d0, 0, w)
                    hidden(d0 - 1)
                    split(d0, 1, w)
                    split_in(XB, 2, q0 + 2 * (n - 1), 4 * (n - 1))
                    split(d0, 2, w)
                    split(d0, 3, w)
                    with v.Fori(0, 3) as i:
                        step.enter(i, 1 if g == 2 else 0)
                        split(i + (d0 + 1), 0, w)
                        down_panel(i, g, d0)
                        for j in range(1, 4):
                            split(i + (d0 + 1), j, w)
                        step.leave(3)
                pr, gt0 = PROJ[layer], GATE[layer]

                def proj_panel(i):
                    s = i + pr
                    v.wait_ge(unit_done, s * 4 + 4)
                    V.tensor_copy(PJ[:, 1, bass.ds(i * 512, 512)], PG[:, s % 2, 1, :]).then_inc(evac_v, 1)

                def gate_panel(i):
                    s = i + gt0
                    v.wait_ge(unit_done, s * 4 + 4)
                    v.wait_ge(wbc_in, 16 * (3 * layer + 3))
                    c = bass.ds(i * 512, 512)
                    V.tensor_tensor(Eb[:, 0, :], PG[:, s % 2, 0, :], wbc[:, c], ALU.add)
                    V.tensor_tensor(Eb[:, 1, :], PG[:, s % 2, 1, :], wbc[:, c], ALU.add).then_inc(evac_v, 1)
                    v.wait_ge(evac_a, s + 1)
                    step(V.scalar_tensor_tensor(Eb[:, :, :], Eb[:, :, :], 1.0, PJ[:, :, c], ALU.add, ALU.mult))
                    V.scalar_tensor_tensor(h[:, :, c], Eb[:, :, :], 0.5, h[:, :, c],
                                           ALU.mult, ALU.add).then_inc(h_ok, 1)

                split(pr, 0, 256)
                down_panel(3, 2, d0)
                v.wait_ge(evac_v, d0 + 4)
                post_norm(f"fpost{layer}")
                for j in range(1, 4):
                    split(pr, j, 256)
                with v.Fori(0, 3) as i:
                    split(i + (pr + 1), 0, 256)
                    proj_panel(i)
                    for j in range(1, 4):
                        split(i + (pr + 1), j, 256)
                split(gt0, 0)
                proj_panel(3)
                split_in(XA, 8, TQ[f"ple{layer}"], 0)
                for j in range(1, 4):
                    split(gt0, j)
                with v.Fori(0, 3) as i:
                    step.enter(i, 1)
                    split(i + (gt0 + 1), 0)
                    gate_panel(i)
                    for j in range(1, 4):
                        split(i + (gt0 + 1), j)
                    step.leave(3)
                if layer == 1:
                    gate_panel(3)
                    break
                for s in range(L1, OUT1 + 1):
                    for j in range(4):
                        split(s, j, shape_of(s)[0] * shape_of(s)[1])
                        if (s, j) == (L1, 0):
                            gate_panel(3)
                            norm_out(2)
                            split_in(XA, 8, TQ["mix1"], 0, 32)
                        stage(s, j)


def kernel(**inputs):
    import concourse.bacc as bacc
    from concourse.bass_utils import run_bass_kernel_spmd

    nc = bacc.Bacc("TRN2", target_bir_lowering=False, num_devices=1, dynamic_dma_scratch_size=1024)
    arrays, tensors = {}, {}
    for name, value in inputs.items():
        a = np.ascontiguousarray(value)
        if name == "nsa_cmp_w1":
            a = np.ascontiguousarray(a.reshape(2, CMP_LEN, P, P).transpose(0, 2, 1, 3))
        arrays[f"in_{name}"] = a
        tensors[name] = nc.dram_tensor(f"in_{name}", a.shape, mybir.dt.from_np(a.dtype), kind="ExternalInput").ap()
    inv = np.power(10000.0, -np.arange(0, 128, 2) / 128.0).astype(np.float32)[None, :]
    arrays["in_rope_inv"] = inv
    tensors["rope_inv"] = nc.dram_tensor("in_rope_inv", inv.shape, F32, kind="ExternalInput").ap()
    tensors["out"] = nc.dram_tensor("out", (1, SEQ, D), F32, kind="ExternalOutput").ap()
    build(nc, tensors)
    r = run_bass_kernel_spmd(nc, [arrays], core_ids=[0])
    return r.results[0]["out"]
```

```python
from contextlib import ExitStack

import numpy as np

import concourse.bass as bass
from concourse import mybir
from concourse.alu_op_type import AluOpType as ALU

F32 = mybir.dt.float32
F32R = mybir.dt.float32r
U32 = mybir.dt.uint32
I32 = mybir.dt.int32
ACT = mybir.ActivationFunctionType
AX = mybir.AxisListType

P = 128
D = 2048
SEQ = 256
NT = SEQ // P
KC = D // P
FFN = 5632
PLE = 256
EPS = 1e-6
NEG = -1e30
TAU = 16.0
CMP_LEN, CMP_STRIDE, NCMP = 32, 16, 15
MLA_SCALE = float((128 + 64) ** -0.5)
NSA_SCALE = float(128 ** -0.5)
GELU_C = float(2.0 * np.sqrt(2.0 / np.pi))
TWO_PI = 6.283185307179586
C1 = 6.28125
C2 = 0.00193500518798828125
C3 = TWO_PI - C1 - C2
MAGIC = 12582912.0
PI_IN = 3.1415925

ZC0, ZC1, ZC2, QG, UQN, UQR, UKK, UKV, KG, VG, GG, OUT0 = 0, 1, 2, 3, 4, 6, 7, 9, 11, 12, 14, 16
FFN0 = OUT0 + 8
GROUPS = (4, 4, 3)
FFN_SLOTS = sum(2 * n + 4 for n in GROUPS)
L1 = FFN0 + FFN_SLOTS + 4
SKC, SVC, SKS, SW1, SKW, SVS, SVW, SGT, SQ, OUT1 = (L1 + i for i in (0, 1, 2, 3, 4, 5, 6, 7, 8, 12))
FFN1 = OUT1 + 8
OUTS, FFNS = (OUT0, OUT1), (FFN0, FFN1)
PROJ = tuple(s + 4 for s in OUTS)
GATE = tuple(f + FFN_SLOTS for f in FFNS)
NSLOTS = GATE[1] + 4
W_GT = 48

TQ = {}
_n = 0
for _name, _k in (("mix0", 8), ("cqkv", 4), ("gla", 4), ("p0", 1), ("ffn0", 8), ("hid0", 22), ("ple0", 8),
                  ("mix1", 8), ("p1", 1), ("ffn1", 8), ("hid1", 22), ("ple1", 8)):
    TQ[_name] = _n
    _n += _k
TQ_END = _n
POW = ["mix0", "cqkv", "gla", "post0", "ffn0", "fpost0", "mix1", "post1", "ffn1", "fpost1"]
POW_W = {"mix0": 2, "cqkv": 4, "gla": 16}


def ffn_base(layer, g):
    return FFNS[layer] + sum(2 * n + 4 for n in GROUPS[:g])


MLA_STEPS = 4
NSA_STEPS = 16
MLA_AT = {(UKV + 2, 1): 0, (UKV + 2, 3): 1, (UKV + 3, 1): 2, (UKV + 3, 3): 3, (UKV + 4, 1): 4, (UKV + 4, 3): 5}


def nsa_plan():
    plan, t = {}, 0
    for g in range(3):
        for j in range(4):
            ops = [("qt", g)] if j == 1 else [("cs", g)] if j == 2 else []
            if (g, j) >= (0, 3):
                ops.append(("st", t))
                t += 1
            plan[(SQ + 1 + g, j)] = ops
    plan[(SQ + 3, 3)] += [("st", t)]
    plan[(OUT1, 0)] = [("qt", 3), ("st", t + 1)]
    plan[(OUT1, 1)] = [("cs", 3), ("st", t + 2)]
    for k, gap in enumerate(((OUT1, 2), (OUT1, 3), (OUT1, 3), (OUT1 + 1, 0), (OUT1 + 1, 1), (OUT1 + 1, 1))):
        plan.setdefault(gap, []).append(("st", t + 3 + k))
    assert t + 3 + k == NSA_STEPS + 1
    return plan


NSA_AT = nsa_plan()
PP_AT = {(OUT0, 2): 0, (OUT1 + 1, 2): 1}
OUT_UNITS = ((0, 0), (0, 1), (1, 0), (1, 1), (0, 2), (1, 2), (0, 3), (1, 3))
CP_STEP = {0: 0, 4: 1, 8: 2, 12: 3}

GLA_AT = {(GG, 1): 0, (GG, 2): 1, (GG, 3): 2, (GG + 1, 0): 3, (GG + 1, 1): 4, (GG + 1, 2): 5}
KT_AT = {(SKC + 1, 1): 0, (SVC + 1, 1): 1, (SKS + 1, 1): 2, (SKW + 1, 1): 3}


def staged():
    plan = {}
    for x in range(4 * QG, 4 * (OUT1 + 2)):
        s, j = x // 4, x % 4
        prompt = s in (QG, GG, GG + 1, OUT0) or s >= SQ + 1
        at = x + 1 if prompt else x + 2
        last = 4 * OUT0 + 3 if s <= OUT0 else 4 * OUT1 + 7
        plan.setdefault((at // 4, at % 4) if at <= last else (last // 4, 4), []).append((s, j))
    return plan


STAGED = staged()


def evac_stage(s):
    return None if s in (0, L1, OUT1 + 1) else 0 if s <= KG else 1


class Ring:

    def __init__(self):
        self.less = 0

    def __call__(self, s):
        return s * 4 - self.less if self.less else s * 4

    def projected(self):
        self.less += 12


class Steps:

    def __init__(self, eng, sem):
        self.eng, self.sem, self.n, self.i, self.per, self.base = eng, sem, 0, None, 0, 0

    def __call__(self, ins):
        ins.then_inc(self.sem, 1)
        self.n += 1
        self.eng.wait_ge(self.sem, self.n if self.i is None else self.n + self.i * self.per)

    def enter(self, i, per):
        self.i, self.per, self.base = i, per, self.n

    def leave(self, times):
        assert self.n - self.base == self.per, (self.n - self.base, self.per)
        self.n = self.base + self.per * times
        self.i = None


def build(nc, T):
    def rows(a):
        return a.rearrange("(c p) n -> p c n", p=P)

    ab_in, ab_out = rows(T["ab_w_in"][0]), rows(T["ab_w_out"][0])
    uq = T["mla_w_uq"][0].rearrange("(c p) (h e) -> p c h e", p=P, e=192)
    ukv = T["mla_w_ukv"][0].rearrange("(c p) (h e) -> p c h e", p=P, e=256)
    nsa_in, nsa_out = rows(T["nsa_w_in"][0]), rows(T["nsa_w_out"][0])
    wg, wu, wd, plg, plp = ([rows(T[n][i]) for i in range(2)] for n in (
        "ffn_w_gate", "ffn_w_up", "ffn_w_down", "ple_w_gate", "ple_w_proj"))
    w1_d = T["nsa_cmp_w1"]
    tok = lambda a: a.rearrange("(m p) d -> p m d", p=P)
    x_d, out_d = tok(T["x"][0]), tok(T["out"][0])
    p_d = [tok(T["p"][i, 0]) for i in range(2)]

    ctx = ExitStack()
    with ctx:
        at = [(nc.sbuf_base + 63) // 64 * 64]

        def sb(name, shape, dt=F32):
            n = int(np.prod(shape[1:])) * 4
            t = nc.alloc_sbuf_tensor_at(name, shape, dt, offset=at[0])
            at[0] += (n + 31) // 32 * 32
            return t

        def sem(name):
            return ctx.enter_context(nc.semaphore(name))

        h = sb("h", [P, NT, D])
        XAh, XAl = sb("XAh", [P, KC, SEQ], F32R), sb("XAl", [P, KC, SEQ], F32R)
        xb0 = at[0]
        XBh, XBl = sb("XBh", [P, KC, SEQ], F32R), sb("XBl", [P, KC, SEQ], F32R)
        BL = nc.alloc_sbuf_tensor_at("BL", [P, 2, CMP_LEN, 2, 60], F32R, offset=xb0)
        raw = sb("raw", [P, 4, 2048])
        wh, wl = sb("wh", [P, 2, 2048], F32R), sb("wl", [P, 2, 2048], F32R)
        ident = sb("ident", [P, P])
        cmask = sb("cmask", [P, 3, P])
        lt = sb("lt", [P, P])
        gt = sb("gt", [P, P])
        endm = sb("endm", [P, P])
        cosT, sinT = sb("cosT", [P, NT, 64]), sb("sinT", [P, NT, 64])
        vcol = sb("vcol", [P, 72])
        posT = sb("posT", [P, 64])
        okm, negm = sb("okm", [P, NT, 16]), sb("negm", [P, NT, 16])
        ss = sb("ss", [P, NT, 4])
        pwi, pwo, mhalf = sb("pwi", [P, 16]), sb("pwo", [P, 16]), sb("mhalf", [P, 16])
        sm = sb("sm", [P, 12])
        rt = sb("rt", [P, 2, 512])
        gnw = sb("gnw", [P, P])
        AL, aw = sb("AL", [17, SEQ]), sb("aw", [17, 512])
        krd = sb("krd", [P, NT, 2, 64])
        KrT = sb("KrT", [P, SEQ])
        decs = sb("decs", [P, 4, 4])
        w2s = sb("w2s", [P, 2, P])
        GE = sb("GE", [P, 2, 4, 32])
        KcT = sb("KcT", [P, 4, 32])
        gbias, gates = sb("gbias", [P, W_GT]), sb("gates", [P, NT, W_GT])
        csc, Pc = sb("csc", [P, NT, 4, 16]), sb("Pc", [P, NT, 4, 32])
        cst = sb("cst", [P, 3, 8])
        PcT = sb("PcT", [P, 2, SEQ])

        ZS = 58112
        z0 = at[0]
        assert z0 + ZS <= nc.sbuf_usable_end, (z0 + ZS, nc.sbuf_usable_end)

        def zt(name, off, shape, dt=F32):
            assert off + int(np.prod(shape[1:])) * 4 <= ZS, name
            return nc.alloc_sbuf_tensor_at(name, shape, dt, offset=z0 + off)

        vin, vin2 = zt("vin", 16384, [72, P]), zt("vin2", 16896, [64, P])
        invb, posi, posf = zt("invb", 17408, [P, 64]), zt("posi", 17664, [P, NT], I32), zt("posf", 17696, [P, NT])
        ang, kk = zt("ang", 17728, [P, NT, 64]), zt("kk", 18240, [P, NT, 64])
        qg, kg = zt("qg", 0, [P, NT, 512]), zt("kg", 4096, [P, NT, 512])
        vg, gg = zt("vg", 8192, [P, NT, 1024]), zt("gg", 16384, [P, NT, 1024])
        SP0, PT0 = zt("SP0", 16384, [P, 2, 384]), zt("PT0", 19456, [P, 2, 384])
        QnT, KnT = zt("QnT", 24576, [P, 8, SEQ]), zt("KnT", 32768, [P, 8, SEQ])
        Vm, zc = zt("Vm", 40960, [P, NT, 1024]), zt("zc", 40960, [P, NT, 1104])
        qr, QrT = zt("qr", 49792, [P, NT, 512]), zt("QrT", 53888, [P, 4, SEQ])
        loga, kinv, E1 = zt("loga", 24576, [P, NT, 512]), zt("kinv", 28672, [P, NT, 512]), zt("E1", 32768, [P, NT, 512])
        qdT, kiT = zt("qdT", 36864, [P, 4, SEQ]), zt("kiT", 40960, [P, 4, SEQ])
        SS, oT = zt("SS", 45056, [P, 4, 3, P]), zt("oT", 51200, [P, 512])
        AT = [zt("ATa", 24576, [P, 2, 512]), zt("ATb", 32768, [P, 2, 512])]
        zq, KB = zt("zq", 0, [P, 2, NT, 512]), zt("KB", 8192, [P, 2, NT, 512])
        SP1, PT1 = zt("SP1", 8192, [P, 2, 384]), zt("PT1", 11264, [P, 2, 384])
        vs, vw = zt("vs", 16384, [P, NT, 512]), zt("vw", 20480, [P, NT, 512])
        kcT, vcT = zt("kcT", 24576, [P, 4, SEQ]), zt("vcT", 28672, [P, 4, SEQ])
        ksT, kwT = zt("ksT", 32768, [P, 4, SEQ]), zt("kwT", 36864, [P, 4, SEQ])
        BT = zt("BT", 40960, [P, CMP_LEN, 60])
        VB = zt("VB", 24576, [P, 4, 4, P])
        QT = zt("QT", 48640, [P, 2, 4, SEQ])
        GX, GU = zt("GX", 48640, [P, 2, 60]), zt("GU", 49152, [P, 2, 60])
        Fm, PJ = zt("Fm", 0, [P, NT, D]), zt("PJ", 16384, [P, NT, D])
        Eb, Hb = zt("Eb", 32768, [P, NT, 512]), zt("Hb", 36864, [P, NT, 512])
        wbc, pp = zt("wbc", 40960, [P, D]), zt("pp", 49152, [P, NT, PLE])
        PXh, PXl = zt("PXh", 51200, [P, 2, SEQ], F32R), zt("PXl", 53248, [P, 2, SEQ], F32R)
        XA, XB, PX = (XAh, XAl), (XBh, XBl), (PXh, PXl)

        PG = ctx.enter_context(nc.psum_tensor("PG", [P, 2, NT, 512], F32))
        MB = ctx.enter_context(nc.psum_tensor("MB", [P, 4, 512], F32))

        raw_in = [sem(f"raw_in{j}") for j in range(4)]
        x_in, start_in, const_in = sem("x_in"), sem("start_in"), sem("const_in")
        pp_in, wbc_in, out_st = sem("pp_in"), sem("wbc_in"), sem("out_st")
        hi_ready, lo_ready = sem("hi_ready"), sem("lo_ready")
        unit_done = sem("unit_done")
        evac_a, evac_v = sem("evac_a"), sem("evac_v")
        tx_ps, tx_hi, tx_lo = sem("tx_ps"), sem("tx_hi"), sem("tx_lo")
        pw_req, pw_done = sem("pw_req"), sem("pw_done")
        const_mk = sem("const_mk")
        act_step, dve_step, pool_step, pe_step = (sem(n) for n in ("act_step", "dve_step", "pool_step", "pe_step"))
        vt_ps, vt_sb = sem("vt_ps"), sem("vt_sb")
        ang_ok, trig_ok = sem("ang_ok"), sem("trig_ok")
        sq_done = sem("sq_done")
        mul_done = sem("mul_done")
        add_done = sem("add_done")
        upd, ssq = sem("upd"), sem("ssq")
        hn_a, hn_v = sem("hn_a"), sem("hn_v")
        h_ok = sem("h_ok")
        zn_ok, kr_ok, qr_ok = sem("zn_ok"), sem("kr_ok"), sem("qr_ok")
        al_ps, al_sb = sem("al_ps"), sem("al_sb")
        qrt_ps, qrt_sb = sem("qrt_ps"), sem("qrt_sb")
        s_done, pt_done, pv_done = sem("s_done"), sem("pt_done"), sem("pv_done")
        mx_ok, exp_ok, o_hi = sem("mx_ok"), sem("exp_ok"), sem("o_hi")
        pt_sb, att_v = sem("pt_sb"), sem("att_v")
        ga_ps, ga_t, ga_n, ga_l, ga_ok = (sem(n) for n in ("ga_ps", "ga_t", "ga_n", "ga_l", "ga_ok"))
        gb_ps, ge_a, ge_v = sem("gb_ps"), sem("ge_a"), sem("ge_v")
        gt_ps, gt_sb, gu_ps, gd_sb, gs_ok = (sem(n) for n in ("gt_ps", "gt_sb", "gu_ps", "gd_sb", "gs_ok"))
        at_zero, at_ps, at_ok, go_ps, go_sq, go_ok = (sem(n) for n in (
            "at_zero", "at_ps", "at_ok", "go_ps", "go_sq", "go_ok"))
        ke_ok, kt_ps, kt_sb = sem("ke_ok"), sem("kt_ps"), sem("kt_sb")
        bt_ok, bh_ok, bl_ok = sem("bt_ok"), sem("bh_ok"), sem("bl_ok")
        ge_x, ge_e, gl_ok = sem("ge_x"), sem("ge_e"), sem("gl_ok")
        c2_ps, c2_a, c2_v, vb_zero = sem("c2_ps"), sem("c2_a"), sem("c2_v"), sem("vb_zero")
        gx_e = sem("gx_e")
        qe_ok, qt_ps, qt_sb = sem("qe_ok"), sem("qt_ps"), sem("qt_sb")
        cs_ps, cs_in, cs_e, cs_ok, cp_ps, pct_sb = (sem(n) for n in (
            "cs_ps", "cs_in", "cs_e", "cs_ok", "cp_ps", "pct_sb"))

        N_START, N_CONST = 10, 6
        COPY0 = {QG: (qg, 0), KG: (kg, 0), UKV: (Vm, 0), UKV + 1: (Vm, 512), VG: (vg, 0), VG + 1: (vg, 512),
                 SVS: (vs, 0), SVW: (vw, 0)}
        block = ctx.enter_context(nc.Block())

        def width(s):
            kc, ncol = shape_of(s)
            return kc * ncol

        def shape_of(s):
            if s == ZC2:
                return 4, 80
            if s == SGT:
                return 4, W_GT
            if UQN <= s < KG:
                return 1, 512
            return 4, 512

        @block.sync
        def _(sp):
            sp.dma_start(h[:, 0, :], x_d[:, 0, :]).then_inc(x_in, 16)
            sp.dma_start(h[:, 1, :], x_d[:, 1, :]).then_inc(x_in, 16)
            consts = [(vin[0:16, :], T["ln_mix_pre"][0].rearrange("(c k) -> c k", k=P)),
                      (vin[16:32, :], T["ln_ffn_pre"][0].rearrange("(c k) -> c k", k=P)),
                      (vin[32:48, :], T["ln_mix_pre"][1].rearrange("(c k) -> c k", k=P)),
                      (vin[48:64, :], T["ln_ffn_pre"][1].rearrange("(c k) -> c k", k=P)),
                      (vin[64:68, :], T["mla_q_norm_w"][0].rearrange("(c k) -> c k", k=P)),
                      (vin[68:72, :], T["mla_kv_norm_w"][0].rearrange("(c k) -> c k", k=P)),
                      (vin2[0:32, :], T["nsa_cmp_pos"][0, 0]),
                      (vin2[32:64, :], T["nsa_cmp_pos"][0, 1]),
                      (posi[:, :], T["positions"].rearrange("a (m p) -> p (a m)", p=P)),
                      (invb[:, :], T["rope_inv"][0:1, :].broadcast_to([P, 64]))]
            late = [(gnw[:, :], T["gla_norm_w"][0:1, :].broadcast_to([P, P])),
                    (aw[0:16, :], T["gla_w_alpha_up"][0]),
                    (aw[16:17, :], T["gla_b_alpha"][0:1, :]),
                    (w2s[:, 0, :], T["nsa_cmp_w2"][0, 0]),
                    (w2s[:, 1, :], T["nsa_cmp_w2"][0, 1]),
                    (gbias[:, :], T["nsa_b_gate"][0:1, :].broadcast_to([P, W_GT]))]
            assert (len(consts), len(late)) == (N_START, N_CONST)
            for dst, src in consts:
                sp.dma_start(dst, src, allow_slow_non_contiguous=True).then_inc(start_in, 16)

            U = Ring()

            def unit(s, j, src, kc, ncol):
                if not (isinstance(s, int) and s == 0):
                    sp.wait_ge(lo_ready, U(s) + (j - 3))
                dst = raw[:, j, 0:kc * ncol].rearrange("p (c n) -> p c n", c=kc)
                if len(src.shape) == 4:
                    dst = raw[:, j, 0:kc * ncol].rearrange("p (c h e) -> p c h e", c=kc, e=src.shape[3])
                sp.dma_start(dst, src).then_inc(raw_in[j], 16)

            def k_units(s, w, col, ncol=512, kc=4, c0=0, wrap=KC):
                for j in range(4):
                    c = (c0 + j * kc) % wrap
                    unit(s, j, w[:, c:c + kc, bass.ds(col, ncol)], kc, ncol)

            for n, s in enumerate((ZC0, ZC1, ZC2)):
                k_units(s, ab_in, 3072 + 512 * n, shape_of(s)[1])
                if n == 0:
                    for dst, src in late:
                        sp.dma_start(dst, src).then_inc(const_in, 16)
            k_units(QG, ab_in, 0)
            for n in range(7):
                for j in range(4):
                    if n < 2:
                        src = uq[:, j:j + 1, 4 * n:4 * n + 4, 0:128]
                    elif n == 2:
                        src = uq[:, j:j + 1, :, 128:192]
                    elif n < 5:
                        src = ukv[:, j:j + 1, 4 * (n - 3):4 * (n - 3) + 4, 0:128]
                    else:
                        src = ukv[:, j:j + 1, 4 * (n - 5):4 * (n - 5) + 4, 128:256]
                    unit(UQN + n, j, src, 1, 512)
            for n in range(5):
                k_units(KG + n, ab_in, 512 * (n + 1))
            for layer in range(2):
                if layer == 0:
                    for n in range(4):
                        k_units(OUTS[0] + n, ab_out, 512 * n, c0=8)
                else:
                    for n, (panel, part) in enumerate(OUT_UNITS):
                        unit(OUT1 + n // 4, n % 4,
                             nsa_out[:, 4 * part:4 * part + 4, 512 * panel:512 * panel + 512], 4, 512)
                    with sp.Fori(0, 2) as i:
                        k_units(i + (OUT1 + 2), nsa_out, i * 512 + 1024)
                for i in range(4):
                    unit(PROJ[layer], i, plp[layer][:, 0:2, 512 * i:512 * i + 512], 2, 512)
                U.projected()
                for g, n in enumerate(GROUPS):
                    b, p0 = ffn_base(layer, g), sum(GROUPS[:g])
                    with sp.Fori(0, n) as i:
                        k_units(i * 2 + b, wg[layer], i * 512 + 512 * p0)
                        k_units(i * 2 + (b + 1), wu[layer], i * 512 + 512 * p0)
                    with sp.Fori(0, 4) as i:
                        k_units(i + (b + 2 * n), wd[layer], i * 512, kc=n, c0=4 * p0, wrap=FFN)
                with sp.Fori(0, 4) as i:
                    k_units(i + GATE[layer], plg[layer], i * 512)
                if layer == 0:
                    kv = {SKC: 0, SVC: 1, SKS: 2, SVS: 3, SKW: 4, SVW: 5}
                    for s in range(L1, SQ):
                        if s == SW1:
                            for j in range(4):
                                unit(s, j, w1_d[j // 2, :, 16 * (j % 2):16 * (j % 2) + 16, :], 16, P)
                        elif s == SGT:
                            k_units(s, nsa_in, 5120, W_GT)
                        else:
                            k_units(s, nsa_in, 2048 + 512 * kv[s])
                    with sp.Fori(0, 4) as i:
                        k_units(i + SQ, nsa_in, i * 512)
            sp.wait_ge(h_ok, 8)
            sp.dma_start(out_d, h[:, :, :]).then_inc(out_st, 16)
            sp.wait_ge(out_st, 16)

        @block.gpsimd
        def _(pool):
            step = Steps(pool, pool_step)

            def select(t, pattern, base, cm, op=ALU.is_ge, fill=0.0):
                step(pool.affine_select(out=t, in_=t, compare_op=op, fill=fill, base=base,
                                        pattern=pattern, channel_multiplier=cm))

            step(pool.memset(ident[:, :], 0.0))
            select(ident[:, :], [[-1, P]], 0, 1, ALU.not_equal, 1.0)
            step(pool.memset(mhalf[:, :], -0.5))
            step(pool.memset(cmask[:, :, :], 0.0))
            select(cmask[:, 0, :], [[-1, P]], 0, 1, fill=NEG)
            select(cmask[:, 2, :], [[-1, P]], 0, 1, fill=NEG)
            step(pool.memset(endm[:, :], 1.0 / TAU))
            select(endm[:, 0:64], [[0, 64]], 63, -1)
            select(endm[:, 64:P], [[0, 64]], -64, 1)
            step(pool.tensor_copy(lt[:, :], endm[:, :]))
            step(pool.tensor_copy(gt[:, :], endm[:, :]))
            select(lt[:, :], [[1, P]], 0, -1)
            select(gt[:, :], [[-1, P]], -1, 1)
            step(pool.memset(okm[:, :, :], 1.0))
            step(pool.memset(negm[:, :, :], 0.0))
            select(okm[:, :, :], [[P, NT], [-CMP_STRIDE, 16]], 1 - CMP_LEN, 1)
            select(negm[:, :, :], [[P, NT], [-CMP_STRIDE, 16]], 1 - CMP_LEN, 1, fill=NEG)
            step(pool.memset(AL[:, :], 1.0))
            step(pool.memset(GE[:, :, :, :], 0.0))
            step(pool.memset(Pc[:, :, :, :], 0.0))
            pool.memset(sm[:, :], 0.0).then_inc(const_mk, 1)
            for k, name in enumerate(POW):
                w = POW_W.get(name, 2)
                pool.wait_ge(pw_req, k + 1)
                pool.tensor_tensor(pwo[:, 0:w], pwi[:, 0:w], mhalf[:, 0:w], ALU.pow).then_inc(pw_done, 1)
                if name == "cqkv":
                    pool.wait_ge(gu_ps, 1)
                    pool.wait_ge(ge_v, 1)
                    pool.memset(AT[0][:, :, :], 0.0)
                    pool.memset(AT[1][:, :, :], 0.0).then_inc(at_zero, 1)
                if name == "mix1":
                    pool.wait_ge(bt_ok, 2)
                    pool.memset(VB[:, :, :, :], 0.0).then_inc(vb_zero, 1)

        @block.tensor
        def _(pe):
            mm = nc.tensor.matmul
            pstep = Steps(pe, pe_step)
            U = Ring()

            def transpose_in(src, n, q, b0=0):
                for b in range(b0, b0 + n):
                    if not (isinstance(q, int) and q + b < 2):
                        pe.wait_ge(tx_lo, q + (b - 1))
                    k = b % 2
                    for c in range(2):
                        for m in range(NT):
                            o = c * SEQ + m * P
                            t = nc.tensor.transpose(MB[:, k, o:o + P], src(2 * b + c, m), ident[:, :])
                    t.then_inc(tx_ps, 1)

            def unit(s, j, X, kc=4, ncol=512, need=None, par=None, pos=None):
                pe.wait_ge(hi_ready, U(s) + (j + 1))
                pe.wait_ge(lo_ready, U(s) + (j + 1))
                if need is not None:
                    pe.wait_ge(tx_lo, need)
                par = s % 2 if par is None else par
                pos = j if pos is None else pos
                k = j % 2
                for c in range(kc):
                    chunk = max(pos, 0) * kc + c
                    hh, ll = (w[:, k, c * ncol:(c + 1) * ncol] for w in (wh, wl))
                    for m in range(NT):
                        o = PG[:, par, m, 0:ncol]
                        xh, xl = (x[:, chunk, m * P:(m + 1) * P] for x in X)
                        beg = c == 0 and pos in (0, -1)
                        end = c == kc - 1 and pos in (3, -1)
                        mm(o, xh, hh, start=beg, stop=False)
                        mm(o, xh, ll, start=False, stop=False)
                        last = mm(o, xl, hh, start=False, stop=end)
                last.then_inc(unit_done, 1)

            def unit_t(s, j, X, x0):
                pe.wait_ge(hi_ready, U(s) + j + 1)
                pe.wait_ge(lo_ready, U(s) + j + 1)
                for f in range(4):
                    o = PG[:, s % 2, f // 2, (f % 2) * SEQ:(f % 2 + 1) * SEQ]
                    hh, ll = (w[:, j % 2, f * P:(f + 1) * P] for w in (wh, wl))
                    xh, xl = (x[:, x0 + j, :] for x in X)
                    mm(o, hh, xh, start=(j == 0 and f % 2 == 0), stop=False, skip_group_check=True)
                    mm(o, hh, xl, start=False, stop=False, skip_group_check=True)
                    last = mm(o, ll, xh, start=False, stop=(j == 3), skip_group_check=True)
                last.then_inc(unit_done, 1)

            def banks_free(s):
                if isinstance(s, int) and s < 2:
                    return
                pe.wait_ge(evac_a, s - 1)
                pe.wait_ge(evac_v, s - 1)

            def att_step(t, nsa):
                n = NSA_STEPS if nsa else MLA_STEPS
                a0 = MLA_STEPS + 2 if nsa else 0
                SP, PT = (SP1, PT1) if nsa else (SP0, PT0)
                b0 = MLA_STEPS if nsa else 0
                if a0 + t:
                    pe.wait_ge(att_v, a0 + t)
                if b0 + min(max(t - 1, 0), n):
                    pe.wait_ge(pt_sb, b0 + min(max(t - 1, 0), n))
                if 2 <= t:
                    a = t - 2
                    if nsa:
                        g, j = a // 4, a % 4
                        pe.wait_ge(pct_sb, g + 1)
                        pe.wait_ge(c2_v, 1)
                        for m in range(NT):
                            o = MB[:, m, 384:512]
                            mm(o, VB[:, g, j, :], PcT[:, g % 2, m * P:(m + 1) * P], start=True, stop=False)
                            for b, v in enumerate((vs, vw)):
                                for kt in range(m + 1):
                                    p0 = (m + kt) * P
                                    last = mm(o, v[:, kt, g * P:(g + 1) * P], PT[:, b, p0:p0 + P],
                                              start=False, stop=(b == 1 and kt == m))
                    else:
                        for b in range(2):
                            hd = 2 * a + b
                            for m in range(NT):
                                for kt in range(m + 1):
                                    p0 = (m + kt) * P
                                    last = mm(MB[:, 2 * b + m, 384:512], Vm[:, kt, hd * P:(hd + 1) * P],
                                              PT[:, b, p0:p0 + P], start=(kt == 0), stop=(kt == m))
                    last.then_inc(pv_done, 1)
                if nsa and t in CP_STEP:
                    pe.wait_ge(cs_ok, CP_STEP[t] + 1)
                    for m in range(NT):
                        last = nc.tensor.transpose(MB[:, 2 + m, 384:512],
                                                   Pc[:, m, :, :].rearrange("p j n -> p (j n)"), ident[:, :])
                    last.then_inc(cp_ps, 1)
                if 1 <= t <= n:
                    for b in range(2):
                        for k in range(3):
                            last = nc.tensor.transpose(MB[:, 2 + b, k * P:(k + 1) * P],
                                                       SP[:, b, k * P:(k + 1) * P], ident[:, :])
                    last.then_inc(pt_done, 1)
                if t < n:
                    for b in range(2):
                        for m in range(NT):
                            o = MB[:, b, m * P:m * P + (m + 1) * P]
                            if nsa:
                                g, j = t // 4, t % 4
                                last = mm(o, QT[:, g % 2, j, m * P:(m + 1) * P],
                                          (ksT, kwT)[b][:, g, 0:(m + 1) * P], start=True, stop=True)
                            else:
                                hd = 2 * t + b
                                mm(o, QnT[:, hd, m * P:(m + 1) * P], KnT[:, hd, 0:(m + 1) * P],
                                   start=True, stop=False)
                                r = slice(64 * b, 64 * b + 64)
                                last = mm(o, QrT[r, t, m * P:(m + 1) * P], KrT[r, 0:(m + 1) * P],
                                          start=False, stop=True)
                    last.then_inc(s_done, 1)

            def four_heads(banks, src, n0=0):
                for c in range(4):
                    for m in range(NT):
                        o = (c % 2) * SEQ + m * P
                        t = nc.tensor.transpose(banks(c // 2)[:, o:o + P], src(c, m), ident[:, :])
                return t

            def pair_of(hd):
                return hd // 2, slice(64 * (hd % 2), 64 * (hd % 2) + 64)

            def gla_gap(k):
                if k == 0:
                    pe.wait_ge(const_in, 16 * N_CONST)
                    for m in range(NT):
                        last = mm(MB[:, 2 + m, :], AL[0:17, m * P:(m + 1) * P], aw[0:17, :], start=True, stop=True)
                    last.then_inc(ga_ps, 1)
                if k == 1:
                    pe.wait_ge(ga_ok, 1)
                    for m in range(NT):
                        mm(MB[:, m, :], lt[:, :], loga[:, m, :], start=True, stop=True)
                        last = mm(MB[:, 2 + m, :], gt[:, :], loga[:, m, :], start=True, stop=True)
                    last.then_inc(gb_ps, 1)
                if k == 2:
                    pe.wait_ge(ge_v, 1)
                    four_heads(lambda b: MB[:, b, :], lambda c, m: qg[:, m, c * P:(c + 1) * P])
                    four_heads(lambda b: MB[:, 2 + b, :], lambda c, m: kinv[:, m, c * P:(c + 1) * P]).then_inc(gt_ps, 1)
                if k == 3:
                    pe.wait_ge(gt_sb, 1)
                    for c in (0, 2, 1):
                        r = slice(64 * (c % 2), 64 * (c % 2) + 64)
                        if c == 1:
                            pstep(last)
                        for hd in range(8):
                            pr, rr = pair_of(hd)
                            last = mm(MB[rr, pr, c * P:(c + 1) * P], kg[r, c // 2, hd * 64:(hd + 1) * 64],
                               vg[r, c // 2, hd * P:(hd + 1) * P], start=True, stop=True)
                    for pr in range(4):
                        for m in range(NT):
                            o = 384 + 4 * pr + 2 * m
                            last = mm(MB[:, 0, o:o + 2], loga[:, m, pr * P:(pr + 1) * P], endm[:, 0:P:64],
                                      start=True, stop=True)
                    last.then_inc(gu_ps, 1)
                if k == 4:
                    pe.wait_ge(gs_ok, 1)
                    for odd in range(2):
                        if odd:
                            pstep(last)
                        for m in range(NT):
                            for hd in range(odd, 8, 2):
                                pr, rr = pair_of(hd)
                                last = mm(MB[:, 2 * m + hd // 4, (hd % 4) * P:(hd % 4 + 1) * P],
                                          kiT[rr, pr, m * P:(m + 1) * P], qdT[rr, pr, m * P:(m + 1) * P],
                                          start=True, stop=True)
                    last.then_inc(at_ps, 1)
                if k == 5:
                    pe.wait_ge(at_ok, 1)
                    for m in range(NT):
                        for hd in range(8):
                            e = hd % 4
                            mm(MB[:, 2 * m + hd // 4, e * P:(e + 1) * P], AT[m][:, hd // 4, e * P:(e + 1) * P],
                               vg[:, m, hd * P:(hd + 1) * P], start=(e == 0), stop=False, skip_group_check=True)
                    for odd in range(2):
                        if odd:
                            pstep(last)
                        for hd in range(odd, 8, 2):
                            pr, rr = pair_of(hd)
                            e = hd % 4
                            for c in range(1, 4):
                                q = slice(64 * (c % 2), 64 * (c % 2) + 64)
                                last = mm(MB[q, 2 * (c // 2) + hd // 4, e * P:(e + 1) * P],
                                          qdT[rr, pr, c * 64:(c + 1) * 64], SS[rr, pr, c - 1, :],
                                          start=False, stop=True, skip_group_check=True)
                    last.then_inc(go_ps, 1)

            def nsa_op(op, g):
                ob = (SQ + 2 + g) % 2
                if op == "qt":
                    pe.wait_ge(qe_ok, g + 1)
                    four_heads(lambda b: PG[:, ob, b, :],
                               lambda c, m: zq[:, g % 2, m, c * P:(c + 1) * P]).then_inc(qt_ps, 1)
                if op == "cs":
                    pe.wait_ge(qt_sb, g + 1)
                    pe.wait_ge(c2_a, 1)
                    for m in range(NT):
                        for j in range(4):
                            o = m * 64 + j * 16
                            last = mm(PG[:, ob, 0, o:o + 16], QT[:, g % 2, j, m * P:(m + 1) * P],
                                      KcT[:, g, 0:16], start=True, stop=True)
                    last.then_inc(cs_ps, 1)
                if op == "st":
                    att_step(g, True)

            def gap(s, j):
                if (s, j) == (QG, 1):
                    pe.wait_ge(zn_ok, 1)
                    transpose_in(lambda c, m: zc[:, m, 16 + c * P:16 + (c + 1) * P], 4, TQ["cqkv"])
                    for m in range(NT):
                        last = nc.tensor.transpose(MB[0:16, 2, m * P:(m + 1) * P], zc[:, m, 0:16], ident[:, :])
                    last.then_inc(al_ps, 1)
                if (s, j) == (UQR + 2, 0):
                    pe.wait_ge(qr_ok, 1)
                    pe.wait_ge(kr_ok, 1)
                    pe.wait_ge(al_sb, 1)
                    pe.wait_ge(tx_lo, TQ["gla"])
                    four_heads(lambda b: MB[:, 2 + b, :], lambda c, m: qr[:, m, c * P:(c + 1) * P])
                    for m in range(NT):
                        last = nc.tensor.transpose(MB[:, 1, m * P:(m + 1) * P],
                                                   krd[:, m, :, :].rearrange("p a e -> p (a e)"), ident[:, :])
                    last.then_inc(qrt_ps, 1)
                if (s, j) in MLA_AT:
                    t = MLA_AT[(s, j)]
                    if t == 0:
                        pe.wait_ge(qrt_sb, 1)
                        pe.wait_ge(evac_a, UKK + 2)
                        pe.wait_ge(evac_v, UKK + 2)
                    if t == 2:
                        pe.wait_ge(evac_a, UKV + 2)
                        pe.wait_ge(evac_v, UKV + 2)
                    att_step(t, False)
                if (s, j) in GLA_AT:
                    if GLA_AT[(s, j)] == 0:
                        pe.wait_ge(att_v, MLA_STEPS + 2)
                    gla_gap(GLA_AT[(s, j)])
                if (s, j) == (OUT0, 1):
                    pe.wait_ge(go_ok, 1)
                    transpose_in(lambda c, m: gg[:, m, c * P:(c + 1) * P], 4, TQ["gla"])
                if (s, j) in PP_AT:
                    layer = PP_AT[(s, j)]
                    pe.wait_ge(pp_in, 16 * layer + 16)
                    transpose_in(lambda c, m: pp[:, m, c * P:(c + 1) * P], 1, TQ[f"p{layer}"])
                if (s, j) in KT_AT:
                    k = KT_AT[(s, j)]
                    pe.wait_ge(ke_ok, k + 1)
                    if k == 1:
                        pe.wait_ge(evac_a, SVC + 1)
                    if k:
                        pe.wait_ge(kt_sb, k)
                    four_heads(lambda b: MB[:, 2 + b, :], lambda c, m: KB[:, k % 2, m, c * P:(c + 1) * P])\
                        .then_inc(kt_ps, 1)
                if (s, j) == (SW1 + 1, 2):
                    pe.wait_ge(gl_ok, 1)
                    pe.wait_ge(tx_lo, TQ["p1"])
                    mm(MB[:, 0, 0:P], w2s[:, 0, :], GE[:, 0, :, :].rearrange("p g n -> p (g n)"), start=True, stop=True)
                    for g in range(4):
                        for jj in range(4):
                            last = mm(MB[32 * jj:32 * jj + 32, 1, g * P:(g + 1) * P], GE[:, 1, g, :], w2s[:, 1, :],
                                      start=True, stop=True)
                    last.then_inc(c2_ps, 1)
                for op, g in NSA_AT.get((s, j), ()):
                    nsa_op(op, g)

            def nsa_guard(s):
                g = s - (SQ + 2)
                if 0 <= g < 4:
                    pe.wait_ge(cs_in, g + 1)
                    pe.wait_ge(qt_sb, g + 1)

            pe.wait_ge(const_mk, 1)
            pe.wait_ge(start_in, 16 * N_START)
            nc.tensor.transpose(MB[:, 2, 0:72], vin[:, :], ident[0:72, 0:72])
            nc.tensor.transpose(MB[:, 2, P:P + 64], vin2[:, :], ident[0:64, 0:64]).then_inc(vt_ps, 1)

            def fresh_slot(s, src, q, ready, count):
                def transposed(b, m):
                    for c in range(2):
                        o, k = c * SEQ + m * P, (2 * b + c) * P
                        t = nc.tensor.transpose(MB[:, b % 4, o:o + P], src[:, m, k:k + P], ident[:, :])
                    return t

                if q:
                    pe.wait_ge(tx_lo, q)
                for m in range(NT):
                    pe.wait_ge(ready[m], count[m])
                    for b in range(4):
                        t = transposed(b, m)
                        if m == NT - 1:
                            t.then_inc(tx_ps, 1)
                banks_free(s)
                for j in range(4):
                    unit(s, j, XA, need=q + 2 * j + 2)
                    if j < 2:
                        for b in (4 + 2 * j, 5 + 2 * j):
                            pe.wait_ge(tx_lo, q + b - 3)
                            transposed(b, 0)
                            transposed(b, 1).then_inc(tx_ps, 1)

            def norm_slot(k, s, name):
                fresh_slot(s, Fm, TQ[name], (hn_a, hn_v), (k + 1, k + 1))

            pe.wait_ge(vt_sb, 2)
            norm_slot(0, 0, "mix0")
            for s in range(1, OUT0):
                banks_free(s)
                for j in range(4):
                    if s in (UQN, UQN + 1):
                        unit_t(s, j, XB, 0)
                    elif s == UQR:
                        unit(s, j, XB, 1)
                    elif s in (UKK, UKK + 1):
                        unit_t(s, j, XB, 4)
                    elif s in (UKV, UKV + 1):
                        unit(s, j, (XBh[:, 4:8, :], XBl[:, 4:8, :]), 1)
                    else:
                        unit(s, j, XA, 4, shape_of(s)[1])
                    if (s, j) == (QG, 3):
                        pe.wait_ge(tx_lo, TQ["gla"])
                    gap(s, j)

            for layer in range(2):
                s0 = OUTS[layer]
                if layer == 0:
                    banks_free(s0)
                    for j in range(4):
                        if j == 0:
                            pe.wait_ge(att_v, MLA_STEPS + 2)
                        if j == 2:
                            pe.wait_ge(tx_lo, TQ["p0"])
                        unit(s0, j, XB)
                        gap(s0, j)
                else:
                    for n, (panel, part) in enumerate(OUT_UNITS):
                        if part == 0:
                            nsa_guard(OUT1 + panel)
                            banks_free(OUT1 + panel)
                        pe.wait_ge(att_v, MLA_STEPS + 2 + 4 * part + 6)
                        unit(OUT1 + n // 4, n % 4, XB, par=(OUT1 + panel) % 2, pos=part)
                        gap(OUT1 + n // 4, n % 4)
                with pe.Fori(0, 3 - layer) as i:
                    banks_free(i + (s0 + 1 + layer))
                    for j in range(4):
                        unit(i + (s0 + 1 + layer), j, XB, par=(i + (s0 + 1 + layer)) % 2)
                for i in range(4):
                    banks_free(PROJ[layer] + i)
                    unit(PROJ[layer], i, PX, kc=2, need=TQ[f"ffn{layer}"], par=(PROJ[layer] + i) % 2, pos=-1)
                U.projected()
                norm_slot((1, 3)[layer], FFNS[layer], f"ffn{layer}")
                for g, n in enumerate(GROUPS):
                    b = ffn_base(layer, g)
                    q0 = TQ[f"hid{layer}"] + 2 * sum(GROUPS[:g])

                    def hid_in(p):
                        pe.wait_ge(evac_v, p * 2 + (b + 2))
                        transpose_in(lambda c, m: Hb[:, m, c * P:(c + 1) * P], 2, q=p * 2 + q0)

                    for j in range(0 if g else 4, 8):
                        if j % 4 == 0:
                            banks_free(b + j // 4)
                        unit(b + j // 4, j % 4, XA)
                    with pe.Fori(0, n - 1) as i:
                        for j in range(8):
                            s = i * 2 + (b + 2 + j // 4)
                            if j % 4 == 0:
                                banks_free(s)
                            unit(s, j % 4, XA, par=(b + j // 4) % 2)
                            if j == 1:
                                hid_in(i)
                    d0 = b + 2 * n
                    banks_free(d0)
                    for j in range(4):
                        need = q0 + 2 * n if (j + 1) * n > 4 * (n - 1) else q0 + 2 * (n - 1)
                        unit(d0, j, XB, kc=n, need=need)
                        if j == 1:
                            hid_in(n - 1)
                    with pe.Fori(0, 3) as i:
                        banks_free(i + (d0 + 1))
                        for j in range(4):
                            unit(i + (d0 + 1), j, XB, kc=n, par=(i + (d0 + 1)) % 2)
                fresh_slot(GATE[layer], h, TQ[f"ple{layer}"], (upd, upd), (4 * layer + 3, 4 * layer + 4))
                with pe.Fori(0, 3) as i:
                    banks_free(i + (GATE[layer] + 1))
                    for j in range(4):
                        unit(i + (GATE[layer] + 1), j, XA, par=(i + (GATE[layer] + 1)) % 2)
                if layer == 1:
                    break
                norm_slot(2, L1, "mix1")
                for s in range(L1 + 1, OUT1):
                    banks_free(s)
                    nsa_guard(s)
                    for j in range(4):
                        if s == SW1:
                            kv, k = j // 2, j % 2
                            pe.wait_ge(hi_ready, U(s) + j + 1)
                            pe.wait_ge(lo_ready, U(s) + j + 1)
                            pe.wait_ge(bl_ok, kv + 1)
                            for l in range(16):
                                o = PG[:, s % 2, kv, 0:120]
                                hh, ll = (w[:, k, l * P:(l + 1) * P] for w in (wh, wl))
                                b = BL[:, kv, 16 * k + l, :, :]
                                mm(o, hh, b.rearrange("p a n -> p (a n)"), start=(k == 0 and l == 0), stop=False,
                                   skip_group_check=True)
                                last = mm(o[:, 0:60], ll, b[:, 0, :], start=False, stop=(k == 1 and l == 15),
                                          skip_group_check=True)
                            last.then_inc(unit_done, 1)
                        else:
                            unit(s, j, XA, 4, shape_of(s)[1])
                        gap(s, j)

        @block.scalar
        def _(act):
            A = nc.scalar.activation
            step = Steps(act, act_step)
            U = Ring()

            def flat(t):
                return t.rearrange("p a t -> p (a t)")

            def split(s, j, w=2048):
                act.wait_ge(raw_in[j], U(s) * 4 + 16)
                if not (isinstance(s, int) and 4 * s + j < 2):
                    act.wait_ge(unit_done, U(s) + (j - 1))
                A(wh[:, j % 2, 0:w], raw[:, j, 0:w], ACT.Copy).then_inc(hi_ready, 1)

            def split_in(X, n, q, c0, col=None, b0=0, banks=2):
                for b in range(b0, b0 + n):
                    act.wait_ge(tx_ps, q + (b + 1))
                    src = MB[:, b % banks, :]
                    if col is None:
                        A(flat(X[:, bass.ds(c0 + 2 * b, 2), :]), src, ACT.Copy).then_inc(tx_hi, 1)
                    else:
                        for c in range(2):
                            k = 2 * b + c
                            last = A(X[:, c0 + k, :], src[:, c * SEQ:(c + 1) * SEQ], ACT.Copy,
                                     scale=vcol[:, col + k:col + k + 1])
                        last.then_inc(tx_hi, 1)

            def fresh_slot(s, name, col=None, done=0):
                for j in range(4):
                    if j > 1 and j >= done:
                        split(s, j)
                    split_in(XAh, 2, TQ[name], 0, col, 2 * j, 4)
                    if j <= 1 and j >= done:
                        split(s, j)

            def norm_sums(k, mid=lambda: None):
                if k == 0:
                    act.wait_ge(x_in, 32)
                for m in range(NT):
                    if k % 2:
                        act.wait_ge(upd, 1 + m + 4 * (k // 2))
                    A(Fm[:, m, :], h[:, m, :], ACT.Square, accum_out=ss[:, m, 0:1]).then_inc(ssq, 1)
                    if m == 0:
                        mid()

            def norm_scale(k):
                act.wait_ge(ssq, 2 * k + 2)
                act.wait_ge(pw_done, POW.index(("mix0", "ffn0", "mix1", "ffn1")[k]) + 1)
                A(Fm[:, 0, :], h[:, 0, :], ACT.Copy, scale=pwo[:, 0:1]).then_inc(hn_a, 1)

            def att_stage(t, nsa):
                n = NSA_STEPS if nsa else MLA_STEPS
                SP, PT = (SP1, PT1) if nsa else (SP0, PT0)
                b0 = MLA_STEPS if nsa else 0
                if 1 <= t <= n:
                    act.wait_ge(pt_done, b0 + t)
                    A(PT[:, :, :], MB[:, 2:4, 0:384], ACT.Copy).then_inc(pt_sb, 1)
                if nsa and t in CP_STEP:
                    g = CP_STEP[t]
                    act.wait_ge(cp_ps, g + 1)
                    A(PcT[:, g % 2, :].rearrange("p (m t) -> p m t", m=2), MB[:, 2:4, 384:512],
                      ACT.Copy).then_inc(pct_sb, 1)
                if t < n:
                    act.wait_ge(mx_ok, b0 + t + 1)
                    for b in range(2):
                        for m in range(NT):
                            c = SP[:, b, m * P:m * P + (m + 1) * P]
                            k = 2 * m + b
                            last = A(c, c, ACT.Exp, bias=sm[:, k:k + 1], accum_out=sm[:, 4 + k:5 + k])
                    last.then_inc(exp_ok, 1)
                if t >= 2:
                    act.wait_ge(pv_done, b0 + t - 1)
                    for b in range(1 if nsa else 2):
                        hd = t - 2 if nsa else 2 * (t - 2) + b
                        last = A(XBh[:, hd, :].rearrange("p (m t) -> p m t", m=2), MB[:, 2 * b:2 * b + 2, 384:512],
                                 ACT.Copy)
                    last.then_inc(o_hi, 1)

            def gla_stage(k):
                if k == 0:
                    act.wait_ge(ga_ps, 1)
                    A(loga[:, :, :], MB[:, 2:4, :], ACT.Copy).then_inc(ga_t, 1)
                    act.wait_ge(ga_n, 1)
                    step(A(E1[:, :, :], E1[:, :, :], ACT.Exp))
                    A(E1[:, :, :], E1[:, :, :], ACT.Ln, bias=1.0).then_inc(ga_l, 1)
                if k == 1:
                    act.wait_ge(gb_ps, 1)
                    A(E1[:, :, :], MB[:, 0:2, :], ACT.Exp).then_inc(ge_a, 1)
                    A(kinv[:, :, :], MB[:, 0:2, :], ACT.Exp, scale=-1.0).then_inc(ge_a, 1)
                    A(rt[:, :, :], MB[:, 2:4, :], ACT.Exp).then_inc(ge_a, 1)
                if k == 2:
                    act.wait_ge(gt_ps, 1)
                    A(flat(qdT[:, :, :]), flat(MB[:, 0:2, :]), ACT.Copy)
                    A(flat(kiT[:, :, :]), flat(MB[:, 2:4, :]), ACT.Copy).then_inc(gt_sb, 1)
                if k == 3:
                    act.wait_ge(gu_ps, 1)
                    A(flat(decs[:, :, :]), MB[:, 0, 384:400], ACT.Exp).then_inc(gd_sb, 1)
                if k == 5:
                    act.wait_ge(go_ps, 1)
                    for m in range(NT):
                        last = A(AT[m][:, :, :], MB[:, 2 * m:2 * m + 2, :], ACT.Square)
                    last.then_inc(go_sq, 1)

            def evac(s):
                act.wait_ge(unit_done, U(s) + 4)
                src = PG[:, s % 2, 0, :]
                if s in (ZC0, ZC1, ZC2):
                    w = shape_of(s)[1]
                    A(zc[:, 0, 512 * s:512 * s + w], src[:, 0:w], ACT.Copy).then_inc(evac_a, 1)
                elif s in (UQN, UQN + 1, UKK, UKK + 1):
                    t, c = (QnT, 4 * (s - UQN)) if s < UKK else (KnT, 4 * (s - UKK))
                    A(flat(t[:, c:c + 2, :]), src, ACT.Copy).then_inc(evac_a, 1)
                elif s in (GG, GG + 1):
                    act.wait_ge(ge_v, 1)
                    if s == GG + 1:
                        act.wait_ge(evac_v, GG + 1)
                    A(rt[:, :, :], PG[:, s % 2, :, :], ACT.Tanh, scale=0.5).then_inc(evac_a, 1)
                elif s in COPY0:
                    t, c = COPY0[s]
                    A(t[:, 0, c:c + 512], src, ACT.Copy).then_inc(evac_a, 1)
                elif s == SVC:
                    A(KB[:, 1, 0, :], src, ACT.Copy).then_inc(evac_a, 1)
                elif s == SW1:
                    act.wait_ge(ge_x, 1)
                    A(GU[:, :, :], GU[:, :, :], ACT.Tanh, scale=GELU_C / 2).then_inc(ge_e, 1)
                    act.drain().then_inc(evac_a, 1)
                elif s == SGT:
                    act.wait_ge(evac_v, SGT + 1)
                    A(gates[:, :, :], gates[:, :, :], ACT.Tanh, scale=0.5).then_inc(gx_e, 1)
                    act.drain().then_inc(evac_a, 1)
                else:
                    act.drain().then_inc(evac_a, 1)

            def at_gap(k):
                if k == (QG, 1):
                    act.wait_ge(tx_ps, TQ["cqkv"] + 1)
                    split_in(XBh, 4, TQ["cqkv"], 0, 64)
                    act.wait_ge(al_ps, 1)
                    act.wait_ge(const_mk, 1)
                    A(AL[0:16, :], MB[0:16, 2, 0:SEQ], ACT.Copy).then_inc(al_sb, 1)
                if k == (UQR + 2, 0):
                    act.wait_ge(qrt_ps, 1)
                    A(flat(QrT[:, :, :]), flat(MB[:, 2:4, :]), ACT.Copy)
                    A(KrT[:, :], MB[:, 1, 0:SEQ], ACT.Copy).then_inc(qrt_sb, 1)
                if k in MLA_AT:
                    att_stage(MLA_AT[k], False)
                if k in GLA_AT:
                    gla_stage(GLA_AT[k])
                if k == (OUT0, 1):
                    split_in(XBh, 4, TQ["gla"], 8)
                    act.wait_ge(go_ok, 1)
                    act.dma_start(wbc[:, :], T["ln_mix_post"][0:1, :].broadcast_to([P, D])).then_inc(wbc_in, 16)
                    act.dma_start(pp[:, :, :], p_d[0]).then_inc(pp_in, 16)
                if k in PP_AT:
                    split_in(PXh, 1, TQ[f"p{PP_AT[k]}"], 0)
                if k in KT_AT:
                    n = KT_AT[k]
                    act.wait_ge(kt_ps, n + 1)
                    A(flat((kcT, vcT, ksT, kwT)[n][:, :, :]), flat(MB[:, 2:4, :]), ACT.Copy).then_inc(kt_sb, 1)
                if k == (SW1 + 1, 2):
                    act.wait_ge(c2_ps, 1)
                    A(flat(KcT[:, :, :]), MB[:, 0, 0:P], ACT.Copy).then_inc(c2_a, 1)
                for op, g in NSA_AT.get(k, ()):
                    if op == "qt":
                        act.wait_ge(qt_ps, g + 1)
                        A(flat(QT[:, g % 2, :, :]), flat(PG[:, (SQ + g) % 2, :, :]), ACT.Copy).then_inc(qt_sb, 1)
                    if op == "cs":
                        act.wait_ge(cs_in, g + 1)
                        A(csc[:, :, :, :], csc[:, :, :, :], ACT.Exp).then_inc(cs_e, 1)
                    if op == "st":
                        att_stage(g, True)
                if k == (OUT1 + 1, 1):
                    act.wait_ge(att_v, MLA_STEPS + NSA_STEPS + 4)
                    act.dma_start(wbc[:, :], T["ln_mix_post"][1:2, :].broadcast_to([P, D])).then_inc(wbc_in, 16)
                    act.dma_start(pp[:, :, :], p_d[1]).then_inc(pp_in, 16)

            def stage(s, j):
                if j == evac_stage(s):
                    evac(s - 1)
                for k in STAGED.get((s, j), ()):
                    at_gap(k)
                if (s, j) in ((SKC + 1, 3), (SVC + 1, 3)):
                    n = s - SKC - 1
                    act.wait_ge(bt_ok, n + 1)
                    A(BL[:, n, :, 0, :], BT[:, :, :], ACT.Copy).then_inc(bh_ok, 1)

            norm_sums(0)
            act.wait_ge(vt_ps, 1)
            A(vcol[:, :], MB[:, 2, 0:72], ACT.Copy).then_inc(vt_sb, 1)
            A(posT[:, :], MB[:, 2, P:P + 64], ACT.Copy).then_inc(vt_sb, 1)
            norm_scale(0)
            act.wait_ge(vt_sb, 2)
            fresh_slot(0, "mix0", 0)
            act.wait_ge(ang_ok, 1)
            A(sinT[:, :, :], ang[:, :, :], ACT.Sin)
            A(cosT[:, :, :], kk[:, :, :], ACT.Sin).then_inc(trig_ok, 1)

            for s in range(1, OUT0 + 1):
                for j in range(4):
                    split(s, j, shape_of(s)[0] * shape_of(s)[1])
                    stage(s, j)
            stage(OUT0, 4)

            for layer in range(2):
                s0 = OUTS[layer]

                def mixer_panel(i, done=None):
                    s = i + s0
                    act.wait_ge(unit_done, done or U(s) + 4)
                    A(rt[:, 0, :], PG[:, s % 2, 0, :], ACT.Square, accum_out=ss[:, 0, bass.ds(i, 1)]).then_inc(sq_done, 1)
                    act.wait_ge(mul_done, i + (4 * layer + 1))
                    A(rt[:, 1, :], PG[:, s % 2, 1, :], ACT.Square, accum_out=ss[:, 1, bass.ds(i, 1)]).then_inc(evac_a, 1)

                if layer == 0:
                    with act.Fori(0, 3) as i:
                        for j in range(4):
                            split(i + (s0 + 1), j)
                            if j == 1:
                                mixer_panel(i)
                else:
                    for s in (OUT1 + 2, OUT1 + 3):
                        for j in range(4):
                            split(s, j)
                            if (s, j) == (OUT1 + 2, 0):
                                mixer_panel(0, U(OUT1 + 1) + 3)
                            if (s, j) == (OUT1 + 2, 1):
                                act.wait_ge(evac_a, OUT1 + 1)
                            if j == 1:
                                mixer_panel(s - OUT1 - 1)

                pr, f0 = PROJ[layer], FFNS[layer]

                def proj_panel(i):
                    act.wait_ge(unit_done, U(pr) + (i + 1))
                    A(PJ[:, :, i * 512:i * 512 + 512], PG[:, (pr + i) % 2, :, :], ACT.Copy).then_inc(evac_a, 1)

                split(pr, 0, 1024)
                mixer_panel(3)
                act.wait_ge(evac_v, s0 + 4)
                act.dma_start(wbc[:, :], T["ln_ffn_post"][layer:layer + 1, :].broadcast_to([P, D]))\
                    .then_inc(wbc_in, 16)
                split(pr, 1, 1024)
                split(pr, 2, 1024)
                proj_panel(0)
                norm_sums((1, 3)[layer], lambda: proj_panel(1))
                split(pr, 3, 1024)
                norm_scale((1, 3)[layer])
                proj_panel(2)
                proj_panel(3)
                U.projected()
                fresh_slot(f0, f"ffn{layer}", 16 + 32 * layer)

                for g, n in enumerate(GROUPS):
                    b = ffn_base(layer, g)
                    q0 = TQ[f"hid{layer}"] + 2 * sum(GROUPS[:g])

                    def gate_tanh(s):
                        act.wait_ge(unit_done, U(s) + 4)
                        act.wait_ge(evac_v, s)
                        A(Eb[:, :, :], PG[:, b % 2, :, :], ACT.Tanh, scale=0.5).then_inc(evac_a, 1)

                    def down_panel(i, g, d):
                        s = i + d
                        if g == 0:
                            act.wait_ge(unit_done, U(s) + 4)
                            A(Fm[:, 0, bass.ds(i * 512, 512)], PG[:, s % 2, 0, :], ACT.Copy).then_inc(evac_a, 1)
                            return
                        act.drain().then_inc(evac_a, 1)
                        if g == 2:
                            act.wait_ge(add_done, i + (4 * layer + 1))
                            A(rt[:, 0, :], Fm[:, 0, bass.ds(i * 512, 512)], ACT.Square,
                              accum_out=ss[:, 0, bass.ds(i, 1)]).then_inc(sq_done, 1)
                            act.wait_ge(evac_v, s + 1)
                            A(rt[:, 1, :], Fm[:, 1, bass.ds(i * 512, 512)], ACT.Square,
                              accum_out=ss[:, 1, bass.ds(i, 1)]).then_inc(sq_done, 1)

                    if g:
                        split(b, 0)
                        split(b, 1)
                        down_panel(3, g - 1, d0)
                        split(b, 2)
                        split(b, 3)
                    split(b + 1, 0)
                    split(b + 1, 1)
                    gate_tanh(b)
                    split(b + 1, 2)
                    split(b + 1, 3)
                    with act.Fori(0, n - 1) as i:
                        s = i * 2 + (b + 2)
                        split(s, 0)
                        split(s, 1)
                        act.drain().then_inc(evac_a, 1)
                        split(s, 2)
                        split_in(XBh, 2, i * 2 + q0, i * 4)
                        split(s, 3)
                        split(s + 1, 0)
                        split(s + 1, 1)
                        gate_tanh(s)
                        split(s + 1, 2)
                        split(s + 1, 3)
                    d0 = b + 2 * n
                    w = n * 512
                    split(d0, 0, w)
                    split(d0, 1, w)
                    act.drain().then_inc(evac_a, 1)
                    split(d0, 2, w)
                    split_in(XBh, 2, q0 + 2 * (n - 1), 4 * (n - 1))
                    split(d0, 3, w)
                    with act.Fori(0, 3) as i:
                        for j in range(4):
                            split(i + (d0 + 1), j, w)
                            if j == 1:
                                down_panel(i, g, d0)
                gt0 = GATE[layer]

                def gate_panel(i):
                    act.wait_ge(evac_v, i + (gt0 + 1))
                    A(Eb[:, :, :], Eb[:, :, :], ACT.Tanh, scale=0.5).then_inc(evac_a, 1)

                split(gt0, 0)
                down_panel(3, 2, d0)
                split(gt0, 1)
                act.wait_ge(upd, 4 * layer + 3)
                act.dma_start(wbc[:, :], T["ple_b_gate"][layer:layer + 1, :].broadcast_to([P, D])).then_inc(wbc_in, 16)
                fresh_slot(gt0, f"ple{layer}", done=2)
                def square_panel(i):
                    act.wait_ge(h_ok, i + 1)
                    for m in range(NT):
                        last = A(rt[:, m, :], h[:, m, bass.ds(i * 512, 512)], ACT.Square,
                                 accum_out=ss[:, m, bass.ds(i, 1)])
                        if not isinstance(i, int):
                            continue
                        last.then_inc(ssq, 1)
                    return last

                with act.Fori(0, 3) as i:
                    if layer == 0:
                        step.enter(i, 1)
                    for j in range(4):
                        split(i + (gt0 + 1), j)
                        if j == 1:
                            gate_panel(i)
                    if layer == 0:
                        step(square_panel(i))
                        step.leave(3)
                if layer == 1:
                    gate_panel(3)
                    break
                split(L1, 0)
                gate_panel(3)
                square_panel(3)
                norm_scale(2)
                fresh_slot(L1, "mix1", 32, done=1)
                for s in range(L1 + 1, OUT1 + 2):
                    for j in range(4):
                        split(s, j, shape_of(s)[0] * shape_of(s)[1])
                        stage(s, j)
                stage(OUT1 + 1, 4)

        @block.vector
        def _(v):
            V = nc.vector
            step = Steps(v, dve_step)
            U = Ring()

            def flat(t):
                return t.rearrange("p a t -> p (a t)")

            def split(s, j, w=2048):
                v.wait_ge(hi_ready, U(s) + (j + 1))
                V.tensor_tensor(wl[:, j % 2, 0:w], raw[:, j, 0:w], wh[:, j % 2, 0:w].bitcast(F32),
                                ALU.subtract).then_inc(lo_ready, 1)

            def split_in(X, n, q, c0, col=None, b0=0, banks=2):
                for b in range(b0, b0 + n):
                    v.wait_ge(tx_hi, q + (b + 1))
                    src = MB[:, b % banks, :]
                    if col is None:
                        c = bass.ds(c0 + 2 * b, 2)
                        V.tensor_tensor(flat(X[1][:, c, :]), src, flat(X[0][:, c, :]).bitcast(F32),
                                        ALU.subtract).then_inc(tx_lo, 1)
                    else:
                        for c in range(2):
                            k = 2 * b + c
                            last = V.scalar_tensor_tensor(
                                X[1][:, c0 + k, :], src[:, c * SEQ:(c + 1) * SEQ], vcol[:, col + k:col + k + 1],
                                X[0][:, c0 + k, :].bitcast(F32), ALU.mult, ALU.subtract)
                        last.then_inc(tx_lo, 1)

            def ask(name):
                v.wait_ge(pw_done, POW.index(name) + 1)

            def fresh_slot(s, name, col=None, done=0):
                for j in range(4):
                    if j > 1 and j >= done:
                        split(s, j)
                    split_in(XA, 2, TQ[name], 0, col, 2 * j, 4)
                    if j <= 1 and j >= done:
                        split(s, j)

            def norm_out(k, between=lambda: None):
                name = ("mix0", "ffn0", "mix1", "ffn1")[k]
                v.wait_ge(ssq, 2 * k + 2)
                src = ss[:, :, 0]
                if k == 2:
                    step(V.tensor_reduce(pwi[:, 0:2], ss[:, :, :], AX.X, ALU.add))
                    src = pwi[:, 0:2]
                V.tensor_scalar(pwi[:, 0:2], src, 1.0 / D, EPS, ALU.mult, ALU.add).then_inc(pw_req, 1)
                between()
                ask(name)
                V.tensor_scalar(Fm[:, 1, :], h[:, 1, :], pwo[:, 1:2], None, ALU.mult).then_inc(hn_v, 1)

            def post_norm(name, between=lambda: None, mid=lambda: None):
                step(V.tensor_reduce(pwi[:, 0:2], ss[:, :, :], AX.X, ALU.add))
                V.tensor_scalar(pwi[:, 0:2], pwi[:, 0:2], 1.0 / D, EPS, ALU.mult, ALU.add).then_inc(pw_req, 1)
                between()
                ask(name)
                for m in range(NT):
                    V.scalar_tensor_tensor(h[:, m, :], Fm[:, m, :], pwo[:, m:m + 1], h[:, m, :],
                                           ALU.mult, ALU.add).then_inc(upd, 1)
                    if m == 0:
                        mid()

            def rope(src, dst, cos, sin, hd, done, par_sem):
                for m in range(NT):
                    n = 512 // (2 * hd)
                    a, b = (rt[:, k, :].rearrange("p (h x e) -> p h x e", x=2, e=hd) for k in range(2))
                    cs, sn = (t[:, m, ::64 // hd].rearrange("p (h x e) -> p h x e", h=1, x=1)
                              .broadcast_to([P, n, 2, hd]) for t in (cos, sin))
                    V.tensor_tensor(a, src(m), cs, ALU.mult)
                    ins = V.tensor_tensor(b, src(m), sn, ALU.mult)
                    if m == NT - 1:
                        ins.then_inc(par_sem, 1)
                        v.wait_ge(par_sem, cur[0] + 1)
                    else:
                        step(ins)
                    V.tensor_tensor(dst(m)[:, :, 0, :], a[:, :, 0, :], b[:, :, 1, :], ALU.subtract)
                    last = V.tensor_tensor(dst(m)[:, :, 1, :], a[:, :, 1, :], b[:, :, 0, :], ALU.add)
                    if m == 0:
                        step(last)
                last.then_inc(done, 1)

            cur = [0]

            def att_stage(t, nsa):
                n = NSA_STEPS if nsa else MLA_STEPS
                SP = SP1 if nsa else SP0
                b0 = MLA_STEPS if nsa else 0
                scale = NSA_SCALE if nsa else MLA_SCALE
                if t < n:
                    v.wait_ge(s_done, b0 + t + 1)
                    for b in range(2):
                        last = V.scalar_tensor_tensor(SP[:, b, :], MB[:, b, 0:384], scale, flat(cmask[:, :, :]),
                                                      ALU.mult, ALU.add)
                    step(last)
                    V.tensor_reduce(sm[:, 0:2], SP[:, :, 0:P], AX.X, ALU.max, negate=True)
                    V.tensor_reduce(sm[:, 2:4], SP[:, :, P:384], AX.X, ALU.max, negate=True).then_inc(mx_ok, 1)
                    v.wait_ge(exp_ok, b0 + t + 1)
                    step(V.reciprocal(sm[:, 8:12], sm[:, 4:8]))
                    if nsa:
                        f = sm[:, 8:12].rearrange("p (m b) -> p m b", m=2)
                        step(V.tensor_tensor(f, f, gates[:, :, 3 * t + 1:3 * t + 3], ALU.mult))
                    for b in range(2):
                        for m in range(NT):
                            c = SP[:, b, m * P:m * P + (m + 1) * P]
                            k = 8 + 2 * m + b
                            last = V.tensor_scalar(c, c, sm[:, k:k + 1], None, ALU.mult)
                    if t < 2:
                        last.then_inc(att_v, 1)
                if t >= 2:
                    v.wait_ge(o_hi, b0 + t - 1)
                    for b in range(1 if nsa else 2):
                        hd = t - 2 if nsa else 2 * (t - 2) + b
                        x = [q[:, hd, :].rearrange("p (m t) -> p m t", m=2) for q in XB]
                        last = V.tensor_tensor(x[1], MB[:, 2 * b:2 * b + 2, 384:512], x[0].bitcast(F32), ALU.subtract)
                    last.then_inc(att_v, 1)

            def gla_stage(k):
                if k == 0:
                    v.wait_ge(ga_t, 1)
                    V.scalar_tensor_tensor(flat(E1[:, :, :]), flat(loga[:, :, :]), -1.0, flat(loga[:, :, :]),
                                           ALU.mult, ALU.min).then_inc(ga_n, 1)
                    v.wait_ge(ga_l, 1)
                    V.scalar_tensor_tensor(flat(loga[:, :, :]), flat(loga[:, :, :]), 0.0, flat(E1[:, :, :]),
                                           ALU.min, ALU.subtract).then_inc(ga_ok, 1)
                if k == 1:
                    v.wait_ge(evac_a, KG + 1)
                    v.wait_ge(ge_a, 1)
                    V.scalar_tensor_tensor(flat(qg[:, :, :]), flat(qg[:, :, :]), 0.125, flat(E1[:, :, :]),
                                           ALU.mult, ALU.mult)
                    v.wait_ge(ge_a, 2)
                    V.tensor_tensor(kinv[:, :, :], kg[:, :, :], kinv[:, :, :], ALU.mult)
                    v.wait_ge(ge_a, 3)
                    V.tensor_tensor(kg[:, :, :], kg[:, :, :], rt[:, :, :], ALU.mult).then_inc(ge_v, 1)
                if k == 3:
                    v.wait_ge(gd_sb, 1)
                    step(V.tensor_copy(SS[:, :, 0, :], MB[:, :, 0:P]))
                    for c in (1, 2):
                        for pr in range(4):
                            ins = V.scalar_tensor_tensor(SS[:, pr, c, :], SS[:, pr, c - 1, :], decs[:, pr, c:c + 1],
                                                         MB[:, pr, c * P:(c + 1) * P], ALU.mult, ALU.add)
                        if c == 1:
                            step(ins)
                    ins.then_inc(gs_ok, 1)
                if k == 4:
                    v.wait_ge(at_zero, 1)
                    v.wait_ge(at_ps, 1)
                    mask = lt[:, :].bitcast(U32).rearrange("p (h t) -> p h t", h=1).broadcast_to([P, 4, P])
                    for m in range(NT):
                        for hf in range(2):
                            last = V.copy_predicated(AT[m][:, hf, :].rearrange("p (h t) -> p h t", h=4), mask,
                                                     MB[:, 2 * m + hf, :].rearrange("p (h t) -> p h t", h=4))
                    last.then_inc(at_ok, 1)
                if k == 5:
                    v.wait_ge(go_sq, 1)
                    for m in range(NT):
                        last = V.tensor_reduce(pwi[:, 8 * m:8 * m + 8], AT[m][:, :, :].rearrange(
                            "p f (h t) -> p (f h) t", h=4), AX.X, ALU.add)
                    step(last)
                    V.tensor_scalar(pwi[:, :], pwi[:, :], 1.0 / P, EPS, ALU.mult, ALU.add).then_inc(pw_req, 1)

            def gla_out():
                ask("gla")
                for m in range(NT):
                    for hf in range(2):
                        k = 8 * m + 4 * hf
                        r = pwo[:, k:k + 4].rearrange("p (h t) -> p h t", t=1).broadcast_to([P, 4, P])
                        step(V.tensor_tensor(oT[:, :].rearrange("p (h t) -> p h t", h=4),
                                             MB[:, 2 * m + hf, :].rearrange("p (h t) -> p h t", h=4), r, ALU.mult))
                        x = gg[:, m, 512 * hf:512 * hf + 512]
                        last = V.tensor_tensor(x, x, oT[:, :], ALU.mult)
                        if k < 12:
                            step(last)
                last.then_inc(go_ok, 1)

            def evac(s):
                v.wait_ge(unit_done, U(s) + 4)
                cur[0] = s
                par = s % 2
                src = PG[:, par, 1, :]
                if s in (ZC0, ZC1, ZC2):
                    w = shape_of(s)[1]
                    V.tensor_copy(zc[:, 1, 512 * s:512 * s + w], src[:, 0:w]).then_inc(evac_v, 1)
                elif s in (UQN, UQN + 1, UKK, UKK + 1):
                    t, c = (QnT, 4 * (s - UQN)) if s < UKK else (KnT, 4 * (s - UKK))
                    V.tensor_copy(flat(t[:, c + 2:c + 4, :]), src).then_inc(evac_v, 1)
                elif s == UQR:
                    rope(lambda m: PG[:, par, m, :].rearrange("p (h x e) -> p h x e", x=2, e=32),
                         lambda m: qr[:, m, :].rearrange("p (h x e) -> p h x e", x=2, e=32), cosT, sinT, 32,
                         qr_ok, evac_v)
                elif s in (GG, GG + 1):
                    v.wait_ge(evac_a, s + 1)
                    c = 512 * (s - GG)
                    V.scalar_tensor_tensor(gg[:, :, c:c + 512], rt[:, :, :], 1.0, PG[:, par, :, :],
                                           ALU.add, ALU.mult).then_inc(evac_v, 1)
                    v.wait_ge(evac_v, s + 1)
                    v.wait_ge(const_in, 16 * N_CONST)
                    for m in range(NT):
                        x = gg[:, m, c:c + 512].rearrange("p (h t) -> p h t", h=4)
                        gn = gnw[:, :].rearrange("p (h t) -> p h t", h=1).broadcast_to([P, 4, P])
                        last = V.scalar_tensor_tensor(x, x, 0.5, gn, ALU.mult, ALU.mult)
                    step(last)
                elif s in COPY0:
                    t, c = COPY0[s]
                    V.tensor_copy(t[:, 1, c:c + 512], src).then_inc(evac_v, 1)
                elif s == SVC:
                    V.tensor_copy(KB[:, 1, 1, :], src).then_inc(evac_v, 1)
                    v.wait_ge(evac_v, s + 1)
                    v.sem_inc(ke_ok, 1)
                elif s in (SKC, SKS, SKW) or SQ <= s < SQ + 4:
                    if s >= SQ:
                        g = s - SQ
                        if g >= 2:
                            v.wait_ge(qt_ps, g - 1)
                        dst, done = (lambda m: zq[:, g % 2, m, :]), qe_ok
                    else:
                        k = {SKC: 0, SKS: 2, SKW: 3}[s]
                        if k >= 2:
                            v.wait_ge(kt_ps, k - 1)
                        dst, done = (lambda m: KB[:, k % 2, m, :]), ke_ok
                    rope(lambda m: PG[:, par, m, :].rearrange("p (h x e) -> p h x e", x=2, e=64),
                         lambda m: dst(m).rearrange("p (h x e) -> p h x e", x=2, e=64), cosT, sinT, 64, done, evac_v)
                elif s == SW1:
                    step(V.tensor_copy(GU[:, :, :], PG[:, par, :, 60:120]))
                    V.tensor_tensor(GX[:, :, :], PG[:, par, :, 0:60], GU[:, :, :], ALU.add).then_inc(evac_v, 1)
                    v.wait_ge(evac_v, s + 1)
                    step(V.tensor_tensor(GU[:, :, :], GX[:, :, :], GX[:, :, :], ALU.mult))
                    step(V.tensor_scalar(GU[:, :, :], GU[:, :, :], 0.044715, 1.0, ALU.mult, ALU.add))
                    V.tensor_tensor(GU[:, :, :], GU[:, :, :], GX[:, :, :], ALU.mult).then_inc(ge_x, 1)
                    v.wait_ge(ge_e, 1)
                    step(V.tensor_scalar(GU[:, :, :], GU[:, :, :], 1.0, 0.5, ALU.add, ALU.mult))
                    x = [t[:, :, :].rearrange("p k (g n) -> p k g n", g=4) for t in (GX, GU)]
                    V.tensor_tensor(GE[:, :, :, 0:NCMP], x[0], x[1], ALU.mult).then_inc(gl_ok, 1)
                elif s == SGT:
                    b = gbias[:, :].rearrange("p (m n) -> p m n", m=1).broadcast_to([P, NT, W_GT])
                    V.tensor_tensor(gates[:, :, :], PG[:, par, :, 0:W_GT], b, ALU.add).then_inc(evac_v, 1)
                    v.wait_ge(gx_e, 1)
                    step(V.tensor_scalar(gates[:, :, :], gates[:, :, :], 1.0, 0.5, ALU.add, ALU.mult))

            def lowrank_norm():
                v.wait_ge(evac_a, ZC2 + 1)
                for k in range(2):
                    for m in range(NT):
                        x = zc[:, m, 16 + 512 * k:528 + 512 * k]
                        step(V.tensor_tensor_reduce(out=rt[:, 0, :], in0=x, in1=x, scale=1.0, scalar=0.0,
                                                    op0=ALU.mult, op1=ALU.add,
                                                    accum_out=pwi[:, 2 * k + m:2 * k + m + 1]))
                V.tensor_scalar(pwi[:, 0:4], pwi[:, 0:4], 1.0 / 512, EPS, ALU.mult, ALU.add).then_inc(pw_req, 1)
                ask("cqkv")
                for k in range(2):
                    for m in range(NT):
                        x = zc[:, m, 16 + 512 * k:528 + 512 * k]
                        last = V.tensor_scalar(x, x, pwo[:, 2 * k + m:2 * k + m + 1], None, ALU.mult)
                last.then_inc(zn_ok, 1)
                for m in range(NT):
                    x = zc[:, m, 1040:1104].rearrange("p (x e) -> p x e", x=2)
                    a, b = (rt[:, k, 0:64].rearrange("p (x e) -> p x e", x=2) for k in range(2))
                    cs, sn = (t[:, m, ::2].rearrange("p (x e) -> p x e", x=1).broadcast_to([P, 2, 32])
                              for t in (cosT, sinT))
                    V.tensor_tensor(a, x, cs, ALU.mult)
                    step(V.tensor_tensor(b, x, sn, ALU.mult))
                    for d in range(2):
                        V.tensor_tensor(krd[:, m, d, 0:32], a[:, 0, :], b[:, 1, :], ALU.subtract)
                        last = V.tensor_tensor(krd[:, m, d, 32:64], a[:, 1, :], b[:, 0, :], ALU.add)
                    if m == 0:
                        step(last)
                last.then_inc(kr_ok, 1)
                v.wait_ge(kr_ok, 1)

            def compressed(g):
                v.wait_ge(cs_ps, g + 1)
                for m in range(NT):
                    nm = negm[:, m, :].rearrange("p (j n) -> p j n", j=1).broadcast_to([P, 4, 16])
                    last = V.scalar_tensor_tensor(
                        csc[:, m, :, :], PG[:, (SQ + g) % 2, 0, 64 * m:64 * m + 64].rearrange("p (j n) -> p j n", j=4),
                        NSA_SCALE, nm, ALU.mult, ALU.add)
                step(last)
                c8 = csc[:, :, :, :].rearrange("p m j n -> p (m j) n")
                col = lambda k: cst[:, k, :].rearrange("p (a n) -> p a n", n=1).broadcast_to([P, 8, 16])
                step(V.tensor_reduce(cst[:, 0, :], c8, AX.X, ALU.max))
                V.tensor_tensor(c8, c8, col(0), ALU.subtract).then_inc(cs_in, 1)
                v.wait_ge(cs_e, g + 1)
                step(V.tensor_reduce(cst[:, 1, :], c8, AX.X, ALU.add))
                step(V.reciprocal(cst[:, 2, :], cst[:, 1, :]))
                f = cst[:, 2, :].rearrange("p (m j) -> p m j", m=2)
                step(V.tensor_tensor(f, f, gates[:, :, 12 * g:12 * g + 12:3], ALU.mult))
                step(V.tensor_tensor(c8, c8, col(2), ALU.mult))
                if g:
                    v.wait_ge(cp_ps, g)
                ok = okm[:, :, :].rearrange("p m (j n) -> p m j n", j=1).broadcast_to([P, NT, 4, 16])
                V.tensor_tensor(Pc[:, :, :, 0:16], csc[:, :, :, :], ok, ALU.mult).then_inc(cs_ok, 1)

            def at_gap(k):
                if k == (QG, 1):
                    split_in(XB, 4, TQ["cqkv"], 0, 64)
                if k in MLA_AT:
                    att_stage(MLA_AT[k], False)
                if k in GLA_AT:
                    gla_stage(GLA_AT[k])
                if k == (OUT0, 1):
                    split_in(XB, 4, TQ["gla"], 8)
                if k in PP_AT:
                    split_in(PX, 1, TQ[f"p{PP_AT[k]}"], 0)
                if k == (SW1 + 1, 2):
                    v.wait_ge(vb_zero, 1)
                    v.wait_ge(c2_ps, 1)
                    for jj in range(4):
                        r = slice(32 * jj, 32 * jj + 32)
                        last = V.tensor_copy(VB[r, :, jj, :], MB[r, 1, :].rearrange("p (g t) -> p g t", g=4))
                    last.then_inc(c2_v, 1)
                for op, g in NSA_AT.get(k, ()):
                    if op == "cs":
                        compressed(g)
                    if op == "st":
                        att_stage(g, True)

            def stage(s, j):
                if j == evac_stage(s):
                    evac(s - 1)
                if (s, j) == (QG, 0):
                    lowrank_norm()
                if (s, j) == (OUT0, 1):
                    gla_out()
                for k in STAGED.get((s, j), ()):
                    at_gap(k)
                if (s, j) in ((SKC + 1, 3), (SVC + 1, 3)):
                    n = s - SKC - 1
                    v.wait_ge(kt_sb, n + 1)
                    if n:
                        v.wait_ge(bh_ok, 1)
                    src = (kcT, vcT)[n][:, :, :].rearrange("p g (n l) -> p l g n", l=16)
                    for a in range(2):
                        c = 32 * n + 16 * a
                        pos = posT[:, c:c + 16].rearrange("p (l g n) -> p l g n", g=1, n=1).broadcast_to([P, 16, 4, 15])
                        last = V.tensor_tensor(BT[:, 16 * a:16 * a + 16, :].rearrange("p l (g n) -> p l g n", g=4),
                                               src[:, :, :, a:a + 15], pos, ALU.add)
                    last.then_inc(bt_ok, 1)
                    v.wait_ge(bh_ok, n + 1)
                    v.wait_ge(bt_ok, n + 1)
                    V.tensor_tensor(BL[:, n, :, 1, :], BT[:, :, :], BL[:, n, :, 0, :].bitcast(F32),
                                    ALU.subtract).then_inc(bl_ok, 1)

            v.wait_ge(x_in, 32)
            norm_out(0)
            v.wait_ge(vt_sb, 2)
            fresh_slot(0, "mix0", 0)

            v.wait_ge(const_mk, 1)
            v.wait_ge(start_in, 16 * N_START)
            step(V.tensor_copy(posf[:, :], posi[:, :]))
            for m in range(NT):
                last = V.tensor_scalar(ang[:, m, :], invb[:, :], posf[:, m:m + 1], None, ALU.mult)
            step(last)
            step(V.tensor_scalar(kk[:, :, :], ang[:, :, :], 1.0 / TWO_PI, MAGIC, ALU.mult, ALU.add))
            step(V.tensor_scalar(kk[:, :, :], kk[:, :, :], MAGIC, None, ALU.subtract))
            for c in (C1, C2, C3):
                step(V.scalar_tensor_tensor(flat(ang[:, :, :]), flat(kk[:, :, :]), -c, flat(ang[:, :, :]),
                                            ALU.mult, ALU.add))
            step(V.tensor_scalar(ang[:, :, :], ang[:, :, :], PI_IN, -PI_IN, ALU.min, ALU.max))
            step(V.scalar_tensor_tensor(flat(kk[:, :, :]), flat(ang[:, :, :]), -1.0, flat(ang[:, :, :]),
                                        ALU.mult, ALU.min))
            V.tensor_scalar(kk[:, :, :], kk[:, :, :], TWO_PI / 4, None, ALU.add).then_inc(ang_ok, 1)
            v.wait_ge(trig_ok, 1)

            for s in range(1, OUT0 + 1):
                for j in range(4):
                    split(s, j, shape_of(s)[0] * shape_of(s)[1])
                    stage(s, j)
            stage(OUT0, 4)

            for layer in range(2):
                s0 = OUTS[layer]

                def mixer_panel(i, done=None):
                    s = i + s0
                    v.wait_ge(unit_done, done or U(s) + 4)
                    v.wait_ge(wbc_in, 16 * (3 * layer + 1))
                    c = bass.ds(i * 512, 512)
                    V.tensor_tensor(Fm[:, 1, c], PG[:, s % 2, 1, :], wbc[:, c], ALU.mult).then_inc(mul_done, 1)
                    v.wait_ge(sq_done, i + (12 * layer + 1))
                    V.tensor_tensor(Fm[:, 0, c], PG[:, s % 2, 0, :], wbc[:, c], ALU.mult).then_inc(evac_v, 1)

                if layer == 0:
                    with v.Fori(0, 3) as i:
                        for j in range(4):
                            split(i + (s0 + 1), j)
                            if j == 1:
                                mixer_panel(i)
                else:
                    for s in (OUT1 + 2, OUT1 + 3):
                        for j in range(4):
                            split(s, j)
                            if (s, j) == (OUT1 + 2, 0):
                                mixer_panel(0, U(OUT1 + 1) + 3)
                            if j == 1:
                                mixer_panel(s - OUT1 - 1)

                pr, f0 = PROJ[layer], FFNS[layer]
                split(pr, 0, 1024)
                mixer_panel(3)
                v.wait_ge(evac_a, s0 + 4)
                v.wait_ge(evac_v, s0 + 4)
                v.sem_inc(evac_v, 4)
                post_norm(f"post{layer}", lambda: split(pr, 1, 1024), lambda: split(pr, 2, 1024))
                norm_out((1, 3)[layer], lambda: split(pr, 3, 1024))
                U.projected()
                fresh_slot(f0, f"ffn{layer}", 16 + 32 * layer)

                for g, n in enumerate(GROUPS):
                    b = ffn_base(layer, g)
                    q0 = TQ[f"hid{layer}"] + 2 * sum(GROUPS[:g])

                    def silu(s):
                        v.wait_ge(evac_a, s + 1)
                        V.scalar_tensor_tensor(Eb[:, :, :], Eb[:, :, :], 1.0, PG[:, b % 2, :, :],
                                               ALU.add, ALU.mult).then_inc(evac_v, 1)

                    def hidden(s):
                        v.wait_ge(unit_done, U(s) + 4)
                        v.wait_ge(evac_v, s)
                        V.scalar_tensor_tensor(Hb[:, :, :], Eb[:, :, :], 0.5, PG[:, (b + 1) % 2, :, :],
                                               ALU.mult, ALU.mult).then_inc(evac_v, 1)

                    def down_panel(i, g, d):
                        s = i + d
                        v.wait_ge(unit_done, U(s) + 4)
                        c = bass.ds(i * 512, 512)
                        if g == 0:
                            V.tensor_copy(Fm[:, 1, c], PG[:, s % 2, 1, :]).then_inc(evac_v, 1)
                            return
                        first = V.tensor_tensor(Fm[:, 0, c], PG[:, s % 2, 0, :], Fm[:, 0, c], ALU.add)
                        if g == 2:
                            first.then_inc(add_done, 1)
                        V.tensor_tensor(Fm[:, 1, c], PG[:, s % 2, 1, :], Fm[:, 1, c], ALU.add).then_inc(evac_v, 1)

                    def weigh(i):
                        c = bass.ds(i * 512, 512)
                        v.wait_ge(wbc_in, 16 * (3 * layer + 2))
                        for m in range(NT):
                            v.wait_ge(sq_done, i * 2 + (12 * layer + 5 + m))
                            last = V.tensor_tensor(Fm[:, m, c], Fm[:, m, c], wbc[:, c], ALU.mult)
                        step(last)

                    if g:
                        split(b, 0)
                        split(b, 1)
                        down_panel(3, g - 1, d0)
                        split(b, 2)
                        split(b, 3)
                    split(b + 1, 0)
                    split(b + 1, 1)
                    silu(b)
                    split(b + 1, 2)
                    split(b + 1, 3)
                    with v.Fori(0, n - 1) as i:
                        s = i * 2 + (b + 2)
                        split(s, 0)
                        split(s, 1)
                        hidden(i * 2 + (b + 1))
                        split(s, 2)
                        split_in(XB, 2, i * 2 + q0, i * 4)
                        split(s, 3)
                        split(s + 1, 0)
                        split(s + 1, 1)
                        silu(s)
                        split(s + 1, 2)
                        split(s + 1, 3)
                    d0 = b + 2 * n
                    w = n * 512
                    split(d0, 0, w)
                    split(d0, 1, w)
                    hidden(d0 - 1)
                    split(d0, 2, w)
                    split_in(XB, 2, q0 + 2 * (n - 1), 4 * (n - 1))
                    split(d0, 3, w)
                    with v.Fori(0, 3) as i:
                        step.enter(i, 1 if g == 2 else 0)
                        for j in range(4):
                            split(i + (d0 + 1), j, w)
                            if j == 1:
                                down_panel(i, g, d0)
                            if j == 2 and g == 2:
                                weigh(i)
                        step.leave(3)
                gt0 = GATE[layer]

                def gate_add(i):
                    s = i + gt0
                    v.wait_ge(unit_done, U(s) + 4)
                    v.wait_ge(wbc_in, 16 * (3 * layer + 3))
                    c = bass.ds(i * 512, 512)
                    V.tensor_tensor(Eb[:, 0, :], PG[:, s % 2, 0, :], wbc[:, c], ALU.add)
                    V.tensor_tensor(Eb[:, 1, :], PG[:, s % 2, 1, :], wbc[:, c], ALU.add).then_inc(evac_v, 1)

                def gate_mul(i):
                    s, c = i + gt0, bass.ds(i * 512, 512)
                    v.wait_ge(evac_a, s + 1)
                    step(V.scalar_tensor_tensor(Eb[:, :, :], Eb[:, :, :], 1.0, PJ[:, :, c], ALU.add, ALU.mult))
                    V.scalar_tensor_tensor(h[:, :, c], Eb[:, :, :], 0.5, h[:, :, c],
                                           ALU.mult, ALU.add).then_inc(h_ok, 1)

                split(gt0, 0)
                down_panel(3, 2, d0)
                v.wait_ge(evac_v, d0 + 4)
                v.wait_ge(sq_done, 12 * layer + 12)
                post_norm(f"fpost{layer}", lambda: weigh(3))
                fresh_slot(gt0, f"ple{layer}", done=1)
                with v.Fori(0, 3) as i:
                    step.enter(i, 1)
                    for j in range(4):
                        split(i + (gt0 + 1), j)
                        if j == 1:
                            gate_add(i)
                        if j == 2:
                            gate_mul(i)
                    step.leave(3)
                if layer == 1:
                    gate_add(3)
                    gate_mul(3)
                    break
                split(L1, 0)
                gate_add(3)
                gate_mul(3)
                norm_out(2)
                fresh_slot(L1, "mix1", 32, done=1)
                for s in range(L1 + 1, OUT1 + 2):
                    for j in range(4):
                        split(s, j, shape_of(s)[0] * shape_of(s)[1])
                        stage(s, j)
                stage(OUT1 + 1, 4)


def kernel(**inputs):
    import concourse.bacc as bacc
    from concourse.bass_utils import run_bass_kernel_spmd

    nc = bacc.Bacc("TRN2", target_bir_lowering=False, num_devices=1, dynamic_dma_scratch_size=1024)
    arrays, tensors = {}, {}
    for name, value in inputs.items():
        a = np.ascontiguousarray(value)
        if name == "nsa_cmp_w1":
            a = np.ascontiguousarray(a.reshape(2, CMP_LEN, P, P).transpose(0, 2, 1, 3))
        arrays[f"in_{name}"] = a
        tensors[name] = nc.dram_tensor(f"in_{name}", a.shape, mybir.dt.from_np(a.dtype), kind="ExternalInput").ap()
    inv = np.power(10000.0, -np.arange(0, 128, 2) / 128.0).astype(np.float32)[None, :]
    arrays["in_rope_inv"] = inv
    tensors["rope_inv"] = nc.dram_tensor("in_rope_inv", inv.shape, F32, kind="ExternalInput").ap()
    tensors["out"] = nc.dram_tensor("out", (1, SEQ, D), F32, kind="ExternalOutput").ap()
    build(nc, tensors)
    r = run_bass_kernel_spmd(nc, [arrays], core_ids=[0])
    return r.results[0]["out"]
```

```python
from contextlib import ExitStack

import numpy as np

import concourse.bass as bass
from concourse import mybir
from concourse.alu_op_type import AluOpType as ALU

F32 = mybir.dt.float32
F32R = mybir.dt.float32r
U32 = mybir.dt.uint32
I32 = mybir.dt.int32
ACT = mybir.ActivationFunctionType
AX = mybir.AxisListType

P = 128
D = 2048
SEQ = 256
NT = SEQ // P
KC = D // P
FFN = 5632
PLE = 256
EPS = 1e-6
NEG = -1e30
TAU = 16.0
CMP_LEN, CMP_STRIDE, NCMP = 32, 16, 15
MLA_SCALE = float((128 + 64) ** -0.5)
NSA_SCALE = float(128 ** -0.5)
GELU_C = float(2.0 * np.sqrt(2.0 / np.pi))
TWO_PI = 6.283185307179586
C1 = 6.28125
C2 = 0.00193500518798828125
C3 = TWO_PI - C1 - C2
MAGIC = 12582912.0
PI_IN = 3.1415925

ZC0, ZC1, ZC2, QG, UQN, UQR, UKK, UKV, KG, VG, GG, OUT0 = 0, 1, 2, 3, 4, 6, 7, 9, 11, 12, 14, 16
FFN0 = OUT0 + 8
GROUPS = (4, 4, 3)
FFN_SLOTS = sum(2 * n + 4 for n in GROUPS)
L1 = FFN0 + FFN_SLOTS + 4
SKC, SVC, SKS, SW1, SKW, SVS, SVW, SGT, SQ, OUT1 = (L1 + i for i in (0, 1, 2, 3, 4, 5, 6, 7, 8, 12))
FFN1 = OUT1 + 8
OUTS, FFNS = (OUT0, OUT1), (FFN0, FFN1)
PROJ = tuple(s + 4 for s in OUTS)
GATE = tuple(f + FFN_SLOTS for f in FFNS)
NSLOTS = GATE[1] + 4
W_GT = 48
W_ZC = 1104 // 3
W_VG = (512 + W_GT) // 2

TQ = {}
_n = 0
for _name, _k in (("mix0", 8), ("cqkv", 4), ("gla", 4), ("p0", 1), ("ffn0", 8), ("hid0", 22), ("ple0", 8),
                  ("mix1", 8), ("p1", 1), ("ffn1", 8), ("hid1", 22), ("ple1", 8)):
    TQ[_name] = _n
    _n += _k
POW = ["mix0", "cqkv", "gla", "post0", "ffn0", "fpost0", "mix1", "post1", "ffn1", "fpost1"]
POW_W = {"mix0": 2, "cqkv": 4, "gla": 16}


def ffn_base(layer, g):
    return FFNS[layer] + sum(2 * n + 4 for n in GROUPS[:g])


MLA_STEPS = 4
NSA_STEPS = 16
MLA_AT = {(UKV + 2, 1): 0, (UKV + 2, 3): 1, (UKV + 3, 1): 2, (UKV + 3, 3): 3, (UKV + 4, 1): 4, (UKV + 4, 3): 5}


def nsa_plan():
    plan, t = {}, 0
    for g in range(3):
        for j in range(4):
            ops = [("qt", g)] if j == 1 else [("cs", g)] if j == 2 else []
            if (g, j) >= (0, 3):
                ops.append(("st", t))
                t += 1
            plan[(SQ + 1 + g, j)] = ops
    plan[(SQ + 3, 3)] += [("st", t)]
    plan[(OUT1, 0)] = [("qt", 3), ("st", t + 1)]
    plan[(OUT1, 1)] = [("cs", 3), ("st", t + 2)]
    for k, gap in enumerate(((OUT1, 2), (OUT1, 3), (OUT1, 3), (OUT1 + 1, 0), (OUT1 + 1, 1), (OUT1 + 1, 1))):
        plan.setdefault(gap, []).append(("st", t + 3 + k))
    assert t + 3 + k == NSA_STEPS + 1
    return plan


NSA_AT = nsa_plan()
PP_AT = {(OUT0, 2): 0, (OUT1 + 1, 2): 1}
OUT_UNITS = ((0, 0), (0, 1), (1, 0), (1, 1), (0, 2), (1, 2), (0, 3), (1, 3))
CP_STEP = {0: 0, 4: 1, 8: 2, 12: 3}

GLA_AT = {(GG, 1): 0, (GG, 2): 1, (GG, 3): 2, (GG + 1, 0): 3, (GG + 1, 1): 4, (GG + 1, 2): 5}
KT_AT = {(SKC + 1, 1): 0, (SVC + 1, 1): 1, (SKS + 1, 1): 2, (SKW + 1, 1): 3}


def units(s):
    return 1 if UQN <= s < KG or any(p <= s < p + 4 for p in PROJ) else 4


BASE = [0]
for _s in range(NSLOTS):
    BASE.append(BASE[-1] + units(_s))


def staged(prompt):
    plan = {}
    for slots in (range(QG, OUT0 + 1), range(L1, OUT1 + 2)):
        run = [(s, j) for s in slots for j in range(units(s))]
        for x, gap in enumerate(run):
            at = x + (1 if gap[0] in prompt else 2)
            plan.setdefault(run[at] if at < len(run) else (slots[-1], 4), []).append(gap)
    return plan


STAGED_ACT = staged((QG, GG, GG + 1, OUT0))
STAGED_DVE = staged((QG, GG, GG + 1, OUT0) + tuple(range(SQ + 1, OUT1 + 2)))


def evac_stage(s):
    return None if s in (0, L1, OUT1 + 1) else 0 if QG < s <= KG else 1


class Ring:

    def __init__(self):
        self.less = 0

    def loop(self, s):
        self.less = 4 * s - BASE[s]

    def __call__(self, s):
        return BASE[s] if isinstance(s, int) else s * 4 - self.less

    def end(self, s):
        return BASE[s + 1] if isinstance(s, int) else s * 4 + (4 - self.less)

    def place(self, s, j):
        return (BASE[s] + j if isinstance(s, int) else j - self.less) % 4

    def landed(self, s, j):
        if isinstance(s, int):
            return 16 * ((BASE[s] + j) // 4 + 1)
        return s * 16 + 4 * (j - self.less - self.place(s, j)) + 16


class Steps:

    def __init__(self, eng, sem):
        self.eng, self.sem, self.n, self.i, self.per, self.base = eng, sem, 0, None, 0, 0

    def __call__(self, ins):
        ins.then_inc(self.sem, 1)
        self.n += 1
        self.eng.wait_ge(self.sem, self.n if self.i is None else self.n + self.i * self.per)

    def enter(self, i, per):
        self.i, self.per, self.base = i, per, self.n

    def leave(self, times):
        assert self.n - self.base == self.per, (self.n - self.base, self.per)
        self.n = self.base + self.per * times
        self.i = None


def build(nc, T):
    def rows(a):
        return a.rearrange("(c p) n -> p c n", p=P)

    ab_in, ab_out = rows(T["ab_w_in"][0]), rows(T["ab_w_out"][0])
    uq, ukv = rows(T["mla_w_uq"][0]), rows(T["mla_w_ukv"][0])
    nsa_in, nsa_out = rows(T["nsa_w_in"][0]), rows(T["nsa_w_out"][0])
    wg, wu, wd, plg, plp = ([rows(T[n][i]) for i in range(2)] for n in (
        "ffn_w_gate", "ffn_w_up", "ffn_w_down", "ple_w_gate", "ple_w_proj"))
    w1_d = T["nsa_cmp_w1"]
    tok = lambda a: a.rearrange("(m p) d -> p m d", p=P)
    x_d, out_d = tok(T["x"][0]), tok(T["out"][0])
    p_d = [tok(T["p"][i, 0]) for i in range(2)]

    ctx = ExitStack()
    with ctx:
        at = [(nc.sbuf_base + 63) // 64 * 64]

        def sb(name, shape, dt=F32):
            n = int(np.prod(shape[1:])) * 4
            t = nc.alloc_sbuf_tensor_at(name, shape, dt, offset=at[0])
            at[0] += (n + 31) // 32 * 32
            return t

        def sem(name):
            return ctx.enter_context(nc.semaphore(name))

        h = sb("h", [P, NT, D])
        XAh, XAl = sb("XAh", [P, KC, SEQ], F32R), sb("XAl", [P, KC, SEQ], F32R)
        xb0 = at[0]
        XBh, XBl = sb("XBh", [P, KC, SEQ], F32R), sb("XBl", [P, KC, SEQ], F32R)
        BL = nc.alloc_sbuf_tensor_at("BL", [P, 2, CMP_LEN, 2, 60], F32R, offset=xb0)
        raw = sb("raw", [P, 4, 2048])
        whl = sb("whl", [P, 2, 2, 2048], F32R)
        wh, wl = whl[:, 0, :, :], whl[:, 1, :, :]
        ident = sb("ident", [P, P])
        cmask = sb("cmask", [P, 3, P])
        lt = sb("lt", [P, P])
        gt = sb("gt", [P, P])
        endm = sb("endm", [P, P])
        cosT, sinT = sb("cosT", [P, NT, 64]), sb("sinT", [P, NT, 64])
        vcol = sb("vcol", [P, 72])
        posT = sb("posT", [P, 64])
        okm, negm = sb("okm", [P, NT, 16]), sb("negm", [P, NT, 16])
        ss = sb("ss", [P, NT, 4])
        pwi, pwo, mhalf = sb("pwi", [P, 16]), sb("pwo", [P, 16]), sb("mhalf", [P, 16])
        sm = sb("sm", [P, 12])
        rt = sb("rt", [P, 2, 512])
        gnw = sb("gnw", [P, P])
        AL, aw = sb("AL", [17, SEQ]), sb("aw", [17, 512])
        krd = sb("krd", [P, NT, 2, 64])
        KrT = sb("KrT", [P, SEQ])
        decs = sb("decs", [P, 4, 4])
        w2s = sb("w2s", [P, 2, P])
        GE = sb("GE", [P, 2, 4, 32])
        KcT = sb("KcT", [P, 4, 32])
        gbias, gates = sb("gbias", [P, W_GT]), sb("gates", [P, NT, W_GT])
        csc, Pc = sb("csc", [P, NT, 4, 16]), sb("Pc", [P, NT, 4, 32])
        cst = sb("cst", [P, 3, 8])
        PcT = sb("PcT", [P, 2, SEQ])

        ZS = 58112
        z0 = at[0]
        assert z0 + ZS <= nc.sbuf_usable_end, (z0 + ZS, nc.sbuf_usable_end)

        def zt(name, off, shape, dt=F32):
            assert off + int(np.prod(shape[1:])) * 4 <= ZS, name
            return nc.alloc_sbuf_tensor_at(name, shape, dt, offset=z0 + off)

        vin, vin2 = zt("vin", 16384, [72, P]), zt("vin2", 16896, [64, P])
        invb, posi, posf = zt("invb", 17408, [P, 64]), zt("posi", 17664, [P, NT], I32), zt("posf", 17696, [P, NT])
        ang, kk = zt("ang", 17728, [P, NT, 64]), zt("kk", 18240, [P, NT, 64])
        qg, kg = zt("qg", 0, [P, NT, 512]), zt("kg", 4096, [P, NT, 512])
        vg, gg = zt("vg", 8192, [P, NT, 1024]), zt("gg", 16384, [P, NT, 1024])
        SP0, PT0 = zt("SP0", 16384, [P, 2, 384]), zt("PT0", 19456, [P, 2, 384])
        QnT, KnT = zt("QnT", 24576, [P, 8, SEQ]), zt("KnT", 32768, [P, 8, SEQ])
        Vm, zc = zt("Vm", 40960, [P, NT, 1024]), zt("zc", 40960, [P, NT, 1104])
        qr, QrT = zt("qr", 49792, [P, NT, 512]), zt("QrT", 53888, [P, 4, SEQ])
        loga, kinv, E1 = zt("loga", 24576, [P, NT, 512]), zt("kinv", 28672, [P, NT, 512]), zt("E1", 32768, [P, NT, 512])
        qdT, kiT = zt("qdT", 36864, [P, 4, SEQ]), zt("kiT", 40960, [P, 4, SEQ])
        SS, oT = zt("SS", 45056, [P, 4, 3, P]), zt("oT", 51200, [P, 512])
        AT = [zt("ATa", 24576, [P, 2, 512]), zt("ATb", 32768, [P, 2, 512])]
        zq, KB = zt("zq", 0, [P, 2, NT, 512]), zt("KB", 8192, [P, 2, NT, 512])
        PT1 = zt("PT1", 11264, [P, 2, 384])
        SP1 = [zt("SP1a", 8192, [P, 2, 384]), zt("SP1b", 40960, [P, 2, 384])]
        vs, vw = zt("vs", 16384, [P, NT, 512]), zt("vw", 20480, [P, NT, 512])
        kcT, vcT = zt("kcT", 24576, [P, 4, SEQ]), zt("vcT", 28672, [P, 4, SEQ])
        ksT, kwT = zt("ksT", 32768, [P, 4, SEQ]), zt("kwT", 36864, [P, 4, SEQ])
        BT = zt("BT", 40960, [P, CMP_LEN, 60])
        VB = zt("VB", 24576, [P, 4, 4, P])
        QT = zt("QT", 48640, [P, 2, 4, SEQ])
        GX, GU = zt("GX", 48640, [60, 2, P]), zt("GU", 49664, [60, 2, P])
        Fm, PJ = zt("Fm", 0, [P, NT, D]), zt("PJ", 16384, [P, NT, D])
        Eb, Hb = zt("Eb", 32768, [P, NT, 512]), zt("Hb", 36864, [P, NT, 512])
        wbc, pp = zt("wbc", 40960, [P, D]), zt("pp", 49152, [P, NT, PLE])
        PXh, PXl = zt("PXh", 51200, [P, 2, SEQ], F32R), zt("PXl", 53248, [P, 2, SEQ], F32R)
        XA, XB, PX = (XAh, XAl), (XBh, XBl), (PXh, PXl)

        PG = ctx.enter_context(nc.psum_tensor("PG", [P, 2, NT, 512], F32))
        MB = ctx.enter_context(nc.psum_tensor("MB", [P, 4, 512], F32))

        raw_in = [sem(f"raw_in{j}") for j in range(4)]
        x_in, start_in, const_in = sem("x_in"), sem("start_in"), sem("const_in")
        pp_in, wbc_in, out_st = sem("pp_in"), sem("wbc_in"), sem("out_st")
        hi_ready, lo_ready = sem("hi_ready"), sem("lo_ready")
        unit_done = sem("unit_done")
        evac_a, evac_v = sem("evac_a"), sem("evac_v")
        tx_ps, tx_hi, tx_lo = sem("tx_ps"), sem("tx_hi"), sem("tx_lo")
        pw_req, pw_done = sem("pw_req"), sem("pw_done")
        const_mk = sem("const_mk")
        act_step, dve_step, pool_step, pe_step = (sem(n) for n in ("act_step", "dve_step", "pool_step", "pe_step"))
        vt_ps, vt_sb = sem("vt_ps"), sem("vt_sb")
        ang_ok, trig_ok = sem("ang_ok"), sem("trig_ok")
        sq_done = sem("sq_done")
        mul_done = sem("mul_done")
        add_done = sem("add_done")
        upd, ssq = sem("upd"), sem("ssq")
        hn_a, hn_v = sem("hn_a"), sem("hn_v")
        h_ok = sem("h_ok")
        zn_ok, kr_ok, qr_ok = sem("zn_ok"), sem("kr_ok"), sem("qr_ok")
        al_ps, al_sb = sem("al_ps"), sem("al_sb")
        qrt_ps, qrt_sb = sem("qrt_ps"), sem("qrt_sb")
        s_done, pt_done, pv_done = sem("s_done"), sem("pt_done"), sem("pv_done")
        mx_ok, exp_ok, o_hi = sem("mx_ok"), sem("exp_ok"), sem("o_hi")
        pt_sb = sem("pt_sb")
        att_v, p_ok, head_ok = sem("att_v"), sem("p_ok"), sem("head_ok")
        ga_ps, ga_t, ga_n, ga_l, ga_ok = (sem(n) for n in ("ga_ps", "ga_t", "ga_n", "ga_l", "ga_ok"))
        gb_ps, ge_a, ge_v = sem("gb_ps"), sem("ge_a"), sem("ge_v")
        gt_ps, gt_sb, gu_ps, gd_sb, gs_ok = (sem(n) for n in ("gt_ps", "gt_sb", "gu_ps", "gd_sb", "gs_ok"))
        at_zero, at_ps, at_ok, go_ps, go_sq, go_ok = (sem(n) for n in (
            "at_zero", "at_ps", "at_ok", "go_ps", "go_sq", "go_ok"))
        ke_ok, kt_ps, kt_sb = sem("ke_ok"), sem("kt_ps"), sem("kt_sb")
        bt_ok, bh_ok, bl_ok = sem("bt_ok"), sem("bh_ok"), sem("bl_ok")
        ge_x, ge_e, ge_ok = sem("ge_x"), sem("ge_e"), sem("ge_ok")
        gl_ps, gl_ok = sem("gl_ps"), sem("gl_ok")
        c2_ps, c2_a, c2_v, vb_zero = sem("c2_ps"), sem("c2_a"), sem("c2_v"), sem("vb_zero")
        gx_e = sem("gx_e")
        qe_ok, qt_ps, qt_sb = sem("qe_ok"), sem("qt_ps"), sem("qt_sb")
        cs_ps, cs_in, cs_e, cs_ok, cp_ps, pct_sb = (sem(n) for n in (
            "cs_ps", "cs_in", "cs_e", "cs_ok", "cp_ps", "pct_sb"))

        N_START, N_CONST = 10, 6
        COPY0 = {QG: (qg, 0), KG: (kg, 0), UKV: (Vm, 0), UKV + 1: (Vm, 512), VG: (vg, 0), VG + 1: (vg, 512),
                 SVS: (vs, 0), SVW: (vw, 0)}
        block = ctx.enter_context(nc.Block())

        def shape_of(s):
            return 4, 512 if not isinstance(s, int) else W_ZC if s <= ZC2 else W_VG if s in (SVW, SGT) else 512

        def width(s):
            return shape_of(s)[0] * shape_of(s)[1]

        @block.sync
        def _(sp):
            sp.dma_start(h[:, 0, :], x_d[:, 0, :]).then_inc(x_in, 16)
            sp.dma_start(h[:, 1, :], x_d[:, 1, :]).then_inc(x_in, 16)
            consts = [(vin[0:16, :], T["ln_mix_pre"][0].rearrange("(c k) -> c k", k=P)),
                      (vin[16:32, :], T["ln_ffn_pre"][0].rearrange("(c k) -> c k", k=P)),
                      (vin[32:48, :], T["ln_mix_pre"][1].rearrange("(c k) -> c k", k=P)),
                      (vin[48:64, :], T["ln_ffn_pre"][1].rearrange("(c k) -> c k", k=P)),
                      (vin[64:68, :], T["mla_q_norm_w"][0].rearrange("(c k) -> c k", k=P)),
                      (vin[68:72, :], T["mla_kv_norm_w"][0].rearrange("(c k) -> c k", k=P)),
                      (vin2[0:32, :], T["nsa_cmp_pos"][0, 0]),
                      (vin2[32:64, :], T["nsa_cmp_pos"][0, 1]),
                      (posi[:, :], T["positions"].rearrange("a (m p) -> p (a m)", p=P)),
                      (invb[:, :], T["rope_inv"][0:1, :].broadcast_to([P, 64]))]
            late = [(gnw[:, :], T["gla_norm_w"][0:1, :].broadcast_to([P, P])),
                    (aw[0:16, :], T["gla_w_alpha_up"][0]),
                    (aw[16:17, :], T["gla_b_alpha"][0:1, :]),
                    (w2s[:, 0, :], T["nsa_cmp_w2"][0, 0]),
                    (w2s[:, 1, :], T["nsa_cmp_w2"][0, 1]),
                    (gbias[:, :], T["nsa_b_gate"][0:1, :].broadcast_to([P, W_GT]))]
            assert (len(consts), len(late)) == (N_START, N_CONST)
            for dst, src in consts:
                sp.dma_start(dst, src, allow_slow_non_contiguous=True).then_inc(start_in, 16)

            U = Ring()

            def unit(s, j, src, kc, ncol):
                if not (isinstance(s, int) and U(s) + j < 4):
                    sp.wait_ge(lo_ready, U(s) + (j - 3))
                place = U.place(s, j)
                dst = raw[:, place, 0:kc * ncol].rearrange("p (c n) -> p c n", c=kc)
                sp.dma_start(dst, src).then_inc(raw_in[place], 16)

            def k_units(s, w, col, ncol=512, kc=4, c0=0, wrap=KC):
                for j in range(4):
                    c = (c0 + j * kc) % wrap
                    unit(s, j, w[:, c:c + kc, bass.ds(col, ncol)], kc, ncol)

            for n, s in enumerate((ZC0, ZC1, ZC2)):
                k_units(s, ab_in, 3072 + W_ZC * n, W_ZC)
                if n == 0:
                    for dst, src in late:
                        sp.dma_start(dst, src).then_inc(const_in, 16)
            k_units(QG, ab_in, 0)
            for n in range(7):
                src = uq[:, :, 512 * n:512 * n + 512] if n < 3 else ukv[:, :, 512 * (n - 3):512 * (n - 3) + 512]
                unit(UQN + n, 0, src, 4, 512)
            for n in range(5):
                k_units(KG + n, ab_in, 512 * (n + 1))
            for layer in range(2):
                if layer == 0:
                    for n in range(4):
                        k_units(OUTS[0] + n, ab_out, 512 * n, c0=8)
                else:
                    for n, (panel, part) in enumerate(OUT_UNITS):
                        unit(OUT1 + n // 4, n % 4,
                             nsa_out[:, 4 * part:4 * part + 4, 512 * panel:512 * panel + 512], 4, 512)
                    U.loop(OUT1)
                    with sp.Fori(0, 2) as i:
                        k_units(i + (OUT1 + 2), nsa_out, i * 512 + 1024)
                for i in range(4):
                    unit(PROJ[layer] + i, 0, plp[layer][:, 0:2, 512 * i:512 * i + 512], 2, 512)
                U.loop(FFNS[layer])
                for g, n in enumerate(GROUPS):
                    b, p0 = ffn_base(layer, g), sum(GROUPS[:g])
                    with sp.Fori(0, n) as i:
                        k_units(i * 2 + b, wg[layer], i * 512 + 512 * p0)
                        k_units(i * 2 + (b + 1), wu[layer], i * 512 + 512 * p0)
                    with sp.Fori(0, 4) as i:
                        k_units(i + (b + 2 * n), wd[layer], i * 512, kc=n, c0=4 * p0, wrap=FFN)
                with sp.Fori(0, 4) as i:
                    k_units(i + GATE[layer], plg[layer], i * 512)
                if layer == 0:
                    kv = {SKC: 0, SVC: 1, SKS: 2, SVS: 3, SKW: 4, SVW: 5}
                    for s in range(L1, SQ):
                        if s == SW1:
                            for j in range(4):
                                unit(s, j, w1_d[j // 2, :, 16 * (j % 2):16 * (j % 2) + 16, :], 16, P)
                        elif s == SGT:
                            k_units(s, nsa_in, 4608 + W_VG, W_VG)
                        else:
                            k_units(s, nsa_in, 2048 + 512 * kv[s], shape_of(s)[1])
                    U.loop(SQ)
                    with sp.Fori(0, 4) as i:
                        k_units(i + SQ, nsa_in, i * 512)
            for i in range(4):
                sp.wait_ge(h_ok, 5 + i)
                sp.dma_start(out_d[:, :, 512 * i:512 * i + 512], h[:, :, 512 * i:512 * i + 512]).then_inc(out_st, 16)
            sp.wait_ge(out_st, 64)

        @block.gpsimd
        def _(pool):
            step = Steps(pool, pool_step)

            def select(t, pattern, base, cm, op=ALU.is_ge, fill=0.0):
                step(pool.affine_select(out=t, in_=t, compare_op=op, fill=fill, base=base,
                                        pattern=pattern, channel_multiplier=cm))

            step(pool.memset(ident[:, :], 0.0))
            select(ident[:, :], [[-1, P]], 0, 1, ALU.not_equal, 1.0)
            step(pool.memset(mhalf[:, :], -0.5))
            step(pool.memset(cmask[:, :, :], 0.0))
            select(cmask[:, 0, :], [[-1, P]], 0, 1, fill=NEG)
            select(cmask[:, 2, :], [[-1, P]], 0, 1, fill=NEG)
            step(pool.memset(endm[:, :], 1.0 / TAU))
            select(endm[:, 0:64], [[0, 64]], 63, -1)
            select(endm[:, 64:P], [[0, 64]], -64, 1)
            step(pool.tensor_copy(lt[:, :], endm[:, :]))
            step(pool.tensor_copy(gt[:, :], endm[:, :]))
            select(lt[:, :], [[1, P]], 0, -1)
            select(gt[:, :], [[-1, P]], -1, 1)
            step(pool.memset(okm[:, :, :], 1.0))
            step(pool.memset(negm[:, :, :], 0.0))
            select(okm[:, :, :], [[P, NT], [-CMP_STRIDE, 16]], 1 - CMP_LEN, 1)
            select(negm[:, :, :], [[P, NT], [-CMP_STRIDE, 16]], 1 - CMP_LEN, 1, fill=NEG)
            step(pool.memset(AL[:, :], 1.0))
            step(pool.memset(GE[:, :, :, :], 0.0))
            step(pool.memset(Pc[:, :, :, :], 0.0))
            pool.memset(sm[:, :], 0.0).then_inc(const_mk, 1)
            for k, name in enumerate(POW):
                w = POW_W.get(name, 2)
                pool.wait_ge(pw_req, k + 1)
                pool.tensor_tensor(pwo[:, 0:w], pwi[:, 0:w], mhalf[:, 0:w], ALU.pow).then_inc(pw_done, 1)
                if name == "cqkv":
                    pool.wait_ge(gu_ps, 1)
                    pool.wait_ge(ge_v, 1)
                    pool.memset(AT[0][:, :, :], 0.0)
                    pool.memset(AT[1][:, :, :], 0.0).then_inc(at_zero, 1)
                if name == "mix1":
                    pool.wait_ge(bt_ok, 2)
                    pool.memset(VB[:, :, :, :], 0.0).then_inc(vb_zero, 1)

        @block.tensor
        def _(pe):
            mm = nc.tensor.matmul
            pstep = Steps(pe, pe_step)
            U = Ring()

            def transpose_in(src, n, q, banks=2):
                for b in range(n):
                    pe.wait_ge(tx_lo, q + (b - 1 if banks == 2 else 0))
                    k = b % banks
                    for c in range(2):
                        for m in range(NT):
                            o = c * SEQ + m * P
                            t = nc.tensor.transpose(MB[:, k, o:o + P], src(2 * b + c, m), ident[:, :])
                    t.then_inc(tx_ps, 1)

            def unit(s, j, X, kc=4, ncol=512, need=None, par=None, pos=None, banks=None):
                pe.wait_ge(hi_ready, U(s) + (j + 1))
                pe.wait_ge(lo_ready, U(s) + (j + 1))
                if need is not None:
                    pe.wait_ge(tx_lo, need)
                par = s % 2 if par is None else par
                pos = j if pos is None else pos
                bank = (lambda m: PG[:, par, m, 0:ncol]) if banks is None else banks
                k = U.place(s, j) % 2
                for c in range(kc):
                    chunk = max(pos, 0) * kc + c
                    hh, ll = (w[:, k, c * ncol:(c + 1) * ncol] for w in (wh, wl))
                    for m in range(NT):
                        o = bank(m)
                        xh, xl = (x[:, chunk, m * P:(m + 1) * P] for x in X)
                        beg = c == 0 and pos in (0, -1)
                        end = c == kc - 1 and pos in (3, -1)
                        mm(o, xh, hh, start=beg, stop=False)
                        mm(o, xh, ll, start=False, stop=False)
                        last = mm(o, xl, hh, start=False, stop=end)
                last.then_inc(unit_done, 1)

            def unit_t(s, X, x0):
                pe.wait_ge(hi_ready, U(s) + 1)
                pe.wait_ge(lo_ready, U(s) + 1)
                k = U.place(s, 0) % 2
                for c in range(4):
                    for f in range(4):
                        o = PG[:, s % 2, f // 2, (f % 2) * SEQ:(f % 2 + 1) * SEQ]
                        hh, ll = (w[:, k, c * 512 + f * P:c * 512 + (f + 1) * P] for w in (wh, wl))
                        xh, xl = (x[:, x0 + c, :] for x in X)
                        mm(o, hh, xh, start=(c == 0 and f % 2 == 0), stop=False, skip_group_check=True)
                        mm(o, hh, xl, start=False, stop=False, skip_group_check=True)
                        last = mm(o, ll, xh, start=False, stop=(c == 3), skip_group_check=True)
                last.then_inc(unit_done, 1)

            def banks_free(s):
                if isinstance(s, int) and s < 2:
                    return
                pe.wait_ge(evac_a, s - 1)
                pe.wait_ge(evac_v, s - 1)

            def mla_step(t):
                if t:
                    pe.wait_ge(att_v, t)
                if t > 1:
                    pe.wait_ge(pt_sb, min(t - 1, MLA_STEPS))
                if 2 <= t:
                    for b in range(2):
                        hd = 2 * (t - 2) + b
                        for m in range(NT):
                            for kt in range(m + 1):
                                p0 = (m + kt) * P
                                last = mm(MB[:, 2 * b + m, 384:512], Vm[:, kt, hd * P:(hd + 1) * P],
                                          PT0[:, b, p0:p0 + P], start=(kt == 0), stop=(kt == m))
                    last.then_inc(pv_done, 1)
                if 1 <= t <= MLA_STEPS:
                    for b in range(2):
                        for k in range(3):
                            last = nc.tensor.transpose(MB[:, 2 + b, k * P:(k + 1) * P],
                                                       SP0[:, b, k * P:(k + 1) * P], ident[:, :])
                    last.then_inc(pt_done, 1)
                if t < MLA_STEPS:
                    for b in range(2):
                        hd, r = 2 * t + b, slice(64 * b, 64 * b + 64)
                        for m in range(NT):
                            o = MB[:, b, m * P:m * P + (m + 1) * P]
                            mm(o, QnT[:, hd, m * P:(m + 1) * P], KnT[:, hd, 0:(m + 1) * P],
                               start=True, stop=False)
                            last = mm(o, QrT[r, t, m * P:(m + 1) * P], KrT[r, 0:(m + 1) * P],
                                      start=False, stop=True)
                    last.then_inc(s_done, 1)

            def nsa_step(t):
                if t == 0:
                    pe.wait_ge(kt_sb, 4)
                if 2 <= t:
                    g, j = (t - 2) // 4, (t - 2) % 4
                    pe.wait_ge(pt_sb, MLA_STEPS + t - 1)
                    pe.wait_ge(pct_sb, g + 1)
                    for m in range(NT):
                        o = MB[:, 2, m * P:(m + 1) * P]
                        mm(o, VB[:, g, j, :], PcT[:, g % 2, m * P:(m + 1) * P], start=True, stop=False)
                        for b, v in enumerate((vs, vw)):
                            for kt in range(m + 1):
                                p0 = (m + kt) * P
                                last = mm(o, v[:, kt, g * P:(g + 1) * P], PT1[:, b, p0:p0 + P],
                                          start=False, stop=(b == 1 and kt == m))
                    last.then_inc(pv_done, 1)
                if t in CP_STEP:
                    pe.wait_ge(cs_ok, CP_STEP[t] + 1)
                    for m in range(NT):
                        last = nc.tensor.transpose(MB[:, 3, m * P:(m + 1) * P],
                                                   Pc[:, m, :, :].rearrange("p j n -> p (j n)"), ident[:, :])
                    last.then_inc(cp_ps, 1)
                if t < NSA_STEPS:
                    g, j = t // 4, t % 4
                    if t:
                        pe.wait_ge(mx_ok, MLA_STEPS + t)
                    else:
                        pe.wait_ge(c2_v, 1)
                        pe.wait_ge(c2_a, 1)
                    for b in range(2):
                        for m in range(NT):
                            last = mm(MB[:, b, m * P:m * P + (m + 1) * P], QT[:, g % 2, j, m * P:(m + 1) * P],
                                      (ksT, kwT)[b][:, g, 0:(m + 1) * P], start=True, stop=True)
                    last.then_inc(s_done, 1)
                if 1 <= t <= NSA_STEPS:
                    pe.wait_ge(p_ok, t)
                    if t > 1:
                        pe.wait_ge(head_ok, t - 1)
                    pe.wait_ge(pct_sb, sum(c <= t for c in CP_STEP))
                    for b in range(2):
                        for k in range(3):
                            last = nc.tensor.transpose(MB[:, 2 + b, k * P:(k + 1) * P],
                                                       SP1[(t - 1) % 2][:, b, k * P:(k + 1) * P], ident[:, :])
                    last.then_inc(pt_done, 1)

            def four_heads(banks, src):
                for c in range(4):
                    for m in range(NT):
                        o = (c % 2) * SEQ + m * P
                        t = nc.tensor.transpose(banks(c // 2)[:, o:o + P], src(c, m), ident[:, :])
                return t

            def pair_of(hd):
                return hd // 2, slice(64 * (hd % 2), 64 * (hd % 2) + 64)

            def gla_gap(k):
                if k == 0:
                    pe.wait_ge(const_in, 16 * N_CONST)
                    for m in range(NT):
                        last = mm(MB[:, 2 + m, :], AL[0:17, m * P:(m + 1) * P], aw[0:17, :], start=True, stop=True)
                    last.then_inc(ga_ps, 1)
                if k == 1:
                    pe.wait_ge(ga_ok, 1)
                    for m in range(NT):
                        mm(MB[:, m, :], lt[:, :], loga[:, m, :], start=True, stop=True)
                        last = mm(MB[:, 2 + m, :], gt[:, :], loga[:, m, :], start=True, stop=True)
                    last.then_inc(gb_ps, 1)
                if k == 2:
                    pe.wait_ge(ge_v, 1)
                    four_heads(lambda b: MB[:, b, :], lambda c, m: qg[:, m, c * P:(c + 1) * P])
                    four_heads(lambda b: MB[:, 2 + b, :], lambda c, m: kinv[:, m, c * P:(c + 1) * P]).then_inc(gt_ps, 1)
                if k == 3:
                    pe.wait_ge(gt_sb, 1)
                    for c in (0, 2, 1):
                        r = slice(64 * (c % 2), 64 * (c % 2) + 64)
                        if c == 1:
                            pstep(last)
                        for hd in range(8):
                            pr, rr = pair_of(hd)
                            last = mm(MB[rr, pr, c * P:(c + 1) * P], kg[r, c // 2, hd * 64:(hd + 1) * 64],
                               vg[r, c // 2, hd * P:(hd + 1) * P], start=True, stop=True)
                    for pr in range(4):
                        for m in range(NT):
                            o = 384 + 4 * pr + 2 * m
                            last = mm(MB[:, 0, o:o + 2], loga[:, m, pr * P:(pr + 1) * P], endm[:, 0:P:64],
                                      start=True, stop=True)
                    last.then_inc(gu_ps, 1)
                if k == 4:
                    pe.wait_ge(gs_ok, 1)
                    for odd in range(2):
                        if odd:
                            pstep(last)
                        for m in range(NT):
                            for hd in range(odd, 8, 2):
                                pr, rr = pair_of(hd)
                                last = mm(MB[:, 2 * m + hd // 4, (hd % 4) * P:(hd % 4 + 1) * P],
                                          kiT[rr, pr, m * P:(m + 1) * P], qdT[rr, pr, m * P:(m + 1) * P],
                                          start=True, stop=True)
                    last.then_inc(at_ps, 1)
                if k == 5:
                    pe.wait_ge(at_ok, 1)
                    for m in range(NT):
                        for hd in range(8):
                            e = hd % 4
                            mm(MB[:, 2 * m + hd // 4, e * P:(e + 1) * P], AT[m][:, hd // 4, e * P:(e + 1) * P],
                               vg[:, m, hd * P:(hd + 1) * P], start=(e == 0), stop=False, skip_group_check=True)
                    for odd in range(2):
                        if odd:
                            pstep(last)
                        for hd in range(odd, 8, 2):
                            pr, rr = pair_of(hd)
                            e = hd % 4
                            for c in range(1, 4):
                                q = slice(64 * (c % 2), 64 * (c % 2) + 64)
                                last = mm(MB[q, 2 * (c // 2) + hd // 4, e * P:(e + 1) * P],
                                          qdT[rr, pr, c * 64:(c + 1) * 64], SS[rr, pr, c - 1, :],
                                          start=False, stop=True, skip_group_check=True)
                    last.then_inc(go_ps, 1)

            def nsa_op(op, g):
                ob = (SQ + 2 + g) % 2
                if op == "qt":
                    pe.wait_ge(qe_ok, g + 1)
                    four_heads(lambda b: PG[:, ob, b, :],
                               lambda c, m: zq[:, g % 2, m, c * P:(c + 1) * P]).then_inc(qt_ps, 1)
                if op == "cs":
                    pe.wait_ge(qt_sb, g + 1)
                    pe.wait_ge(c2_a, 1)
                    for m in range(NT):
                        for j in range(4):
                            o = m * 64 + j * 16
                            last = mm(PG[:, ob, 0, o:o + 16], QT[:, g % 2, j, m * P:(m + 1) * P],
                                      KcT[:, g, 0:16], start=True, stop=True)
                    last.then_inc(cs_ps, 1)
                if op == "st":
                    nsa_step(g)

            def gap(s, j):
                if (s, j) == (QG, 2):
                    pe.wait_ge(zn_ok, 1)
                    transpose_in(lambda c, m: zc[:, m, 16 + c * P:16 + (c + 1) * P], 4, TQ["cqkv"])
                    for m in range(NT):
                        last = nc.tensor.transpose(MB[0:16, 2, m * P:(m + 1) * P], zc[:, m, 0:16], ident[:, :])
                    last.then_inc(al_ps, 1)
                if (s, j) == (UQR + 2, 0):
                    pe.wait_ge(qr_ok, 1)
                    pe.wait_ge(kr_ok, 1)
                    pe.wait_ge(al_sb, 1)
                    pe.wait_ge(tx_lo, TQ["gla"])
                    four_heads(lambda b: MB[:, 2 + b, :], lambda c, m: qr[:, m, c * P:(c + 1) * P])
                    for m in range(NT):
                        last = nc.tensor.transpose(MB[:, 1, m * P:(m + 1) * P],
                                                   krd[:, m, :, :].rearrange("p a e -> p (a e)"), ident[:, :])
                    last.then_inc(qrt_ps, 1)
                if (s, j) in MLA_AT:
                    t = MLA_AT[(s, j)]
                    if t == 0:
                        pe.wait_ge(qrt_sb, 1)
                        pe.wait_ge(evac_a, UKK + 2)
                        pe.wait_ge(evac_v, UKK + 2)
                    if t == 2:
                        pe.wait_ge(evac_a, UKV + 2)
                        pe.wait_ge(evac_v, UKV + 2)
                    mla_step(t)
                if (s, j) in GLA_AT:
                    if GLA_AT[(s, j)] == 0:
                        pe.wait_ge(att_v, MLA_STEPS + 2)
                    gla_gap(GLA_AT[(s, j)])
                if (s, j) == (OUT0, 1):
                    pe.wait_ge(go_ok, 1)
                    transpose_in(lambda c, m: gg[:, m, c * P:(c + 1) * P], 4, TQ["gla"], 4)
                if (s, j) in PP_AT:
                    layer = PP_AT[(s, j)]
                    pe.wait_ge(pp_in, 16 * layer + 16)
                    transpose_in(lambda c, m: pp[:, m, c * P:(c + 1) * P], 1, TQ[f"p{layer}"])
                if (s, j) in KT_AT:
                    k = KT_AT[(s, j)]
                    pe.wait_ge(ke_ok, k + 1)
                    if k == 1:
                        pe.wait_ge(evac_a, SVC + 1)
                    if k:
                        pe.wait_ge(kt_sb, k)
                    four_heads(lambda b: MB[:, 2 + b, :], lambda c, m: KB[:, k % 2, m, c * P:(c + 1) * P])\
                        .then_inc(kt_ps, 1)
                if (s, j) == (SW1 + 1, 2):
                    pe.wait_ge(ge_ok, 1)
                    pe.wait_ge(tx_lo, TQ["p1"])
                    for kv in range(2):
                        last = nc.tensor.transpose(MB[:, 0, 64 * kv:64 * kv + 60], GU[:, kv, :], ident[0:60, 0:60])
                    last.then_inc(gl_ps, 1)
                if (s, j) == (SW1 + 2, 2):
                    pe.wait_ge(gl_ok, 1)
                    mm(MB[:, 0, 0:P], w2s[:, 0, :], GE[:, 0, :, :].rearrange("p g n -> p (g n)"), start=True, stop=True)
                    for g in range(4):
                        for jj in range(4):
                            last = mm(MB[32 * jj:32 * jj + 32, 1, g * P:(g + 1) * P], GE[:, 1, g, :], w2s[:, 1, :],
                                      start=True, stop=True)
                    last.then_inc(c2_ps, 1)
                for op, g in NSA_AT.get((s, j), ()):
                    nsa_op(op, g)

            def nsa_guard(s):
                g = s - (SQ + 2)
                if 0 <= g < 4:
                    pe.wait_ge(cs_in, g + 1)
                    pe.wait_ge(qt_sb, g + 1)

            pe.wait_ge(const_mk, 1)
            pe.wait_ge(start_in, 16 * N_START)
            nc.tensor.transpose(MB[:, 2, 0:72], vin[:, :], ident[0:72, 0:72])
            nc.tensor.transpose(MB[:, 2, P:P + 64], vin2[:, :], ident[0:64, 0:64]).then_inc(vt_ps, 1)

            def fresh_slot(s, src, q, ready, count):
                def transposed(b, m):
                    for c in range(2):
                        o, k = c * SEQ + m * P, (2 * b + c) * P
                        t = nc.tensor.transpose(MB[:, b % 4, o:o + P], src[:, m, k:k + P], ident[:, :])
                    return t

                if q:
                    pe.wait_ge(tx_lo, q)
                for m in range(NT):
                    pe.wait_ge(ready[m], count[m])
                    for b in range(4):
                        t = transposed(b, m)
                        if m == NT - 1:
                            t.then_inc(tx_ps, 1)
                banks_free(s)
                for j in range(4):
                    unit(s, j, XA, *shape_of(s), need=q + 2 * j + 2)
                    if j < 2:
                        for b in (4 + 2 * j, 5 + 2 * j):
                            pe.wait_ge(tx_lo, q + b - 3)
                            transposed(b, 0)
                            transposed(b, 1).then_inc(tx_ps, 1)

            def norm_slot(k, s, name):
                fresh_slot(s, Fm, TQ[name], (hn_a, hn_v), (k + 1, k + 1))

            pe.wait_ge(vt_sb, 2)
            norm_slot(0, 0, "mix0")
            for s in range(1, OUT0):
                banks_free(s)
                for j in range(units(s)):
                    if s in (UQN, UQN + 1):
                        unit_t(s, XB, 0)
                    elif s == UQR:
                        unit(s, j, XB, pos=-1)
                    elif s in (UKK, UKK + 1):
                        unit_t(s, XB, 4)
                    elif s in (UKV, UKV + 1):
                        unit(s, j, (XBh[:, 4:8, :], XBl[:, 4:8, :]), pos=-1)
                    else:
                        unit(s, j, XA, *shape_of(s))
                    if (s, j) == (QG, 3):
                        pe.wait_ge(tx_lo, TQ["gla"])
                    gap(s, j)

            for layer in range(2):
                s0 = OUTS[layer]
                if layer == 0:
                    banks_free(s0)
                    for j in range(4):
                        if j == 0:
                            pe.wait_ge(att_v, MLA_STEPS + 2)
                        if j >= 2:
                            pe.wait_ge(tx_lo, TQ["gla"] + 2 * j - 2)
                        unit(s0, j, XB)
                        gap(s0, j)
                else:
                    for n, (panel, part) in enumerate(OUT_UNITS):
                        if part == 0:
                            nsa_guard(OUT1 + panel)
                            banks_free(OUT1 + panel)
                        pe.wait_ge(head_ok, 4 * part + 4)
                        unit(OUT1 + n // 4, n % 4, XB, par=(OUT1 + panel) % 2, pos=part)
                        gap(OUT1 + n // 4, n % 4)
                U.loop(s0)
                with pe.Fori(0, 3 - layer) as i:
                    banks_free(i + (s0 + 1 + layer))
                    for j in range(4):
                        unit(i + (s0 + 1 + layer), j, XB, par=(i + (s0 + 1 + layer)) % 2)
                for i in range(4):
                    if i >= 2:
                        banks_free(PROJ[layer] + i - 2)
                    unit(PROJ[layer] + i, 0, PX, kc=2, need=TQ[f"ffn{layer}"], par=(PROJ[layer] + i) % 2, pos=-1,
                         banks=(lambda m: MB[:, 2 * i + m, :]) if i < 2 else None)
                U.loop(FFNS[layer])
                pe.wait_ge(evac_a, PROJ[layer] + 2)
                norm_slot((1, 3)[layer], FFNS[layer], f"ffn{layer}")
                for g, n in enumerate(GROUPS):
                    b = ffn_base(layer, g)
                    q0 = TQ[f"hid{layer}"] + 2 * sum(GROUPS[:g])

                    def hid_in(p):
                        pe.wait_ge(evac_v, p * 2 + (b + 2))
                        transpose_in(lambda c, m: Hb[:, m, c * P:(c + 1) * P], 2, q=p * 2 + q0)

                    for j in range(0 if g else 4, 8):
                        if j % 4 == 0:
                            banks_free(b + j // 4)
                        unit(b + j // 4, j % 4, XA)
                    with pe.Fori(0, n - 1) as i:
                        for j in range(8):
                            s = i * 2 + (b + 2 + j // 4)
                            if j % 4 == 0:
                                banks_free(s)
                            unit(s, j % 4, XA, par=(b + j // 4) % 2)
                            if j == 1:
                                hid_in(i)
                    d0 = b + 2 * n
                    banks_free(d0)
                    for j in range(4):
                        need = q0 + 2 * n if (j + 1) * n > 4 * (n - 1) else q0 + 2 * (n - 1)
                        unit(d0, j, XB, kc=n, need=need)
                        if j == 1:
                            hid_in(n - 1)
                    with pe.Fori(0, 3) as i:
                        banks_free(i + (d0 + 1))
                        for j in range(4):
                            unit(i + (d0 + 1), j, XB, kc=n, par=(i + (d0 + 1)) % 2)
                fresh_slot(GATE[layer], h, TQ[f"ple{layer}"], (upd, upd), (4 * layer + 3, 4 * layer + 4))
                with pe.Fori(0, 3) as i:
                    banks_free(i + (GATE[layer] + 1))
                    for j in range(4):
                        unit(i + (GATE[layer] + 1), j, XA, par=(i + (GATE[layer] + 1)) % 2)
                if layer == 1:
                    break
                norm_slot(2, L1, "mix1")
                for s in range(L1 + 1, OUT1):
                    banks_free(s)
                    nsa_guard(s)
                    for j in range(units(s)):
                        if s == SW1:
                            kv, k, buf = j // 2, j % 2, U.place(s, j) % 2
                            pe.wait_ge(hi_ready, U(s) + j + 1)
                            pe.wait_ge(lo_ready, U(s) + j + 1)
                            pe.wait_ge(bl_ok, kv + 1)
                            for l in range(16):
                                for part in range(2):
                                    last = mm(PG[0:60, s % 2, kv, 0:2 * P], BL[:, kv, 16 * k + l, part, :],
                                              whl[:, :, buf, l * P:(l + 1) * P],
                                              start=(k == l == part == 0), stop=(k == part == 1 and l == 15))
                            last.then_inc(unit_done, 1)
                        else:
                            unit(s, j, XA, *shape_of(s))
                        gap(s, j)

        @block.scalar
        def _(act):
            A = nc.scalar.activation
            step = Steps(act, act_step)
            U = Ring()

            def flat(t):
                return t.rearrange("p a t -> p (a t)")

            def split(s, j, w=None):
                w = w or width(s)
                place = U.place(s, j)
                act.wait_ge(raw_in[place], U.landed(s, j))
                if not (isinstance(s, int) and U(s) + j < 2):
                    act.wait_ge(unit_done, U(s) + (j - 1))
                A(wh[:, place % 2, 0:w], raw[:, place, 0:w], ACT.Copy).then_inc(hi_ready, 1)

            def split_in(X, n, q, c0, col=None, b0=0, banks=2):
                for b in range(b0, b0 + n):
                    act.wait_ge(tx_ps, q + (b + 1))
                    src = MB[:, b % banks, :]
                    if col is None:
                        A(flat(X[:, bass.ds(c0 + 2 * b, 2), :]), src, ACT.Copy).then_inc(tx_hi, 1)
                    else:
                        for c in range(2):
                            k = 2 * b + c
                            last = A(X[:, c0 + k, :], src[:, c * SEQ:(c + 1) * SEQ], ACT.Copy,
                                     scale=vcol[:, col + k:col + k + 1])
                        last.then_inc(tx_hi, 1)

            def fresh_slot(s, name, col=None, done=0, after=lambda: None):
                for j in range(4):
                    if j == 2:
                        after()
                    if j > 1 and j >= done:
                        split(s, j)
                    split_in(XAh, 2, TQ[name], 0, col, 2 * j, 4)
                    if j <= 1 and j >= done:
                        split(s, j)

            def norm_sums(k, mid=lambda: None):
                if k == 0:
                    act.wait_ge(x_in, 32)
                for m in range(NT):
                    if k % 2:
                        act.wait_ge(upd, 1 + m + 4 * (k // 2))
                    A(Fm[:, m, :], h[:, m, :], ACT.Square, accum_out=ss[:, m, 0:1]).then_inc(ssq, 1)
                    if m == 0:
                        mid()

            def norm_scale(k):
                act.wait_ge(ssq, 2 * k + 2)
                act.wait_ge(pw_done, POW.index(("mix0", "ffn0", "mix1", "ffn1")[k]) + 1)
                A(Fm[:, 0, :], h[:, 0, :], ACT.Copy, scale=pwo[:, 0:1]).then_inc(hn_a, 1)

            def exps(t, SP):
                act.wait_ge(mx_ok, t + 1)
                for b in range(2):
                    for m in range(NT):
                        c = SP[:, b, m * P:m * P + (m + 1) * P]
                        k = 2 * m + b
                        last = A(c, c, ACT.Exp, bias=sm[:, k:k + 1], accum_out=sm[:, 4 + k:5 + k])
                last.then_inc(exp_ok, 1)

            def mla_stage(t):
                if 1 <= t <= MLA_STEPS:
                    act.wait_ge(pt_done, t)
                    A(PT0[:, :, :], MB[:, 2:4, 0:384], ACT.Copy).then_inc(pt_sb, 1)
                if t < MLA_STEPS:
                    exps(t, SP0)
                if t >= 2:
                    act.wait_ge(pv_done, t - 1)
                    for b in range(2):
                        last = A(XBh[:, 2 * (t - 2) + b, :].rearrange("p (m t) -> p m t", m=2),
                                 MB[:, 2 * b:2 * b + 2, 384:512], ACT.Copy)
                    last.then_inc(o_hi, 1)

            def nsa_stage(t):
                if t >= 2:
                    act.wait_ge(pv_done, MLA_STEPS + t - 1)
                    A(XBh[:, t - 2, :], MB[:, 2, 0:SEQ], ACT.Copy).then_inc(o_hi, 1)
                if t in CP_STEP:
                    g = CP_STEP[t]
                    act.wait_ge(cp_ps, g + 1)
                    A(PcT[:, g % 2, :], MB[:, 3, 0:SEQ], ACT.Copy).then_inc(pct_sb, 1)
                if t < NSA_STEPS:
                    exps(MLA_STEPS + t, SP1[t % 2])
                if 1 <= t <= NSA_STEPS:
                    act.wait_ge(pt_done, MLA_STEPS + t)
                    A(PT1[:, :, :], MB[:, 2:4, 0:384], ACT.Copy).then_inc(pt_sb, 1)

            def gla_stage(k):
                if k == 0:
                    act.wait_ge(ga_ps, 1)
                    A(loga[:, :, :], MB[:, 2:4, :], ACT.Copy).then_inc(ga_t, 1)
                    act.wait_ge(ga_n, 1)
                    step(A(E1[:, :, :], E1[:, :, :], ACT.Exp))
                    A(E1[:, :, :], E1[:, :, :], ACT.Ln, bias=1.0).then_inc(ga_l, 1)
                if k == 1:
                    act.wait_ge(gb_ps, 1)
                    A(E1[:, :, :], MB[:, 0:2, :], ACT.Exp).then_inc(ge_a, 1)
                    A(kinv[:, :, :], MB[:, 0:2, :], ACT.Exp, scale=-1.0).then_inc(ge_a, 1)
                    A(rt[:, :, :], MB[:, 2:4, :], ACT.Exp).then_inc(ge_a, 1)
                if k == 2:
                    act.wait_ge(gt_ps, 1)
                    A(flat(qdT[:, :, :]), flat(MB[:, 0:2, :]), ACT.Copy)
                    A(flat(kiT[:, :, :]), flat(MB[:, 2:4, :]), ACT.Copy).then_inc(gt_sb, 1)
                if k == 3:
                    act.wait_ge(gu_ps, 1)
                    A(flat(decs[:, :, :]), MB[:, 0, 384:400], ACT.Exp).then_inc(gd_sb, 1)
                if k == 5:
                    act.wait_ge(go_ps, 1)
                    for m in range(NT):
                        last = A(AT[m][:, :, :], MB[:, 2 * m:2 * m + 2, :], ACT.Square)
                    last.then_inc(go_sq, 1)

            def evac(s):
                act.wait_ge(unit_done, U.end(s))
                src = PG[:, s % 2, 0, :]
                if s in (ZC0, ZC1, ZC2):
                    A(zc[:, 0, W_ZC * s:W_ZC * (s + 1)], src[:, 0:W_ZC], ACT.Copy).then_inc(evac_a, 1)
                elif s in (UQN, UQN + 1, UKK, UKK + 1):
                    t, c = (QnT, 4 * (s - UQN)) if s < UKK else (KnT, 4 * (s - UKK))
                    A(flat(t[:, c:c + 2, :]), src, ACT.Copy).then_inc(evac_a, 1)
                elif s in (GG, GG + 1):
                    act.wait_ge(ge_v, 1)
                    if s == GG + 1:
                        act.wait_ge(evac_v, GG + 1)
                    A(rt[:, :, :], PG[:, s % 2, :, :], ACT.Tanh, scale=0.5).then_inc(evac_a, 1)
                elif s in COPY0:
                    t, c = COPY0[s]
                    w = shape_of(s)[1]
                    A(t[:, 0, c:c + w], src[:, 0:w], ACT.Copy).then_inc(evac_a, 1)
                elif s == SVC:
                    A(KB[:, 1, 0, :], src, ACT.Copy).then_inc(evac_a, 1)
                elif s == SW1:
                    act.wait_ge(ge_x, 1)
                    A(GU[:, :, :], GU[:, :, :], ACT.Tanh, scale=GELU_C / 2).then_inc(ge_e, 1)
                    act.drain().then_inc(evac_a, 1)
                elif s == SGT:
                    act.wait_ge(evac_v, SGT + 1)
                    A(gates[:, :, :], gates[:, :, :], ACT.Tanh, scale=0.5).then_inc(gx_e, 1)
                    act.drain().then_inc(evac_a, 1)
                else:
                    act.drain().then_inc(evac_a, 1)

            def at_gap(k):
                if k == (QG, 2):
                    act.wait_ge(tx_ps, TQ["cqkv"] + 1)
                    split_in(XBh, 4, TQ["cqkv"], 0, 64)
                    act.wait_ge(al_ps, 1)
                    act.wait_ge(const_mk, 1)
                    A(AL[0:16, :], MB[0:16, 2, 0:SEQ], ACT.Copy).then_inc(al_sb, 1)
                if k == (UQR + 2, 0):
                    act.wait_ge(qrt_ps, 1)
                    A(flat(QrT[:, :, :]), flat(MB[:, 2:4, :]), ACT.Copy)
                    A(KrT[:, :], MB[:, 1, 0:SEQ], ACT.Copy).then_inc(qrt_sb, 1)
                if k in MLA_AT:
                    mla_stage(MLA_AT[k])
                if k in GLA_AT:
                    gla_stage(GLA_AT[k])
                if k == (OUT0, 1):
                    split_in(XBh, 4, TQ["gla"], 8, banks=4)
                    act.wait_ge(go_ok, 1)
                    act.dma_start(wbc[:, :], T["ln_mix_post"][0:1, :].broadcast_to([P, D])).then_inc(wbc_in, 16)
                    act.dma_start(pp[:, :, :], p_d[0]).then_inc(pp_in, 16)
                if k in PP_AT:
                    split_in(PXh, 1, TQ[f"p{PP_AT[k]}"], 0)
                if k in KT_AT:
                    n = KT_AT[k]
                    act.wait_ge(kt_ps, n + 1)
                    A(flat((kcT, vcT, ksT, kwT)[n][:, :, :]), flat(MB[:, 2:4, :]), ACT.Copy).then_inc(kt_sb, 1)
                if k == (SW1 + 2, 2):
                    act.wait_ge(c2_ps, 1)
                    A(flat(KcT[:, :, :]), MB[:, 0, 0:P], ACT.Copy).then_inc(c2_a, 1)
                for op, g in NSA_AT.get(k, ()):
                    if op == "qt":
                        act.wait_ge(qt_ps, g + 1)
                        A(flat(QT[:, g % 2, :, :]), flat(PG[:, (SQ + g) % 2, :, :]), ACT.Copy).then_inc(qt_sb, 1)
                    if op == "cs":
                        act.wait_ge(cs_in, g + 1)
                        A(csc[:, :, :, :], csc[:, :, :, :], ACT.Exp).then_inc(cs_e, 1)
                    if op == "st":
                        nsa_stage(g)
                if k == (OUT1 + 1, 1):
                    act.wait_ge(head_ok, NSA_STEPS)
                    act.dma_start(wbc[:, :], T["ln_mix_post"][1:2, :].broadcast_to([P, D])).then_inc(wbc_in, 16)
                    act.dma_start(pp[:, :, :], p_d[1]).then_inc(pp_in, 16)

            def stage(s, j):
                if j == evac_stage(s):
                    evac(s - 1)
                if (s, j) == (ZC1, 1):
                    act.wait_ge(ang_ok, 1)
                    A(sinT[:, :, :], ang[:, :, :], ACT.Sin)
                    A(cosT[:, :, :], kk[:, :, :], ACT.Sin).then_inc(trig_ok, 1)
                for k in STAGED_ACT.get((s, j), ()):
                    at_gap(k)
                if (s, j) in ((SKC + 1, 3), (SVC + 1, 3)):
                    n = s - SKC - 1
                    act.wait_ge(bt_ok, n + 1)
                    A(BL[:, n, :, 0, :], BT[:, :, :], ACT.Copy).then_inc(bh_ok, 1)

            norm_sums(0)
            act.wait_ge(vt_ps, 1)
            A(vcol[:, :], MB[:, 2, 0:72], ACT.Copy).then_inc(vt_sb, 1)
            A(posT[:, :], MB[:, 2, P:P + 64], ACT.Copy).then_inc(vt_sb, 1)
            norm_scale(0)
            act.wait_ge(vt_sb, 2)
            fresh_slot(0, "mix0", 0)
            for s in range(1, OUT0 + 1):
                for j in range(units(s)):
                    split(s, j)
                    stage(s, j)
            stage(OUT0, 4)

            for layer in range(2):
                s0 = OUTS[layer]

                def mixer_panel(i, done=None):
                    s = i + s0
                    act.wait_ge(unit_done, done or U.end(s))
                    A(rt[:, 0, :], PG[:, s % 2, 0, :], ACT.Square, accum_out=ss[:, 0, bass.ds(i, 1)]).then_inc(sq_done, 1)
                    act.wait_ge(mul_done, i + (4 * layer + 1))
                    A(rt[:, 1, :], PG[:, s % 2, 1, :], ACT.Square, accum_out=ss[:, 1, bass.ds(i, 1)]).then_inc(evac_a, 1)

                U.loop(s0)
                if layer == 0:
                    with act.Fori(0, 3) as i:
                        for j in range(4):
                            split(i + (s0 + 1), j)
                            if j == 1:
                                mixer_panel(i)
                else:
                    for s in (OUT1 + 2, OUT1 + 3):
                        for j in range(4):
                            split(s, j)
                            if (s, j) == (OUT1 + 2, 0):
                                mixer_panel(0, U(OUT1 + 1) + 3)
                            if (s, j) == (OUT1 + 2, 1):
                                act.wait_ge(evac_a, OUT1 + 1)
                            if j == 1:
                                mixer_panel(s - OUT1 - 1)

                pr, f0 = PROJ[layer], FFNS[layer]

                def proj_panel(i):
                    act.wait_ge(unit_done, U.end(pr + i))
                    src = MB[:, 2 * i:2 * i + 2, :] if i < 2 else PG[:, (pr + i) % 2, :, :]
                    A(PJ[:, :, i * 512:i * 512 + 512], src, ACT.Copy).then_inc(evac_a, 1)

                split(pr, 0, 1024)
                mixer_panel(3)
                split(pr + 1, 0, 1024)
                act.wait_ge(evac_v, s0 + 4)
                act.dma_start(wbc[:, :], T["ln_ffn_post"][layer:layer + 1, :].broadcast_to([P, D]))\
                    .then_inc(wbc_in, 16)
                split(pr + 2, 0, 1024)
                proj_panel(0)
                norm_sums((1, 3)[layer])
                split(pr + 3, 0, 1024)
                norm_scale((1, 3)[layer])
                proj_panel(1)
                U.loop(f0)
                split(f0, 0)
                proj_panel(2)
                fresh_slot(f0, f"ffn{layer}", 16 + 32 * layer, done=1, after=lambda: proj_panel(3))

                for g, n in enumerate(GROUPS):
                    b = ffn_base(layer, g)
                    q0 = TQ[f"hid{layer}"] + 2 * sum(GROUPS[:g])

                    def gate_tanh(s):
                        act.wait_ge(unit_done, U.end(s))
                        act.wait_ge(evac_v, s)
                        A(Eb[:, :, :], PG[:, b % 2, :, :], ACT.Tanh, scale=0.5).then_inc(evac_a, 1)

                    def down_panel(i, g, d):
                        s = i + d
                        if g == 0:
                            act.wait_ge(unit_done, U.end(s))
                            A(Fm[:, 0, bass.ds(i * 512, 512)], PG[:, s % 2, 0, :], ACT.Copy).then_inc(evac_a, 1)
                            return
                        act.drain().then_inc(evac_a, 1)
                        if g == 2:
                            act.wait_ge(add_done, i + (4 * layer + 1))
                            A(rt[:, 0, :], Fm[:, 0, bass.ds(i * 512, 512)], ACT.Square,
                              accum_out=ss[:, 0, bass.ds(i, 1)]).then_inc(sq_done, 1)
                            act.wait_ge(evac_v, s + 1)
                            A(rt[:, 1, :], Fm[:, 1, bass.ds(i * 512, 512)], ACT.Square,
                              accum_out=ss[:, 1, bass.ds(i, 1)]).then_inc(sq_done, 1)

                    if g:
                        split(b, 0)
                        split(b, 1)
                        down_panel(3, g - 1, d0)
                        split(b, 2)
                        split(b, 3)
                    split(b + 1, 0)
                    split(b + 1, 1)
                    gate_tanh(b)
                    split(b + 1, 2)
                    split(b + 1, 3)
                    with act.Fori(0, n - 1) as i:
                        s = i * 2 + (b + 2)
                        split(s, 0)
                        split(s, 1)
                        act.drain().then_inc(evac_a, 1)
                        split(s, 2)
                        split_in(XBh, 2, i * 2 + q0, i * 4)
                        split(s, 3)
                        split(s + 1, 0)
                        split(s + 1, 1)
                        gate_tanh(s)
                        split(s + 1, 2)
                        split(s + 1, 3)
                    d0 = b + 2 * n
                    w = n * 512
                    split(d0, 0, w)
                    split(d0, 1, w)
                    act.drain().then_inc(evac_a, 1)
                    split(d0, 2, w)
                    split_in(XBh, 2, q0 + 2 * (n - 1), 4 * (n - 1))
                    split(d0, 3, w)
                    with act.Fori(0, 3) as i:
                        for j in range(4):
                            split(i + (d0 + 1), j, w)
                            if j == 1:
                                down_panel(i, g, d0)
                gt0 = GATE[layer]

                def gate_panel(i):
                    act.wait_ge(evac_v, i + (gt0 + 1))
                    A(Eb[:, :, :], Eb[:, :, :], ACT.Tanh, scale=0.5).then_inc(evac_a, 1)

                split(gt0, 0)
                down_panel(3, 2, d0)
                split(gt0, 1)
                act.wait_ge(upd, 4 * layer + 3)
                act.dma_start(wbc[:, :], T["ple_b_gate"][layer:layer + 1, :].broadcast_to([P, D])).then_inc(wbc_in, 16)
                fresh_slot(gt0, f"ple{layer}", done=2)
                def square_panel(i):
                    act.wait_ge(h_ok, i + 1)
                    for m in range(NT):
                        last = A(rt[:, m, :], h[:, m, bass.ds(i * 512, 512)], ACT.Square,
                                 accum_out=ss[:, m, bass.ds(i, 1)])
                        if not isinstance(i, int):
                            continue
                        last.then_inc(ssq, 1)
                    return last

                with act.Fori(0, 3) as i:
                    if layer == 0:
                        step.enter(i, 1)
                    for j in range(4):
                        split(i + (gt0 + 1), j)
                        if j == 1:
                            gate_panel(i)
                    if layer == 0:
                        step(square_panel(i))
                        step.leave(3)
                if layer == 1:
                    gate_panel(3)
                    break
                split(L1, 0)
                gate_panel(3)
                square_panel(3)
                norm_scale(2)
                fresh_slot(L1, "mix1", 32, done=1)
                for s in range(L1 + 1, OUT1 + 2):
                    for j in range(units(s)):
                        split(s, j)
                        stage(s, j)
                stage(OUT1 + 1, 4)

        @block.vector
        def _(v):
            V = nc.vector
            step = Steps(v, dve_step)
            U = Ring()

            def flat(t):
                return t.rearrange("p a t -> p (a t)")

            def split(s, j, w=None):
                v.wait_ge(hi_ready, U(s) + (j + 1))
                w = w or width(s)
                place = U.place(s, j)
                k = place % 2
                V.tensor_tensor(wl[:, k, 0:w], raw[:, place, 0:w], wh[:, k, 0:w].bitcast(F32),
                                ALU.subtract).then_inc(lo_ready, 1)

            def split_in(X, n, q, c0, col=None, b0=0, banks=2):
                for b in range(b0, b0 + n):
                    v.wait_ge(tx_hi, q + (b + 1))
                    src = MB[:, b % banks, :]
                    if col is None:
                        c = bass.ds(c0 + 2 * b, 2)
                        V.tensor_tensor(flat(X[1][:, c, :]), src, flat(X[0][:, c, :]).bitcast(F32),
                                        ALU.subtract).then_inc(tx_lo, 1)
                    else:
                        for c in range(2):
                            k = 2 * b + c
                            last = V.scalar_tensor_tensor(
                                X[1][:, c0 + k, :], src[:, c * SEQ:(c + 1) * SEQ], vcol[:, col + k:col + k + 1],
                                X[0][:, c0 + k, :].bitcast(F32), ALU.mult, ALU.subtract)
                        last.then_inc(tx_lo, 1)

            def ask(name):
                v.wait_ge(pw_done, POW.index(name) + 1)

            def fresh_slot(s, name, col=None, done=0):
                for j in range(4):
                    if j > 1 and j >= done:
                        split(s, j)
                    split_in(XA, 2, TQ[name], 0, col, 2 * j, 4)
                    if j <= 1 and j >= done:
                        split(s, j)

            def norm_out(k, between=lambda: None):
                name = ("mix0", "ffn0", "mix1", "ffn1")[k]
                v.wait_ge(ssq, 2 * k + 2)
                src = ss[:, :, 0]
                if k == 2:
                    step(V.tensor_reduce(pwi[:, 0:2], ss[:, :, :], AX.X, ALU.add))
                    src = pwi[:, 0:2]
                V.tensor_scalar(pwi[:, 0:2], src, 1.0 / D, EPS, ALU.mult, ALU.add).then_inc(pw_req, 1)
                between()
                ask(name)
                V.tensor_scalar(Fm[:, 1, :], h[:, 1, :], pwo[:, 1:2], None, ALU.mult).then_inc(hn_v, 1)

            def post_norm(name, between=lambda: None, mid=lambda: None):
                step(V.tensor_reduce(pwi[:, 0:2], ss[:, :, :], AX.X, ALU.add))
                V.tensor_scalar(pwi[:, 0:2], pwi[:, 0:2], 1.0 / D, EPS, ALU.mult, ALU.add).then_inc(pw_req, 1)
                between()
                ask(name)
                for m in range(NT):
                    V.scalar_tensor_tensor(h[:, m, :], Fm[:, m, :], pwo[:, m:m + 1], h[:, m, :],
                                           ALU.mult, ALU.add).then_inc(upd, 1)
                    if m == 0:
                        mid()

            def rope(src, dst, cos, sin, hd, done, par_sem):
                for m in range(NT):
                    n = 512 // (2 * hd)
                    a, b = (rt[:, k, :].rearrange("p (h x e) -> p h x e", x=2, e=hd) for k in range(2))
                    cs, sn = (t[:, m, ::64 // hd].rearrange("p (h x e) -> p h x e", h=1, x=1)
                              .broadcast_to([P, n, 2, hd]) for t in (cos, sin))
                    V.tensor_tensor(a, src(m), cs, ALU.mult)
                    ins = V.tensor_tensor(b, src(m), sn, ALU.mult)
                    if m == NT - 1:
                        ins.then_inc(par_sem, 1)
                        v.wait_ge(par_sem, cur[0] + 1)
                    else:
                        step(ins)
                    V.tensor_tensor(dst(m)[:, :, 0, :], a[:, :, 0, :], b[:, :, 1, :], ALU.subtract)
                    last = V.tensor_tensor(dst(m)[:, :, 1, :], a[:, :, 1, :], b[:, :, 0, :], ALU.add)
                    if m == 0:
                        step(last)
                last.then_inc(done, 1)

            cur = [0]

            def softmax(t, SP, scale, gate=None, meanwhile=lambda: None):
                v.wait_ge(s_done, t + 1)
                for b in range(2):
                    last = V.scalar_tensor_tensor(SP[:, b, :], MB[:, b, 0:384], scale, flat(cmask[:, :, :]),
                                                  ALU.mult, ALU.add)
                step(last)
                V.tensor_reduce(sm[:, 0:2], SP[:, :, 0:P], AX.X, ALU.max, negate=True)
                V.tensor_reduce(sm[:, 2:4], SP[:, :, P:384], AX.X, ALU.max, negate=True).then_inc(mx_ok, 1)
                meanwhile()
                v.wait_ge(exp_ok, t + 1)
                step(V.reciprocal(sm[:, 8:12], sm[:, 4:8]))
                if gate is not None:
                    f = sm[:, 8:12].rearrange("p (m b) -> p m b", m=2)
                    step(V.tensor_tensor(f, f, gate, ALU.mult))
                for b in range(2):
                    for m in range(NT):
                        c = SP[:, b, m * P:m * P + (m + 1) * P]
                        k = 8 + 2 * m + b
                        last = V.tensor_scalar(c, c, sm[:, k:k + 1], None, ALU.mult)
                return last

            def mla_stage(t):
                if t < MLA_STEPS:
                    last = softmax(t, SP0, MLA_SCALE)
                if t >= 2:
                    v.wait_ge(o_hi, t - 1)
                    for b in range(2):
                        x = [q[:, 2 * (t - 2) + b, :].rearrange("p (m t) -> p m t", m=2) for q in XB]
                        last = V.tensor_tensor(x[1], MB[:, 2 * b:2 * b + 2, 384:512], x[0].bitcast(F32), ALU.subtract)
                last.then_inc(att_v, 1)

            def nsa_stage(t, meanwhile):
                if t >= 2:
                    v.wait_ge(o_hi, MLA_STEPS + t - 1)
                    V.tensor_tensor(XBl[:, t - 2, :], MB[:, 2, 0:SEQ], XBh[:, t - 2, :].bitcast(F32),
                                    ALU.subtract).then_inc(head_ok, 1)
                if t < NSA_STEPS:
                    softmax(MLA_STEPS + t, SP1[t % 2], NSA_SCALE,
                            gates[:, :, 3 * t + 1:3 * t + 3], meanwhile).then_inc(p_ok, 1)

            def gla_stage(k):
                if k == 0:
                    v.wait_ge(ga_t, 1)
                    V.scalar_tensor_tensor(flat(E1[:, :, :]), flat(loga[:, :, :]), -1.0, flat(loga[:, :, :]),
                                           ALU.mult, ALU.min).then_inc(ga_n, 1)
                    v.wait_ge(ga_l, 1)
                    V.scalar_tensor_tensor(flat(loga[:, :, :]), flat(loga[:, :, :]), 0.0, flat(E1[:, :, :]),
                                           ALU.min, ALU.subtract).then_inc(ga_ok, 1)
                if k == 1:
                    v.wait_ge(evac_a, KG + 1)
                    v.wait_ge(ge_a, 1)
                    V.scalar_tensor_tensor(flat(qg[:, :, :]), flat(qg[:, :, :]), 0.125, flat(E1[:, :, :]),
                                           ALU.mult, ALU.mult)
                    v.wait_ge(ge_a, 2)
                    V.tensor_tensor(kinv[:, :, :], kg[:, :, :], kinv[:, :, :], ALU.mult)
                    v.wait_ge(ge_a, 3)
                    V.tensor_tensor(kg[:, :, :], kg[:, :, :], rt[:, :, :], ALU.mult).then_inc(ge_v, 1)
                if k == 3:
                    v.wait_ge(gd_sb, 1)
                    step(V.tensor_copy(SS[:, :, 0, :], MB[:, :, 0:P]))
                    for c in (1, 2):
                        for pr in range(4):
                            ins = V.scalar_tensor_tensor(SS[:, pr, c, :], SS[:, pr, c - 1, :], decs[:, pr, c:c + 1],
                                                         MB[:, pr, c * P:(c + 1) * P], ALU.mult, ALU.add)
                        if c == 1:
                            step(ins)
                    ins.then_inc(gs_ok, 1)
                if k == 4:
                    v.wait_ge(at_zero, 1)
                    v.wait_ge(at_ps, 1)
                    mask = lt[:, :].bitcast(U32).rearrange("p (h t) -> p h t", h=1).broadcast_to([P, 4, P])
                    for m in range(NT):
                        for hf in range(2):
                            last = V.copy_predicated(AT[m][:, hf, :].rearrange("p (h t) -> p h t", h=4), mask,
                                                     MB[:, 2 * m + hf, :].rearrange("p (h t) -> p h t", h=4))
                    last.then_inc(at_ok, 1)
                if k == 5:
                    v.wait_ge(go_sq, 1)
                    for m in range(NT):
                        last = V.tensor_reduce(pwi[:, 8 * m:8 * m + 8], AT[m][:, :, :].rearrange(
                            "p f (h t) -> p (f h) t", h=4), AX.X, ALU.add)
                    step(last)
                    V.tensor_scalar(pwi[:, :], pwi[:, :], 1.0 / P, EPS, ALU.mult, ALU.add).then_inc(pw_req, 1)

            def gla_out():
                ask("gla")
                for m in range(NT):
                    for hf in range(2):
                        k = 8 * m + 4 * hf
                        r = pwo[:, k:k + 4].rearrange("p (h t) -> p h t", t=1).broadcast_to([P, 4, P])
                        step(V.tensor_tensor(oT[:, :].rearrange("p (h t) -> p h t", h=4),
                                             MB[:, 2 * m + hf, :].rearrange("p (h t) -> p h t", h=4), r, ALU.mult))
                        x = gg[:, m, 512 * hf:512 * hf + 512]
                        last = V.tensor_tensor(x, x, oT[:, :], ALU.mult)
                        if k < 12:
                            step(last)
                last.then_inc(go_ok, 1)

            def evac(s):
                v.wait_ge(unit_done, U.end(s))
                cur[0] = s
                par = s % 2
                src = PG[:, par, 1, :]
                if s in (ZC0, ZC1, ZC2):
                    V.tensor_copy(zc[:, 1, W_ZC * s:W_ZC * (s + 1)], src[:, 0:W_ZC]).then_inc(evac_v, 1)
                elif s in (UQN, UQN + 1, UKK, UKK + 1):
                    t, c = (QnT, 4 * (s - UQN)) if s < UKK else (KnT, 4 * (s - UKK))
                    V.tensor_copy(flat(t[:, c + 2:c + 4, :]), src).then_inc(evac_v, 1)
                elif s == UQR:
                    rope(lambda m: PG[:, par, m, :].rearrange("p (h x e) -> p h x e", x=2, e=32),
                         lambda m: qr[:, m, :].rearrange("p (h x e) -> p h x e", x=2, e=32), cosT, sinT, 32,
                         qr_ok, evac_v)
                elif s in (GG, GG + 1):
                    v.wait_ge(evac_a, s + 1)
                    c = 512 * (s - GG)
                    V.scalar_tensor_tensor(gg[:, :, c:c + 512], rt[:, :, :], 1.0, PG[:, par, :, :],
                                           ALU.add, ALU.mult).then_inc(evac_v, 1)
                    v.wait_ge(evac_v, s + 1)
                    v.wait_ge(const_in, 16 * N_CONST)
                    for m in range(NT):
                        x = gg[:, m, c:c + 512].rearrange("p (h t) -> p h t", h=4)
                        gn = gnw[:, :].rearrange("p (h t) -> p h t", h=1).broadcast_to([P, 4, P])
                        last = V.scalar_tensor_tensor(x, x, 0.5, gn, ALU.mult, ALU.mult)
                    step(last)
                elif s in COPY0:
                    t, c = COPY0[s]
                    w = shape_of(s)[1]
                    V.tensor_copy(t[:, 1, c:c + w], src[:, 0:w]).then_inc(evac_v, 1)
                elif s == SVC:
                    V.tensor_copy(KB[:, 1, 1, :], src).then_inc(evac_v, 1)
                    v.wait_ge(evac_v, s + 1)
                    v.sem_inc(ke_ok, 1)
                elif s in (SKC, SKS, SKW) or SQ <= s < SQ + 4:
                    if s >= SQ:
                        g = s - SQ
                        if g >= 2:
                            v.wait_ge(qt_ps, g - 1)
                        dst, done = (lambda m: zq[:, g % 2, m, :]), qe_ok
                    else:
                        k = {SKC: 0, SKS: 2, SKW: 3}[s]
                        if k >= 2:
                            v.wait_ge(kt_ps, k - 1)
                        dst, done = (lambda m: KB[:, k % 2, m, :]), ke_ok
                    rope(lambda m: PG[:, par, m, :].rearrange("p (h x e) -> p h x e", x=2, e=64),
                         lambda m: dst(m).rearrange("p (h x e) -> p h x e", x=2, e=64), cosT, sinT, 64, done, evac_v)
                elif s == SW1:
                    step(V.tensor_copy(GU[:, :, :], PG[0:60, par, :, P:2 * P]))
                    V.tensor_tensor(GX[:, :, :], PG[0:60, par, :, 0:P], GU[:, :, :], ALU.add).then_inc(evac_v, 1)
                    v.wait_ge(evac_v, s + 1)
                    step(V.tensor_tensor(GU[:, :, :], GX[:, :, :], GX[:, :, :], ALU.mult))
                    step(V.tensor_scalar(GU[:, :, :], GU[:, :, :], 0.044715, 1.0, ALU.mult, ALU.add))
                    V.tensor_tensor(GU[:, :, :], GU[:, :, :], GX[:, :, :], ALU.mult).then_inc(ge_x, 1)
                    v.wait_ge(ge_e, 1)
                    step(V.tensor_scalar(GU[:, :, :], GU[:, :, :], 1.0, 0.5, ALU.add, ALU.mult))
                    V.tensor_tensor(GU[:, :, :], GX[:, :, :], GU[:, :, :], ALU.mult).then_inc(ge_ok, 1)
                elif s == SGT:
                    b = gbias[:, :].rearrange("p (m n) -> p m n", m=1).broadcast_to([P, NT, W_GT])
                    V.tensor_copy(vw[:, :, W_VG:512], PG[:, par, :, 0:512 - W_VG])
                    V.tensor_tensor(gates[:, :, :], PG[:, par, :, 512 - W_VG:W_VG], b, ALU.add).then_inc(evac_v, 1)
                    v.wait_ge(gx_e, 1)
                    step(V.tensor_scalar(gates[:, :, :], gates[:, :, :], 1.0, 0.5, ALU.add, ALU.mult))

            def lowrank_sums(k):
                for m in range(NT):
                    x = zc[:, m, 16 + 512 * k:528 + 512 * k]
                    step(V.tensor_tensor_reduce(out=rt[:, 0, :], in0=x, in1=x, scale=1.0, scalar=0.0,
                                                op0=ALU.mult, op1=ALU.add,
                                                accum_out=pwi[:, 2 * k + m:2 * k + m + 1]))

            def lowrank_scale():
                ask("cqkv")
                for k in range(2):
                    for m in range(NT):
                        x = zc[:, m, 16 + 512 * k:528 + 512 * k]
                        last = V.tensor_scalar(x, x, pwo[:, 2 * k + m:2 * k + m + 1], None, ALU.mult)
                last.then_inc(zn_ok, 1)

            def rope_kr():
                v.wait_ge(trig_ok, 1)
                for m in range(NT):
                    x = zc[:, m, 1040:1104].rearrange("p (x e) -> p x e", x=2)
                    a, b = (rt[:, k, 0:64].rearrange("p (x e) -> p x e", x=2) for k in range(2))
                    cs, sn = (t[:, m, ::2].rearrange("p (x e) -> p x e", x=1).broadcast_to([P, 2, 32])
                              for t in (cosT, sinT))
                    V.tensor_tensor(a, x, cs, ALU.mult)
                    step(V.tensor_tensor(b, x, sn, ALU.mult))
                    for d in range(2):
                        V.tensor_tensor(krd[:, m, d, 0:32], a[:, 0, :], b[:, 1, :], ALU.subtract)
                        last = V.tensor_tensor(krd[:, m, d, 32:64], a[:, 1, :], b[:, 0, :], ALU.add)
                    if m == 0:
                        step(last)
                last.then_inc(kr_ok, 1)
                v.wait_ge(kr_ok, 1)

            def compressed(g):
                v.wait_ge(cs_ps, g + 1)
                for m in range(NT):
                    nm = negm[:, m, :].rearrange("p (j n) -> p j n", j=1).broadcast_to([P, 4, 16])
                    last = V.scalar_tensor_tensor(
                        csc[:, m, :, :], PG[:, (SQ + g) % 2, 0, 64 * m:64 * m + 64].rearrange("p (j n) -> p j n", j=4),
                        NSA_SCALE, nm, ALU.mult, ALU.add)
                step(last)
                c8 = csc[:, :, :, :].rearrange("p m j n -> p (m j) n")
                col = lambda k: cst[:, k, :].rearrange("p (a n) -> p a n", n=1).broadcast_to([P, 8, 16])
                step(V.tensor_reduce(cst[:, 0, :], c8, AX.X, ALU.max))
                V.tensor_tensor(c8, c8, col(0), ALU.subtract).then_inc(cs_in, 1)
                v.wait_ge(cs_e, g + 1)
                step(V.tensor_reduce(cst[:, 1, :], c8, AX.X, ALU.add))
                step(V.reciprocal(cst[:, 2, :], cst[:, 1, :]))
                f = cst[:, 2, :].rearrange("p (m j) -> p m j", m=2)
                step(V.tensor_tensor(f, f, gates[:, :, 12 * g:12 * g + 12:3], ALU.mult))
                step(V.tensor_tensor(c8, c8, col(2), ALU.mult))
                if g:
                    v.wait_ge(cp_ps, g)
                ok = okm[:, :, :].rearrange("p m (j n) -> p m j n", j=1).broadcast_to([P, NT, 4, 16])
                V.tensor_tensor(Pc[:, :, :, 0:16], csc[:, :, :, :], ok, ALU.mult).then_inc(cs_ok, 1)

            def angles():
                v.wait_ge(const_mk, 1)
                v.wait_ge(start_in, 16 * N_START)
                step(V.tensor_copy(posf[:, :], posi[:, :]))
                for m in range(NT):
                    last = V.tensor_scalar(ang[:, m, :], invb[:, :], posf[:, m:m + 1], None, ALU.mult)
                step(last)
                step(V.tensor_scalar(kk[:, :, :], ang[:, :, :], 1.0 / TWO_PI, MAGIC, ALU.mult, ALU.add))
                step(V.tensor_scalar(kk[:, :, :], kk[:, :, :], MAGIC, None, ALU.subtract))
                for c in (C1, C2, C3):
                    step(V.scalar_tensor_tensor(flat(ang[:, :, :]), flat(kk[:, :, :]), -c, flat(ang[:, :, :]),
                                                ALU.mult, ALU.add))
                step(V.tensor_scalar(ang[:, :, :], ang[:, :, :], PI_IN, -PI_IN, ALU.min, ALU.max))
                step(V.scalar_tensor_tensor(flat(kk[:, :, :]), flat(ang[:, :, :]), -1.0, flat(ang[:, :, :]),
                                            ALU.mult, ALU.min))
                V.tensor_scalar(kk[:, :, :], kk[:, :, :], TWO_PI / 4, None, ALU.add).then_inc(ang_ok, 1)

            early = set()

            def split_once(s, j):
                if (s, j) not in early:
                    split(s, j)
                    early.add((s, j))

            def at_gap(k):
                if k == (QG, 2):
                    split_in(XB, 4, TQ["cqkv"], 0, 64)
                if k in MLA_AT:
                    mla_stage(MLA_AT[k])
                if k in GLA_AT:
                    gla_stage(GLA_AT[k])
                if k == (OUT0, 1):
                    split_in(XB, 4, TQ["gla"], 8, banks=4)
                if k in PP_AT:
                    split_in(PX, 1, TQ[f"p{PP_AT[k]}"], 0)
                if k == (SW1 + 1, 2):
                    v.wait_ge(gl_ps, 1)
                    for kv in range(2):
                        last = V.tensor_copy(GE[:, kv, :, 0:NCMP], MB[:, 0, 64 * kv:64 * kv + 60].rearrange(
                            "p (g n) -> p g n", g=4))
                    last.then_inc(gl_ok, 1)
                if k == (SW1 + 2, 2):
                    v.wait_ge(vb_zero, 1)
                    v.wait_ge(c2_ps, 1)
                    for jj in range(4):
                        r = slice(32 * jj, 32 * jj + 32)
                        last = V.tensor_copy(VB[r, :, jj, :], MB[r, 1, :].rearrange("p (g t) -> p g t", g=4))
                    last.then_inc(c2_v, 1)
                for op, g in NSA_AT.get(k, ()):
                    if op == "cs":
                        compressed(g)
                    if op == "st":
                        x = 4 * k[0] + k[1] + 2
                        nsa_stage(g, lambda: split_once(x // 4, x % 4))

            def stage(s, j):
                if j == evac_stage(s):
                    evac(s - 1)
                if (s, j) == (ZC1, 0):
                    angles()
                if (s, j) == (ZC2, 2):
                    v.wait_ge(evac_a, ZC1 + 1)
                    lowrank_sums(0)
                if (s, j) == (QG, 1):
                    v.wait_ge(evac_a, ZC2 + 1)
                    lowrank_sums(1)
                    V.tensor_scalar(pwi[:, 0:4], pwi[:, 0:4], 1.0 / 512, EPS, ALU.mult, ALU.add).then_inc(pw_req, 1)
                if (s, j) == (QG, 2):
                    lowrank_scale()
                if (s, j) == (QG, 3):
                    rope_kr()
                if (s, j) == (OUT0, 1):
                    gla_out()
                for k in STAGED_DVE.get((s, j), ()):
                    at_gap(k)
                if (s, j) in ((SKC + 1, 3), (SVC + 1, 3)):
                    n = s - SKC - 1
                    v.wait_ge(kt_sb, n + 1)
                    if n:
                        v.wait_ge(bh_ok, 1)
                    src = (kcT, vcT)[n][:, :, :].rearrange("p g (n l) -> p l g n", l=16)
                    for a in range(2):
                        c = 32 * n + 16 * a
                        pos = posT[:, c:c + 16].rearrange("p (l g n) -> p l g n", g=1, n=1).broadcast_to([P, 16, 4, 15])
                        last = V.tensor_tensor(BT[:, 16 * a:16 * a + 16, :].rearrange("p l (g n) -> p l g n", g=4),
                                               src[:, :, :, a:a + 15], pos, ALU.add)
                    last.then_inc(bt_ok, 1)
                    v.wait_ge(bh_ok, n + 1)
                    v.wait_ge(bt_ok, n + 1)
                    V.tensor_tensor(BL[:, n, :, 1, :], BT[:, :, :], BL[:, n, :, 0, :].bitcast(F32),
                                    ALU.subtract).then_inc(bl_ok, 1)

            v.wait_ge(x_in, 32)
            norm_out(0)
            v.wait_ge(vt_sb, 2)
            fresh_slot(0, "mix0", 0)


            for s in range(1, OUT0 + 1):
                for j in range(units(s)):
                    split(s, j)
                    stage(s, j)
            stage(OUT0, 4)

            for layer in range(2):
                s0 = OUTS[layer]

                def mixer_panel(i, done=None):
                    s = i + s0
                    v.wait_ge(unit_done, done or U.end(s))
                    v.wait_ge(wbc_in, 16 * (3 * layer + 1))
                    c = bass.ds(i * 512, 512)
                    V.tensor_tensor(Fm[:, 1, c], PG[:, s % 2, 1, :], wbc[:, c], ALU.mult).then_inc(mul_done, 1)
                    v.wait_ge(sq_done, i + (12 * layer + 1))
                    V.tensor_tensor(Fm[:, 0, c], PG[:, s % 2, 0, :], wbc[:, c], ALU.mult).then_inc(evac_v, 1)

                U.loop(s0)
                if layer == 0:
                    with v.Fori(0, 3) as i:
                        for j in range(4):
                            split(i + (s0 + 1), j)
                            if j == 1:
                                mixer_panel(i)
                else:
                    for s in (OUT1 + 2, OUT1 + 3):
                        for j in range(4):
                            split(s, j)
                            if (s, j) == (OUT1 + 2, 0):
                                mixer_panel(0, U(OUT1 + 1) + 3)
                            if j == 1:
                                mixer_panel(s - OUT1 - 1)

                pr, f0 = PROJ[layer], FFNS[layer]
                split(pr, 0, 1024)
                mixer_panel(3)
                v.wait_ge(evac_a, s0 + 4)
                v.wait_ge(evac_v, s0 + 4)
                v.sem_inc(evac_v, 4)
                post_norm(f"post{layer}", mid=lambda: split(pr + 1, 0, 1024))
                split(pr + 2, 0, 1024)
                norm_out((1, 3)[layer], lambda: split(pr + 3, 0, 1024))
                U.loop(f0)
                split(f0, 0)
                fresh_slot(f0, f"ffn{layer}", 16 + 32 * layer, done=1)

                for g, n in enumerate(GROUPS):
                    b = ffn_base(layer, g)
                    q0 = TQ[f"hid{layer}"] + 2 * sum(GROUPS[:g])

                    def silu(s):
                        v.wait_ge(evac_a, s + 1)
                        V.scalar_tensor_tensor(Eb[:, :, :], Eb[:, :, :], 1.0, PG[:, b % 2, :, :],
                                               ALU.add, ALU.mult).then_inc(evac_v, 1)

                    def hidden(s):
                        v.wait_ge(unit_done, U.end(s))
                        v.wait_ge(evac_v, s)
                        V.scalar_tensor_tensor(Hb[:, :, :], Eb[:, :, :], 0.5, PG[:, (b + 1) % 2, :, :],
                                               ALU.mult, ALU.mult).then_inc(evac_v, 1)

                    def down_panel(i, g, d):
                        s = i + d
                        v.wait_ge(unit_done, U.end(s))
                        c = bass.ds(i * 512, 512)
                        if g == 0:
                            V.tensor_copy(Fm[:, 1, c], PG[:, s % 2, 1, :]).then_inc(evac_v, 1)
                            return
                        first = V.tensor_tensor(Fm[:, 0, c], PG[:, s % 2, 0, :], Fm[:, 0, c], ALU.add)
                        if g == 2:
                            first.then_inc(add_done, 1)
                        V.tensor_tensor(Fm[:, 1, c], PG[:, s % 2, 1, :], Fm[:, 1, c], ALU.add).then_inc(evac_v, 1)

                    def weigh(i):
                        c = bass.ds(i * 512, 512)
                        v.wait_ge(wbc_in, 16 * (3 * layer + 2))
                        for m in range(NT):
                            v.wait_ge(sq_done, i * 2 + (12 * layer + 5 + m))
                            last = V.tensor_tensor(Fm[:, m, c], Fm[:, m, c], wbc[:, c], ALU.mult)
                        step(last)

                    if g:
                        split(b, 0)
                        split(b, 1)
                        down_panel(3, g - 1, d0)
                        split(b, 2)
                        split(b, 3)
                    split(b + 1, 0)
                    split(b + 1, 1)
                    silu(b)
                    split(b + 1, 2)
                    split(b + 1, 3)
                    with v.Fori(0, n - 1) as i:
                        s = i * 2 + (b + 2)
                        split(s, 0)
                        split(s, 1)
                        hidden(i * 2 + (b + 1))
                        split(s, 2)
                        split_in(XB, 2, i * 2 + q0, i * 4)
                        split(s, 3)
                        split(s + 1, 0)
                        split(s + 1, 1)
                        silu(s)
                        split(s + 1, 2)
                        split(s + 1, 3)
                    d0 = b + 2 * n
                    w = n * 512
                    split(d0, 0, w)
                    split(d0, 1, w)
                    hidden(d0 - 1)
                    split(d0, 2, w)
                    split_in(XB, 2, q0 + 2 * (n - 1), 4 * (n - 1))
                    split(d0, 3, w)
                    with v.Fori(0, 3) as i:
                        step.enter(i, 1 if g == 2 else 0)
                        for j in range(4):
                            if j == 1 and g == 2:
                                down_panel(i, g, d0)
                            split(i + (d0 + 1), j, w)
                            if j == 1 and g == 2:
                                weigh(i)
                            if j == 1 and g < 2:
                                down_panel(i, g, d0)
                        step.leave(3)
                gt0 = GATE[layer]

                def gate_add(i):
                    s = i + gt0
                    v.wait_ge(unit_done, U.end(s))
                    v.wait_ge(wbc_in, 16 * (3 * layer + 3))
                    c = bass.ds(i * 512, 512)
                    V.tensor_tensor(Eb[:, 0, :], PG[:, s % 2, 0, :], wbc[:, c], ALU.add)
                    V.tensor_tensor(Eb[:, 1, :], PG[:, s % 2, 1, :], wbc[:, c], ALU.add).then_inc(evac_v, 1)

                def gate_mul(i):
                    s, c = i + gt0, bass.ds(i * 512, 512)
                    v.wait_ge(evac_a, s + 1)
                    step(V.scalar_tensor_tensor(Eb[:, :, :], Eb[:, :, :], 1.0, PJ[:, :, c], ALU.add, ALU.mult))
                    V.scalar_tensor_tensor(h[:, :, c], Eb[:, :, :], 0.5, h[:, :, c],
                                           ALU.mult, ALU.add).then_inc(h_ok, 1)

                split(gt0, 0)
                down_panel(3, 2, d0)
                v.wait_ge(evac_v, d0 + 4)
                v.wait_ge(sq_done, 12 * layer + 12)
                post_norm(f"fpost{layer}", lambda: weigh(3))
                fresh_slot(gt0, f"ple{layer}", done=1)
                with v.Fori(0, 3) as i:
                    step.enter(i, 1)
                    for j in range(4):
                        if j == 1:
                            gate_add(i)
                        split(i + (gt0 + 1), j)
                        if j == 1:
                            gate_mul(i)
                    step.leave(3)
                if layer == 1:
                    gate_add(3)
                    gate_mul(3)
                    break
                split(L1, 0)
                gate_add(3)
                gate_mul(3)
                norm_out(2)
                fresh_slot(L1, "mix1", 32, done=1)
                for s in range(L1 + 1, OUT1 + 2):
                    for j in range(units(s)):
                        split_once(s, j)
                        stage(s, j)
                stage(OUT1 + 1, 4)


def kernel(**inputs):
    import concourse.bacc as bacc
    from concourse.bass_utils import run_bass_kernel_spmd

    nc = bacc.Bacc("TRN2", target_bir_lowering=False, num_devices=1, dynamic_dma_scratch_size=1024)
    arrays, tensors = {}, {}
    for name, value in inputs.items():
        a = np.ascontiguousarray(value)
        if name == "nsa_cmp_w1":
            a = np.ascontiguousarray(a.reshape(2, CMP_LEN, P, P).transpose(0, 2, 1, 3))
        if name in ("mla_w_uq", "mla_w_ukv"):
            w = a.reshape(a.shape[:2] + (8, -1))
            a = np.concatenate([w[..., :P].reshape(a.shape[:2] + (-1,)), w[..., P:].reshape(a.shape[:2] + (-1,))], 2)
        arrays[f"in_{name}"] = a
        tensors[name] = nc.dram_tensor(f"in_{name}", a.shape, mybir.dt.from_np(a.dtype), kind="ExternalInput").ap()
    inv = np.power(10000.0, -np.arange(0, 128, 2) / 128.0).astype(np.float32)[None, :]
    arrays["in_rope_inv"] = inv
    tensors["rope_inv"] = nc.dram_tensor("in_rope_inv", inv.shape, F32, kind="ExternalInput").ap()
    tensors["out"] = nc.dram_tensor("out", (1, SEQ, D), F32, kind="ExternalOutput").ap()
    build(nc, tensors)
    r = run_bass_kernel_spmd(nc, [arrays], core_ids=[0])
    return r.results[0]["out"]
```
